# Optimizing a Trainium2 kernel written in Bass

```python
import math
import jax, jax.numpy as jnp
from jax import lax
import numpy as np

D_MODEL = 1024
BATCH = 1
SEQ = 512
DEPTH = 1

HEAD_DIM = 64
DIL_GROUPS = ((128, 1), (512, 4), (2048, 16))
N_DIL = len(DIL_GROUPS)
DIL_HEADS_PER_GROUP = 4
DIL_HEADS = N_DIL * DIL_HEADS_PER_GROUP
DIL_WIDTH = DIL_HEADS * HEAD_DIM
DIL_OUT = DIL_HEADS_PER_GROUP * HEAD_DIM
FOX_HEADS = 8
FOX_WIDTH = FOX_HEADS * HEAD_DIM
BLOCK = 128
D_FF = 2816
N_MOD = 9
RMS_EPS = 1e-6
ALIBI_MAX_BIAS = 8.0
NEG_INF = -1e30
IN_SIZES = (DIL_WIDTH, DIL_WIDTH, DIL_WIDTH, FOX_WIDTH, FOX_WIDTH, FOX_WIDTH,
            FOX_HEADS, D_MODEL, D_MODEL)
N_IN = sum(IN_SIZES)

kernel_name = "hybrid_dilated_fox_macaron_block"

def rms_norm(x, g):
    xf = x.astype(jnp.float32)
    y = xf * lax.rsqrt(jnp.mean(xf * xf, axis=-1, keepdims=True) + RMS_EPS)
    return (y * g.astype(jnp.float32)).astype(x.dtype)

def modulate(h, shift, scale):
    return h * (1 + scale[:, None, :]) + shift[:, None, :]

def swiglu(h, w_gate, w_up, w_down):
    return (jax.nn.silu(h @ w_gate) * (h @ w_up)) @ w_down

def alibi_slopes():
    s = np.array([2.0 ** (-ALIBI_MAX_BIAS * (i + 1) / DIL_HEADS) for i in range(DIL_HEADS)],
                 dtype=np.float32)
    return jnp.asarray(s.reshape(N_DIL, DIL_HEADS_PER_GROUP))

def dilated_window_attention(q, k, v, slopes, window, dilation):
    bsz, seq, nh, e = q.shape
    n_back = window // dilation
    span = dilation * BLOCK
    s_pad = -(-seq // span) * span
    sub_len = s_pad // dilation
    nb = sub_len // BLOCK

    def to_sub(t):
        t = jnp.pad(t, ((0, 0), (0, s_pad - seq), (0, 0), (0, 0)))
        t = t.reshape(bsz, sub_len, dilation, nh, e).transpose(0, 2, 3, 1, 4)
        return t.reshape(bsz, dilation, nh, nb, BLOCK, e)

    def with_prev(t):
        prev = jnp.pad(t[:, :, :, :-1], ((0, 0), (0, 0), (0, 0), (1, 0), (0, 0), (0, 0)))
        return jnp.concatenate([prev, t], axis=4)

    qs = to_sub(q)
    kb, vb = with_prev(to_sub(k)), with_prev(to_sub(v))
    scores = jnp.einsum('bdhnqe,bdhnke->bdhnqk', qs, kb).astype(jnp.float32) / math.sqrt(e)
    qi = jnp.arange(BLOCK)[:, None]
    ki = jnp.arange(2 * BLOCK)[None, :]
    rel = BLOCK + qi - ki
    blk = jnp.arange(nb)[:, None, None]
    valid = (rel >= 0) & (rel <= n_back) & ((blk > 0) | (ki >= BLOCK))
    bias = -slopes.astype(jnp.float32)[:, None, None] * (rel * dilation).astype(jnp.float32)
    scores = jnp.where(valid, scores + bias[:, None], NEG_INF)
    lse = jax.nn.logsumexp(scores, axis=-1)
    p = jnp.exp(scores - lse[..., None])
    o = jnp.einsum('bdhnqk,bdhnke->bdhnqe', p.astype(v.dtype), vb)

    def from_sub(t):
        t = t.reshape(bsz, dilation, nh, sub_len, -1).transpose(0, 3, 1, 2, 4)
        return t.reshape(bsz, s_pad, nh, -1)[:, :seq]

    return from_sub(o), from_sub(lse[..., None])[..., 0]

def forgetting_attention(q, k, v, f_logit):
    bsz, seq, nh, e = q.shape
    nb = seq // BLOCK
    cum = jnp.cumsum(jax.nn.log_sigmoid(f_logit.astype(jnp.float32)), axis=1).transpose(0, 2, 1)
    kt = k.transpose(0, 2, 1, 3)
    vt = v.transpose(0, 2, 1, 3)
    q_blocks = q.reshape(bsz, nb, BLOCK, nh, e).transpose(1, 0, 3, 2, 4)
    cum_blocks = cum.reshape(bsz, nh, nb, BLOCK).transpose(2, 0, 1, 3)
    key_pos = jnp.arange(seq)
    scale = 1.0 / math.sqrt(e)

    def one_block(args):
        qb, cb, b = args
        s = jnp.einsum('bhqe,bhke->bhqk', qb, kt).astype(jnp.float32) * scale
        s = s + cb[..., None] - cum[:, :, None, :]
        q_pos = b * BLOCK + jnp.arange(BLOCK)
        s = jnp.where(key_pos[None, :] <= q_pos[:, None], s, NEG_INF)
        p = jax.nn.softmax(s, axis=-1)
        return jnp.einsum('bhqk,bhke->bhqe', p.astype(vt.dtype), vt)

    out = lax.map(one_block, (q_blocks, cum_blocks, jnp.arange(nb)))
    return out.transpose(1, 0, 3, 2, 4).reshape(bsz, seq, nh * e)

def hybrid_mixer(h, w_in, forget_bias, w_branch_a, w_branch_b, w_out):
    bsz, seq, _ = h.shape
    proj = h @ w_in
    offsets = [int(o) for o in np.cumsum(IN_SIZES)[:-1]]
    qa, ka, va, qb, kb, vb, f_logit, ga, gb = jnp.split(proj, offsets, axis=-1)

    qa = qa.reshape(bsz, seq, N_DIL, DIL_HEADS_PER_GROUP, HEAD_DIM)
    ka = ka.reshape(bsz, seq, N_DIL, DIL_HEADS_PER_GROUP, HEAD_DIM)
    va = va.reshape(bsz, seq, N_DIL, DIL_HEADS_PER_GROUP, HEAD_DIM)
    slopes = alibi_slopes()
    outs, lses = [], []
    for g, (window, dilation) in enumerate(DIL_GROUPS):
        o, lse = dilated_window_attention(qa[:, :, g], ka[:, :, g], va[:, :, g],
                                          slopes[g], window, dilation)
        outs.append(o)
        lses.append(lse)
    weights = jax.nn.softmax(jnp.stack(lses, axis=0), axis=0)
    y_a = jnp.sum(weights[..., None].astype(h.dtype) * jnp.stack(outs, axis=0), axis=0)
    y_a = y_a.reshape(bsz, seq, DIL_OUT) @ w_branch_a

    f_logit = f_logit + forget_bias
    y_b = forgetting_attention(qb.reshape(bsz, seq, FOX_HEADS, HEAD_DIM),
                               kb.reshape(bsz, seq, FOX_HEADS, HEAD_DIM),
                               vb.reshape(bsz, seq, FOX_HEADS, HEAD_DIM), f_logit)
    y_b = y_b @ w_branch_b

    merged = jax.nn.sigmoid(ga) * y_a + jax.nn.sigmoid(gb) * y_b
    return merged @ w_out

def setup_inputs(seed: int = 0) -> dict:
    key = jax.random.key(seed)
    ks = jax.random.split(key, 20)
    f32 = jnp.float32

    def w(k, shape, fan_in):
        return jax.random.normal(k, shape, f32) * fan_in ** -0.5

    def gain(k, shape):
        return 1.0 + 0.02 * jax.random.normal(k, shape, f32)

    return {
        "x": jax.random.normal(ks[0], (BATCH, SEQ, D_MODEL), f32),
        "c": jax.random.normal(ks[1], (BATCH, D_MODEL), f32),
        "ada_w": w(ks[2], (DEPTH, D_MODEL, N_MOD * D_MODEL), D_MODEL),
        "ada_b": 0.02 * jax.random.normal(ks[3], (DEPTH, N_MOD * D_MODEL), f32),
        "norm_ffn1": gain(ks[4], (DEPTH, D_MODEL)),
        "ffn1_w_gate": w(ks[5], (DEPTH, D_MODEL, D_FF), D_MODEL),
        "ffn1_w_up": w(ks[6], (DEPTH, D_MODEL, D_FF), D_MODEL),
        "ffn1_w_down": w(ks[7], (DEPTH, D_FF, D_MODEL), D_FF),
        "norm_mix": gain(ks[8], (DEPTH, D_MODEL)),
        "w_in": w(ks[9], (DEPTH, D_MODEL, N_IN), D_MODEL),
        "forget_bias": jnp.linspace(1.0, 6.0, FOX_HEADS, dtype=f32)[None, :]
                       + 0.1 * jax.random.normal(ks[10], (DEPTH, FOX_HEADS), f32),
        "w_branch_a": w(ks[11], (DEPTH, DIL_OUT, D_MODEL), DIL_OUT),
        "w_branch_b": w(ks[12], (DEPTH, FOX_WIDTH, D_MODEL), FOX_WIDTH),
        "w_out": w(ks[13], (DEPTH, D_MODEL, D_MODEL), D_MODEL),
        "norm_ffn2": gain(ks[14], (DEPTH, D_MODEL)),
        "ffn2_w_gate": w(ks[15], (DEPTH, D_MODEL, D_FF), D_MODEL),
        "ffn2_w_up": w(ks[16], (DEPTH, D_MODEL, D_FF), D_MODEL),
        "ffn2_w_down": w(ks[17], (DEPTH, D_FF, D_MODEL), D_FF),
        "norm_final": gain(ks[18], (D_MODEL,)),
    }

def reference(x, c, ada_w, ada_b, norm_ffn1, ffn1_w_gate, ffn1_w_up, ffn1_w_down,
              norm_mix, w_in, forget_bias, w_branch_a, w_branch_b, w_out,
              norm_ffn2, ffn2_w_gate, ffn2_w_up, ffn2_w_down, norm_final):
    c_act = jax.nn.silu(c)
    for layer in range(DEPTH):
        mod = c_act @ ada_w[layer] + ada_b[layer]
        (sh1, sc1, gt1, sh2, sc2, gt2, sh3, sc3, gt3) = jnp.split(mod, N_MOD, axis=-1)
        h = modulate(rms_norm(x, norm_ffn1[layer]), sh1, sc1)
        x = x + 0.5 * gt1[:, None, :] * swiglu(h, ffn1_w_gate[layer], ffn1_w_up[layer],
                                               ffn1_w_down[layer])
        h = modulate(rms_norm(x, norm_mix[layer]), sh2, sc2)
        x = x + gt2[:, None, :] * hybrid_mixer(h, w_in[layer], forget_bias[layer],
                                               w_branch_a[layer], w_branch_b[layer],
                                               w_out[layer])
        h = modulate(rms_norm(x, norm_ffn2[layer]), sh3, sc3)
        x = x + 0.5 * gt3[:, None, :] * swiglu(h, ffn2_w_gate[layer], ffn2_w_up[layer],
                                               ffn2_w_down[layer])
    return rms_norm(x, norm_final)


_drawn_inputs = setup_inputs


def setup_inputs(seed=0):
    import zlib

    import numpy as np

    out = dict(_drawn_inputs(seed))
    spreads = {}
    factors = {'norm_ffn1': 6.654, 'norm_mix': 7.094, 'norm_ffn2': 7.606, 'norm_final': 2.874}
    for name, (base, spread) in spreads.items():
        noise = np.random.default_rng([zlib.crc32(name.encode()), seed]).standard_normal(out[name].shape)
        drawn = base * np.exp(spread * noise) if base else spread * noise
        out[name] = __import__('jax').numpy.asarray(drawn.astype(out[name].dtype))
    for name, factor in factors.items():
        out[name] = (out[name] * factor).astype(out[name].dtype)
    return out
```

```python
from contextlib import ExitStack

import concourse.bass as bass
from concourse import mybir

F32 = mybir.dt.float32
F32R = mybir.dt.float32r
I32 = mybir.dt.int32
ALU = mybir.AluOpType
ACT = mybir.ActivationFunctionType
AX = mybir.AxisListType

P = 128
D = 1024
T = 512
KC = D // P
TB = T // P
DFF = 2816
FB = DFF // P
SC = 256
E_ = 64
NG, GH, FH = 3, 4, 8
DILW, FOXW = NG * GH * E_, FH * E_
DILATION = (1, 4, 16)
EPS = 1e-6
NEG = -1e30
COL_Q, COL_K, COL_V = 0, DILW, 2 * DILW
COL_FQ = 3 * DILW
COL_FK, COL_FV, COL_F = COL_FQ + FOXW, COL_FQ + 2 * FOXW, COL_FQ + 3 * FOXW
COL_GA = COL_F + FH

GU_IT = DFF // SC
DOWN_PARTS = ((0, 8), (8, 8), (16, 6))
N_DOWN = (D // SC) * len(DOWN_PARTS)
N_FFN = 2 * GU_IT + N_DOWN
N_QKV, N_OVER, N_BR, N_OUT = 9, 14, 4, 4
S_MIX = N_FFN
S_OVER = S_MIX + N_QKV
S_BR = S_OVER + N_OVER
S_OUT = S_BR + N_BR
S_FFN2 = S_OUT + N_OUT
N_SLOTS = S_FFN2 + N_FFN

PRO_CHUNKS = 2 * KC
GU_PAIRS, DOWN_PAIRS = 2, 3
PAIR_STEPS = 2 * KC

SLOPE = [2.0 ** (-8.0 * (i + 1) / (NG * GH)) for i in range(NG * GH)]


def attention_tiles():
    tiles, job = [], 0
    for h in range(GH):
        tiles.append((job, 0, h, [(0, 0, P), (1, P, 2 * P)]))
        tiles.append((job, 0, h, [(2, 0, 2 * P), (3, 2 * P, 2 * P)]))
        job += 1
    for g in (1, 2):
        for h in range(GH):
            tiles.append((job, g, h, [(r, r * P, P) for r in range(TB)]))
            job += 1
    for h in range(FH):
        tiles.append((job, 3, h, [(0, 0, P), (1, P, 2 * P)]))
        tiles.append((job, 3, h, [(2, 0, 3 * P)]))
        tiles.append((job, 3, h, [(3, 0, 4 * P)]))
        job += 1
    return tiles


TILES = attention_tiles()
N_TILES = len(TILES)
LAST_TILE = {}
for _u, _t in enumerate(TILES):
    LAST_TILE[_t[0]] = _u
FIRST_FOX = 2 * GH + 2 * GH
COMB_LN, COMB_EXP = FIRST_FOX + 4, FIRST_FOX + 11
FIN_BANK = (0, 2, 6, 4)
JOBS = {t[0]: (t[1], t[2]) for t in TILES}


def mixer_columns():
    cols_ = [COL_V + SC * g for g in range(NG)]
    for g in range(NG):
        cols_ += [COL_Q + SC * g, COL_K + SC * g]
    for c0 in (COL_FQ, COL_FK, COL_FV):
        cols_ += [c0, c0 + SC]
    return cols_ + [COL_GA + SC * j for j in range(2 * D // SC)]


def key_blocks(group, t):
    if group == 0:
        return [t] if t == 0 else [t - 1, t]
    if group in (1, 2):
        return [t]
    return list(range(t + 1))


def build(nc, x, c, ada_w, ada_b, norm_ffn1, w_gate1, w_up1, w_down1, norm_mix, w_in, forget_bias,
          w_branch_a, w_branch_b, w_out, norm_ffn2, w_gate2, w_up2, w_down2, norm_final, out):
    ctx = ExitStack()
    with ctx:
        def sb(name, shape, dt=F32, where=ctx):
            return where.enter_context(nc.sbuf_tensor(name, shape, dt))

        def sem(name):
            return ctx.enter_context(nc.semaphore(name))

        xT = sb("xT", [P, KC, T])
        h_hi = sb("h_hi", [P, KC, T], F32R)
        h_lo = sb("h_lo", [P, KC, T], F32R)
        raw = [sb(f"raw{s}", [P, KC * SC]) for s in range(2)]
        w_hi = [sb(f"w_hi{s}", [P, KC * SC], F32R) for s in range(2)]
        w_lo = [sb(f"w_lo{s}", [P, KC * SC], F32R) for s in range(2)]
        tmpA = sb("tmpA", [P, 2, T])
        tmpB = sb("tmpB", [P, 2, T])
        ident = sb("ident", [P, P])
        ones = sb("ones", [P, P])
        rows = sb("rows", [112, P])
        cols = sb("cols", [P, 112])
        c_act = sb("c_act", [P, KC])
        mod = sb("mod", [P, 9 * KC])
        scale_a = sb("scale_a", [P, 3, KC])
        gate_c = sb("gate_c", [P, 3, KC])
        ada_col = sb("ada_col", [P, 2 * KC])
        ss = sb("ss", [P, TB])
        var = sb("var", [P, TB])
        std = sb("std", [P, TB])
        r0 = sb("r0", [P, TB])
        nw = sb("nw", [P, TB])
        rstd = sb("rstd", [P, TB])
        ss_part = sb("ss_part", [P, TB, KC])
        fbias = sb("fbias", [FH, 1])

        GAIN = 80
        banks = [ctx.enter_context(nc.psum_tensor(f"bank{i}", [P, T], F32)) for i in range(8)]

        ffn1 = ExitStack()
        ada_ring = [sb(f"ada{s}", [P, KC, P], where=ffn1) for s in range(2)]
        ada_acc = [sb(f"ada_acc{s}", [P, P], where=ffn1) for s in range(2 * DOWN_PAIRS)]
        pro = ExitStack()
        x_nat = sb("x_nat", [P, TB, D], where=pro)
        ada_pro = [sb(f"ada_pro{s}", [P, KC, D], where=pro) for s in range(2)]
        acc_pro = [sb(f"acc_pro{s}", [P, D], where=pro) for s in range(2)]
        pro.close()
        hid1 = [sb(f"hid1_{s}", [P, FB, T], F32R, where=ffn1) for s in ("hi", "lo")]
        ffn1.close()

        mix = ExitStack()
        dil = sb("dil", [P, 9 * 2 * T], where=mix)
        dq = [dil[:, (g * 6) * T:(g * 6 + 2) * T].rearrange("p (c t) -> p c t", c=2) for g in range(NG)]
        dk = [dil[:, (g * 6 + 2) * T:(g * 6 + 4) * T].rearrange("p (c t) -> p c t", c=2) for g in range(NG)]
        dv = [dil[:, (g * 6 + 4) * T:(g * 6 + 6) * T].rearrange("p (t e) -> p t e", t=TB) for g in range(NG)]
        ckb = [dil[:, s * T:(s + 1) * T] for s in range(2)]
        gates = dil[:, 2 * T:18 * T].rearrange("p (c t) -> p c t", c=16)
        o_dil = sb("o_dil", [P, NG, TB, GH * E_], where=mix)
        o_fox = sb("o_fox", [P, TB, FOXW], where=mix)
        pT = sb("pT", [P, 2, T], where=mix)
        alibi = sb("alibi", [P, 2, 2 * P], where=mix)
        rel = sb("rel", [P, 2 * P], where=mix)
        m_band = sb("m_band", [P, 2 * P], where=mix)
        m_causal = sb("m_causal", [P, P], where=mix)
        m_res = sb("m_res", [P, P], where=mix)
        i_rel = sb("i_rel", [P, 2 * P], I32, where=mix)
        i_and = sb("i_and", [P, P], I32, where=mix)
        nsel = sb("nsel", [FH, FH, P], where=mix)
        wf = sb("wf", [P, KC, FH], where=mix)
        wf_hi = sb("wf_hi", [P, KC * FH + P], F32R, where=mix)
        wf_lo = sb("wf_lo", [P, KC * FH + P], F32R, where=mix)
        f_x, f_abs, ls_row, zeros_row = tmpA[0:FH, 0, :], tmpA[0:FH, 1, :], tmpB[0:FH, 0, :], tmpB[0:FH, 1, :]
        cum_row = sb("cum_row", [FH, T], where=mix)
        cum_col = sb("cum_col", [P, TB, FH], where=mix)
        mx = sb("mx", [P, 4, TB, FH], where=mix)
        nmx = sb("nmx", [P, 2, TB], where=mix)
        zs = sb("zs", [P, 4, TB, FH], where=mix)
        rz = sb("rz", [P, 2, TB], where=mix)
        lse = sb("lse", [P, NG, TB * GH], where=mix)
        gmax = sb("gmax", [P, TB * GH], where=mix)
        gw = sb("gw", [P, NG, TB * GH], where=mix)
        gsum = sb("gsum", [P, TB * GH], where=mix)
        gw0 = sb("gw0", [P, TB * GH], where=mix)
        foxmem = ExitStack()
        fq = sb("fq", [P, 4, T], where=foxmem)
        fk = sb("fk", [P, 4, T], where=foxmem)
        fv = sb("fv", [P, TB, FOXW], where=foxmem)
        foxmem.close()
        ybr = ExitStack()
        y_hi = sb("y_hi", [P, 6, T], F32R, where=ybr)
        y_lo = sb("y_lo", [P, 6, T], F32R, where=ybr)
        ybr.close()
        mix.close()

        ffn2 = ExitStack()
        hid2 = [sb(f"hid2_{s}", [P, FB, T], F32R, where=ffn2) for s in ("hi", "lo")]
        ffn2.close()
        fin = ExitStack()
        y_sb = sb("y_sb", [P, TB, D], where=fin)
        fin.close()

        lse_dram = nc.dram_tensor("lse_scratch", [T, GH], F32).ap()
        gw_dram = nc.dram_tensor("gw_scratch", [T, GH], F32).ap()

        raw_landed = [sem(f"raw_landed{s}") for s in range(2)]
        br_b_landed = [sem(f"br_b_landed{s}") for s in range(2)]
        split_hi = sem("split_hi")
        split_done = sem("split_done")
        slot_used = sem("slot_used")
        bank01_free = sem("bank01_free")
        bank23_free = sem("bank23_free")
        hid_hi_ready, hid_ready = sem("hid_hi_ready"), sem("hid_ready")
        x_updated = sem("x_updated")
        sq_ready, stat_done = sem("sq_ready"), sem("stat_done")
        ident_step, const_ready = sem("ident_step"), sem("const_ready")
        rows_landed, fb_landed = sem("rows_landed"), sem("fb_landed")
        x_landed = [sem(f"x_landed{t}") for t in range(TB)]
        rows_turned, cols_ready, cact_ready = sem("rows_turned"), sem("cols_ready"), sem("cact_ready")
        x_turned, ss_ready = sem("x_turned"), sem("ss_ready")
        pro_landed = [sem(f"pro_landed{k}") for k in range(2 * KC)]
        ada_landed = [sem(f"ada_landed{s}") for s in range(2)]
        pro_step, pro_turned, pro_red = sem("pro_step"), sem("pro_turned"), sem("pro_red")
        ada_step = sem("ada_step")
        ada_red = sem("ada_red")
        ada_mm = sem("ada_mm")
        mod_ready = sem("mod_ready")
        coef_ready = sem("coef_ready")
        ss_step, neg_step = sem("ss_step"), sem("neg_step")
        var_ready, std_ready, rstd_step = sem("var_ready"), sem("std_ready"), sem("rstd_step")
        diag_ready, rstd_bc = sem("diag_ready"), sem("rstd_bc")
        t_ready, h_hi_ready, h_ready = sem("t_ready"), sem("h_hi_ready"), sem("h_ready")
        qkv_evac = sem("qkv_evac")
        mask_step, mask_ready, res_ready = sem("mask_step"), sem("mask_ready"), sem("res_ready")
        wf_zero = sem("wf_zero")
        wf_landed, wf_hi_ready, wf_ready = sem("wf_landed"), sem("wf_hi_ready"), sem("wf_ready")
        f_ready, f_step, f_act = sem("f_ready"), sem("f_step"), sem("f_act")
        cum_ready = sem("cum_ready")
        cum_turned, cumcol_ready = sem("cum_turned"), sem("cumcol_ready")
        proj_ready = sem("proj_ready")
        p0_free, p1_free = sem("p0_free"), sem("p1_free")
        ck_ready, ck_free = sem("ck_ready"), sem("ck_free")
        scores_ready = sem("scores_ready")
        alibi_ready, bias_step = sem("alibi_ready"), sem("bias_step")
        scores_read = sem("scores_read")
        max_step, max_ready = sem("max_step"), sem("max_ready")
        probs_ready, turned, pT_ready = sem("probs_ready"), sem("turned"), sem("pT_ready")
        pv_ready, rz_ready, o_free = sem("pv_ready"), sem("rz_ready"), sem("o_free")
        comb, comb_act = sem("comb"), sem("comb_act")
        lse_out, lse_in, gw_out, gw_in = sem("lse_out"), sem("lse_in"), sem("gw_out"), sem("gw_in")
        y_turned, y0_ready, ysum_ready = sem("y_turned"), sem("y0_ready"), sem("ysum_ready")
        y_hi_ready, y_ready = sem("y_hi_ready"), sem("y_ready")
        sig_ready, br_ready = sem("sig_ready"), sem("br_ready")
        merge_step, msum_ready, merge_hi, merged = sem("merge_step"), sem("msum_ready"), sem("merge_hi"), sem("merged")
        xg_ready, fin_turned = sem("xg_ready"), sem("fin_turned")
        y_act, y_dve, out_done = sem("y_act"), sem("y_dve"), sem("out_done")

        BANKS = (KC // 2, KC // 2 + 2 * GU_IT)
        FFN_SLOT = (0, S_FFN2)
        N_PAIRS = GU_IT * GU_PAIRS + 2 * DOWN_PAIRS
        assert PRO_CHUNKS + 2 * N_PAIRS == 9 * KC

        def slot_size(n):
            for base in FFN_SLOT:
                if base + 2 * GU_IT <= n < base + N_FFN and (n - base - 2 * GU_IT) % 3 == 2:
                    return DOWN_PARTS[2][1] * SC
            return 6 * SC if S_BR <= n < S_OUT else KC * SC

        def landed(eng, n, loop=0):
            eng.wait_ge(raw_landed[n % 2], 16 * (n // 2 + 1) + loop)
            if S_BR <= n < S_OUT:
                eng.wait_ge(br_b_landed[n % 2], 16 * ((n - S_BR) // 2 + 1))

        def norm_t(k):
            return (tmpA, tmpB)[k // 2 % 2][:, k % 2, :]

        block = ctx.enter_context(nc.Block())

        @block.sync
        def _(sp):
            def rows_of(w):
                return w.rearrange("(k p) c -> p k c", p=P)

            def slot_dst(n, nk, at=0):
                return raw[n % 2][:, at:at + nk * SC].rearrange("p (k c) -> p k c", k=nk)

            def load(n, nk, src, loop=0):
                if n >= 2:
                    sp.wait_ge(split_done, n - 1 + loop)
                sp.dma_start(slot_dst(n, nk), src).then_inc(raw_landed[n % 2], 16)

            def gate_up(base, wg, wu, i):
                for j, w in enumerate((wg, wu)):
                    load(base + j, KC, rows_of(w)[:, :, bass.ds(SC * i, SC)], 2 * i)

            def gate_up_from1(wg, wu, i):
                for j, w in enumerate((wg, wu)):
                    load(2 + j, KC, rows_of(w)[:, :, bass.ds(SC * i + SC, SC)], 2 * i)

            def down(base, w, j):
                for s in range(6):
                    k0, nk = DOWN_PARTS[s % 3]
                    load(base + s, nk, rows_of(w)[:, k0:k0 + nk, bass.ds(2 * SC * j + SC * (s // 3), SC)], 6 * j)

            for t in range(TB):
                sp.dma_start(x_nat[:, t, :], x[t * P:(t + 1) * P, :]).then_inc(x_landed[t], 16)
            load(0, KC, rows_of(w_gate1)[:, :, 0:SC])
            for j in range(2):
                for k in range(KC):
                    sp.dma_start(ada_pro[j][:, k, :], ada_w[k * P:(k + 1) * P, j * D:(j + 1) * D])\
                      .then_inc(pro_landed[j * KC + k], 16)
            load(1, KC, rows_of(w_up1)[:, :, 0:SC])
            with sp.Fori(0, GU_IT - 1) as i:
                gate_up_from1(w_gate1, w_up1, i)
            with sp.Fori(0, 2) as j:
                down(2 * GU_IT, w_down1, j)
            for m, col in enumerate(mixer_columns()):
                load(S_MIX + m, KC, rows_of(w_in)[:, :, col:col + SC])
                if m == 0:
                    sp.wait_ge(slot_used, N_FFN)
                    sp.dma_start(wf[:, :, :], rows_of(w_in)[:, :, COL_F:COL_F + FH]).then_inc(wf_landed, 16)
            for d2 in range(N_BR):
                n = S_BR + d2
                load(n, 2, rows_of(w_branch_a)[:, :, d2 * SC:(d2 + 1) * SC])
                sp.dma_start(slot_dst(n, 4, at=2 * SC), rows_of(w_branch_b)[:, :, d2 * SC:(d2 + 1) * SC])\
                  .then_inc(br_b_landed[n % 2], 16)
            for d2 in range(N_OUT):
                load(S_OUT + d2, KC, rows_of(w_out)[:, :, d2 * SC:(d2 + 1) * SC])
            with sp.Fori(0, GU_IT) as i:
                gate_up(S_FFN2, w_gate2, w_up2, i)
            with sp.Fori(0, 2) as j:
                down(S_FFN2 + 2 * GU_IT, w_down2, j)
            for t in range(TB):
                sp.wait_ge(y_act, t + 1)
                sp.wait_ge(y_dve, t + 1)
                sp.dma_start(out[t * P:(t + 1) * P, :], y_sb[:, t, :]).then_inc(out_done, 16)
            sp.wait_ge(out_done, 16 * TB)

        @block.gpsimd
        def _(pool):
            pool.memset(ident[:, :], 0.0).then_inc(ident_step, 1)
            pool.memset(ones[:, :], 1.0).then_inc(const_ready, 1)
            pool.wait_ge(ident_step, 1)
            pool.affine_select(out=ident[:, :], in_=ident[:, :], compare_op=ALU.not_equal, fill=1.0,
                               base=0, pattern=[[-1, P]], channel_multiplier=1).then_inc(const_ready, 1)

            def ada_pair(pair, i=0):
                if pair:
                    pool.wait_ge(ada_step, PAIR_STEPS * pair + GU_PAIRS * PAIR_STEPS * i)
                for s in range(2):
                    col = (PRO_CHUNKS + 2 * pair + s) * P + 2 * GU_PAIRS * P * i
                    pool.dma_start(ada_ring[s][:, :, :],
                                   ada_w.rearrange("(k p) c -> p k c", p=P)[:, :, bass.ds(col, P)])\
                        .then_inc(ada_landed[s], 16)

            ada_pair(0)
            with pool.Fori(0, GU_IT) as i:
                for q in range(GU_PAIRS):
                    ada_pair(q + 1, i)
            for pair in range(GU_IT * GU_PAIRS + 1, N_PAIRS):
                ada_pair(pair)

            pool.wait_ge(slot_used, N_FFN)
            pool.iota(i_rel[:, :], pattern=[[-1, 2 * P]], base=P, channel_multiplier=1).then_inc(mask_step, 1)
            pool.memset(m_band[:, :], 0.0).then_inc(mask_step, 1)
            pool.memset(m_causal[:, :], 0.0).then_inc(mask_step, 1)
            pool.memset(nsel[:, :, :], 0.0).then_inc(mask_step, 1)
            for w in (wf_hi, wf_lo):
                pool.memset(w[:, KC * FH:].bitcast(F32), 0.0).then_inc(wf_zero, 1)
            pool.wait_ge(mask_step, 4)
            pool.affine_select(out=m_band[:, :], in_=m_band[:, :], compare_op=ALU.is_ge, fill=NEG, base=P,
                               pattern=[[-1, 2 * P]], channel_multiplier=1).then_inc(mask_step, 1)
            pool.wait_ge(mask_step, 5)
            pool.affine_select(out=m_band[:, :], in_=m_band[:, :], compare_op=ALU.is_ge, fill=NEG, base=0,
                               pattern=[[1, 2 * P]], channel_multiplier=-1).then_inc(mask_ready, 1)
            pool.affine_select(out=m_causal[:, :], in_=m_causal[:, :], compare_op=ALU.is_ge, fill=NEG, base=0,
                               pattern=[[-1, P]], channel_multiplier=1).then_inc(mask_ready, 1)
            pool.affine_select(out=nsel[:, :, :], in_=nsel[:, :, :], compare_op=ALU.not_equal, fill=-1.0, base=0,
                               pattern=[[-1, FH], [0, P]], channel_multiplier=1).then_inc(mask_ready, 1)

            pool.wait_ge(comb, 1)
            pool.dma_start(lse_dram.rearrange("(t p) h -> p t h", p=P),
                           lse[:, 0, :].rearrange("p (t h) -> p t h", t=TB)).then_inc(lse_out, 16)
            pool.wait_ge(lse_out, 16)
            pool.dma_start(lse[:, 0, :], lse_dram.rearrange("(i r) h -> i (r h)", r=TB)).then_inc(lse_in, 16)
            pool.wait_ge(comb, 8)
            pool.dma_start(gw_dram.rearrange("(i r) h -> i (r h)", r=TB), gw[:, 0, :]).then_inc(gw_out, 16)
            pool.wait_ge(gw_out, 16)
            pool.dma_start(gw0[:, :].rearrange("p (t h) -> p t h", t=TB),
                           gw_dram.rearrange("(t p) h -> p t h", p=P)).then_inc(gw_in, 16)

        @block.scalar
        def _(act):
            def hi(n, loop=0, loop_landed=0):
                landed(act, n, loop_landed)
                if n >= 2:
                    act.wait_ge(slot_used, n - 1 + loop)
                m = slot_size(n)
                act.activation(w_hi[n % 2][:, 0:m], raw[n % 2][:, 0:m], ACT.Copy).then_inc(split_hi, 1)

            def norm(q, shift_col):
                act.wait_ge(var_ready, q + 1)
                act.activation(std[:, :], var[:, :], ACT.Sqrt).then_inc(std_ready, 1)
                if q == 3:
                    return
                for k in range(KC):
                    act.wait_ge(t_ready, KC * q + k + 1)
                    act.activation(h_hi[:, k, :], norm_t(k), ACT.Identity,
                                   bias=mod[:, shift_col + k:shift_col + k + 1]).then_inc(h_hi_ready, 1)

            def ffn_gate_up(fi, i, hid):
                base, bank0, hid0 = FFN_SLOT[fi], BANKS[fi], 2 * GU_IT * fi
                for f in range(2):
                    act.wait_ge(slot_used, base + 1 + 2 * i)
                    act.wait_ge(bank23_free, bank0 - 1 + f + 2 * i)
                    act.activation(tmpA[:, f, :], banks[f][:, :], ACT.Silu).then_inc(bank01_free, 1)
                hi(base + 2, loop=2 * i, loop_landed=16 * i)
                for f in range(2):
                    act.wait_ge(bank23_free, bank0 + 1 + f + 2 * i)
                    act.activation(hid[0][:, 2 * i + f, :], tmpB[:, f, :], ACT.Copy).then_inc(hid_hi_ready, 1)
                hi(base + 3, loop=2 * i, loop_landed=16 * i)

            def ffn_down(fi, j, last=False):
                base, x0 = FFN_SLOT[fi] + 2 * GU_IT, 2 * KC * fi
                for s in range(6):
                    if s % 3 == 2:
                        squares(x0 + 2 * (s // 3), 4 * j, first=s == 2)
                    if not (last and s >= 4):
                        hi(base + s + 2, loop=6 * j, loop_landed=48 * j)

            def squares(x0, loop=0, first=False):
                for dd in range(2):
                    act.wait_ge(x_updated, x0 + dd + 1 + loop)
                    if not first:
                        act.wait_ge(stat_done, x0 + dd - 1 + loop)
                    act.activation(tmpA[:, dd, :], xT[:, bass.ds(x0 % KC + dd + loop, 1), :], ACT.Square)\
                       .then_inc(sq_ready, 1)

            def merge_hi_part(d):
                act.wait_ge(msum_ready, d + 1)
                act.activation(h_hi[:, d, :], tmpB[:, d % 2, :], ACT.Copy).then_inc(merge_hi, 1)

            act.dma_start(rows[0:72, :], ada_b.rearrange("(r p) -> r p", p=P)).then_inc(rows_landed, 16)
            act.dma_start(rows[72:80, :], c.rearrange("(r p) -> r p", p=P)).then_inc(rows_landed, 16)
            for n, g in enumerate((norm_ffn1, norm_mix, norm_ffn2, norm_final)):
                act.dma_start(rows[GAIN + KC * n:GAIN + KC * (n + 1), :], g.rearrange("(r p) -> r p", p=P))\
                   .then_inc(rows_landed, 16)
            act.dma_start(fbias[:, :], forget_bias.rearrange("(h a) -> h a", a=1)).then_inc(fb_landed, 16)
            act.wait_ge(cols_ready, 1)
            act.activation(c_act[:, :], cols[:, 72:80], ACT.Silu).then_inc(cact_ready, 1)
            for t in range(TB):
                act.wait_ge(x_landed[t], 16)
                act.activation(tmpA[:, :, :].rearrange("p a t -> p (a t)"), x_nat[:, t, :], ACT.Square,
                               accum_out=ss[:, t:t + 1]).then_inc(ss_ready, 1)
                act.wait_ge(ss_ready, t + 1)
            hi(0)
            norm(0, 0)
            hi(1)
            with act.Fori(0, GU_IT) as i:
                ffn_gate_up(0, i, hid1)
            with act.Fori(0, 2) as j:
                ffn_down(0, j)
            norm(1, 3 * KC)

            act.wait_ge(wf_landed, 16)
            act.activation(wf_hi[:, 0:KC * FH], wf[:, :, :].rearrange("p k h -> p (k h)"), ACT.Copy)\
               .then_inc(wf_hi_ready, 1)
            for m in range(N_QKV):
                if m == 2:
                    act.wait_ge(f_step, 3)
                    act.activation(f_abs, f_abs, ACT.Exp).then_inc(f_act, 1)
                    act.wait_ge(f_act, 1)
                    act.activation(f_abs, f_abs, ACT.Ln, bias=1.0).then_inc(f_act, 1)
                hi(S_MIX + 2 + m)

            def exp_tile(u):
                job, g, h, subs = TILES[u]
                act.wait_ge(max_ready, u + 1)
                if u >= 2:
                    act.wait_ge(turned, u - 1)
                for n, (t, c0, w) in enumerate(subs):
                    last = act.activation(tmpB[:, u % 2, c0:c0 + w], tmpA[:, u % 2, c0:c0 + w], ACT.Exp,
                                          bias=nmx[:, u % 2, n:n + 1], accum_out=zs[:, g, t, h:h + 1])
                last.then_inc(probs_ready, 1)

            def evac_pT(u):
                _, _, _, subs = TILES[u]
                w = subs[-1][1] + subs[-1][2]
                act.wait_ge(turned, u + 1)
                if u >= 2:
                    act.wait_ge(pv_ready, u - 1)
                act.activation(pT[:, u % 2, 0:w], banks[4 + u % 2][:, 0:w], ACT.Copy).then_inc(pT_ready, 1)

            for m in range(N_OVER):
                for j in range(3):
                    s = 3 * m + j
                    if j == 0 and 4 <= m - 1 < 4 + FH:
                        h = m - 1 - 4
                        act.wait_ge(ck_ready, h + 1)
                        if h >= 2:
                            act.wait_ge(scores_read, FIRST_FOX + 3 * (h - 1))
                        act.activation(ckb[h % 2], banks[0][:, :], ACT.Copy).then_inc(ck_free, 1)
                    if 0 <= s - 2 < N_TILES:
                        evac_pT(s - 2)
                    if 0 <= s - 1 < N_TILES:
                        exp_tile(s - 1)
                    if j == 0 and m >= 1:
                        hi(S_OVER + m + 1)
                    if s == COMB_LN:
                        act.wait_ge(o_free, len(JOBS) - FH)
                        act.activation(gw[:, :, :].rearrange("p g (t h) -> p g t h", t=TB), zs[:, 0:NG, :, 0:GH],
                                       ACT.Ln).then_inc(comb_act, 1)
                    if s == COMB_EXP:
                        act.wait_ge(comb, 4)
                        act.activation(gw[:, :, :], gw[:, :, :], ACT.Exp).then_inc(comb_act, 1)
            hi(S_OVER + N_OVER + 1)

            for fb in range(2):
                act.wait_ge(y_turned, 2 * fb + 1)
                act.activation(tmpA[:, fb, :], banks[2 + 2 * fb][:, :], ACT.Copy).then_inc(y0_ready, 1)
            for fc in range(4):
                act.wait_ge(y_turned, 4 + fc + 1)
                act.activation(y_hi[:, 2 + fc, :], banks[(6 + fc) % 8][:, :], ACT.Copy).then_inc(y_hi_ready, 1)
            for fb in range(2):
                act.wait_ge(ysum_ready, fb + 1)
                act.activation(y_hi[:, fb, :], tmpB[:, fb, :], ACT.Copy).then_inc(y_hi_ready, 1)
            act.wait_ge(p1_free, N_OVER)
            for d in range(KC):
                act.activation(gates[:, d::KC, :], gates[:, d::KC, :], ACT.Sigmoid).then_inc(sig_ready, 1)
                if d >= 1:
                    merge_hi_part(d - 1)
                if d % 2 == 1:
                    hi(S_BR + d // 2 + 2)
            merge_hi_part(KC - 1)
            for d2 in range(N_OUT):
                squares(KC + 2 * d2)
                hi(S_OUT + d2 + 2)
            norm(2, 6 * KC)
            with act.Fori(0, GU_IT) as i:
                ffn_gate_up(1, i, hid2)
            for j in range(2):
                ffn_down(1, j, last=j == 1)
            for k in range(KC):
                act.activation(xT[:, k, :], xT[:, k, :], ACT.Copy, scale=cols[:, GAIN + 3 * KC + k:GAIN + 3 * KC + k + 1])\
                   .then_inc(xg_ready, 1)
            norm(3, None)
            for t in range(TB):
                act.wait_ge(fin_turned, 2 * t + 1)
                act.wait_ge(rstd_step, 4 * 4)
                act.activation(y_sb[:, t, 0:T], banks[FIN_BANK[t]][:, :], ACT.Copy, scale=rstd[:, t:t + 1]).then_inc(y_act, 1)

        @block.vector
        def _(dve):
            def lo(n, loop=0):
                dve.wait_ge(split_hi, n + 1 + loop)
                m = slot_size(n)
                dve.tensor_tensor(w_lo[n % 2][:, 0:m], raw[n % 2][:, 0:m], w_hi[n % 2][:, 0:m].bitcast(F32),
                                  ALU.subtract).then_inc(split_done, 1)

            def norm_stats(q):
                if q == 0:
                    dve.wait_ge(ss_ready, TB)
                else:
                    dve.wait_ge(ss_step, (KC + 1) * q - 1)
                    dve.tensor_reduce(ss[:, :], ss_part[:, :, :], AX.X, ALU.add).then_inc(ss_step, 1)
                    dve.wait_ge(ss_step, (KC + 1) * q)
                dve.tensor_scalar(var[:, :], ss[:, :], 1.0 / D, EPS, ALU.mult, ALU.add).then_inc(var_ready, 1)
                dve.wait_ge(std_ready, q + 1)
                dve.reciprocal(r0[:, :], std[:, :]).then_inc(rstd_step, 1)
                dve.wait_ge(rstd_step, 4 * q + 1)
                dve.tensor_tensor(nw[:, :], r0[:, :], r0[:, :], ALU.mult).then_inc(rstd_step, 1)
                dve.wait_ge(rstd_step, 4 * q + 2)
                dve.tensor_tensor(nw[:, :], nw[:, :], var[:, :], ALU.mult).then_inc(rstd_step, 1)
                dve.wait_ge(rstd_step, 4 * q + 3)
                dve.scalar_tensor_tensor(out=rstd[:, :], in0=nw[:, :], scalar=-3.0, in1=r0[:, :], op0=ALU.add,
                                         op1=ALU.mult).then_inc(neg_step, 1)
                dve.wait_ge(neg_step, q + 1)
                dve.tensor_scalar(rstd[:, :], rstd[:, :], -0.5, None, ALU.mult).then_inc(rstd_step, 1)
                dve.wait_ge(rstd_step, 4 * q + 4)

            def block_stats(x0, loop=0, q=0):
                for dd in range(2):
                    dve.wait_ge(stat_done, x0 + dd + 1 + loop)
                    dve.tensor_reduce(ss_part[:, :, bass.ds(x0 % KC + dd + loop, 1)].rearrange("p t c -> p (t c)"),
                                      banks[(5, 7)[dd]][:, :].rearrange("p (t f) -> p t f", t=TB), AX.X,
                                      ALU.add).then_inc(ss_step, 1)

            def norm(q):
                norm_stats(q)
                rstd_diag(q)
                norm_apply(q)

            def rstd_diag(q):
                dve.tensor_tensor(tmpB[:, 0, :].rearrange("p (t n) -> p t n", t=TB),
                                  ident[:, :].unsqueeze(1).broadcast_to([P, TB, P]),
                                  rstd[:, :].unsqueeze(2).broadcast_to([P, TB, P]), ALU.mult).then_inc(diag_ready, 1)

            def norm_apply(q):
                dve.wait_ge(rstd_bc, q + 1)
                for k in range(KC + 1):
                    if k < KC:
                        if k >= 4:
                            dve.wait_ge(h_ready, KC * q + k - 3)
                        dve.scalar_tensor_tensor(out=norm_t(k), in0=banks[6][:, :], scalar=scale_a[:, q, k:k + 1],
                                                 in1=xT[:, k, :], op0=ALU.mult, op1=ALU.mult).then_inc(t_ready, 1)
                    if k >= 1:
                        c0 = 3 * KC * q + k - 1
                        dve.wait_ge(h_hi_ready, KC * q + k)
                        dve.scalar_tensor_tensor(out=h_lo[:, k - 1, :], in0=norm_t(k - 1), scalar=mod[:, c0:c0 + 1],
                                                 in1=h_hi[:, k - 1, :].bitcast(F32), op0=ALU.add,
                                                 op1=ALU.subtract).then_inc(h_ready, 1)

            def ada_pair(q, pair, batch, step, landed_):
                for k in range(KC):
                    for s in range(2):
                        acc, w, ck = ada_acc[2 * q + s], ada_ring[s][:, k, :], c_act[:, k:k + 1]
                        if k == 0:
                            dve.wait_ge(ada_landed[s], landed_)
                            dve.wait_ge(mod_ready, batch + 1)
                            dve.tensor_scalar(acc[:, :], w, ck, None, ALU.mult).then_inc(ada_step, 1)
                        else:
                            dve.wait_ge(ada_step, step + 2 * (k - 1) + s + 1)
                            dve.scalar_tensor_tensor(out=acc[:, :], in0=w, scalar=ck, in1=acc[:, :], op0=ALU.mult,
                                                     op1=ALU.add).then_inc(ada_step, 1)

            def ada_add(batch, col, n):
                dve.wait_ge(ada_mm, batch + 1)
                for s0 in range(0, n, TB):
                    m = min(n - s0, TB)
                    ins = dve.tensor_reduce(ada_col[:, s0:s0 + m],
                                            banks[4 if s0 == 0 else 6][:, 0:m * P].rearrange("p (s k) -> p s k", s=m),
                                            AX.X, ALU.add)
                ins.then_inc(ada_red, 1)
                dve.wait_ge(ada_red, batch + 1)
                dve.tensor_tensor(mod[:, bass.ds(col, n)], ada_col[:, 0:n], cols[:, bass.ds(col, n)], ALU.add)\
                   .then_inc(mod_ready, 1)

            def gu(fi, i, hid):
                base, bank0, hid0 = FFN_SLOT[fi], BANKS[fi], 2 * GU_IT * fi
                per = GU_PAIRS * PAIR_STEPS
                if fi == 0:
                    ada_pair(0, 0, i, per * i, 16 * GU_PAIRS * i + 16)
                lo(base + 2, 2 * i)
                if fi == 0:
                    ada_pair(1, 1, i, per * i + PAIR_STEPS, 16 * GU_PAIRS * i + 32)
                for f in range(2):
                    dve.wait_ge(slot_used, base + 2 + 2 * i)
                    dve.wait_ge(bank01_free, bank0 + 1 + f + 2 * i)
                    dve.tensor_tensor(tmpB[:, f, :], banks[2 + f][:, :], tmpA[:, f, :], ALU.mult)\
                       .then_inc(bank23_free, 1)
                for f in range(2):
                    dve.wait_ge(hid_hi_ready, hid0 + 1 + f + 2 * i)
                    dve.tensor_tensor(hid[1][:, 2 * i + f, :], tmpB[:, f, :],
                                      hid[0][:, 2 * i + f, :].bitcast(F32), ALU.subtract).then_inc(hid_ready, 1)
                lo(base + 3, 2 * i)
                if fi == 0:
                    ada_add(i, PRO_CHUNKS + 2 * GU_PAIRS * i, 2 * GU_PAIRS)

            def add_to_x(g, used, x0, bank, loop_used=0, loop_x=0):
                for dd in range(2):
                    dve.wait_ge(slot_used, used + loop_used)
                    blk = bass.ds(x0 % KC + dd + loop_x, 1)
                    dve.scalar_tensor_tensor(out=xT[:, blk, :], in0=banks[bank + dd][:, :].unsqueeze(1),
                                             scalar=gate_c[:, g, blk], in1=xT[:, blk, :],
                                             op0=ALU.mult, op1=ALU.add).then_inc(x_updated, 1)

            def down(fi, j, last=False):
                base, x0 = FFN_SLOT[fi] + 2 * GU_IT, 2 * KC * fi
                done, per = GU_IT * GU_PAIRS, DOWN_PAIRS * PAIR_STEPS
                for s in range(6):
                    if s % 3 == 2:
                        add_to_x(2 * fi, base + s + 1, x0 + 2 * (s // 3), s // 3 * 2, 6 * j, 4 * j)
                    if s == 5:
                        block_stats(x0 + 2, 4 * j)
                    if not (last and s >= 4):
                        lo(base + s + 2, 6 * j)
                    if s == 3:
                        block_stats(x0, 4 * j)
                    if fi == 0 and s % 2 == 0:
                        q = s // 2
                        ada_pair(q, done + q, GU_IT + j, PAIR_STEPS * (done + q) + per * j,
                                 16 * (done + q + 1) + 16 * DOWN_PAIRS * j)
                if fi == 0:
                    ada_add(GU_IT + j, PRO_CHUNKS + 2 * done + 2 * DOWN_PAIRS * j, 2 * DOWN_PAIRS)

            def coef(q, sem_):
                return dve.scalar_tensor_tensor(out=scale_a[:, q, :], in0=mod[:, (3 * q + 1) * KC:(3 * q + 2) * KC],
                                                scalar=1.0, in1=cols[:, GAIN + KC * q:GAIN + KC * (q + 1)],
                                                op0=ALU.add, op1=ALU.mult)

            def gate(q):
                return dve.tensor_scalar(gate_c[:, q, :], mod[:, (3 * q + 2) * KC:(3 * q + 3) * KC],
                                         1.0 if q == 1 else 0.5, None, ALU.mult)

            dve.wait_ge(rows_turned, 1)
            dve.tensor_copy(cols[:, :], banks[7][:, 0:112]).then_inc(cols_ready, 1)
            for k in range(KC):
                dve.wait_ge(x_turned, k + 1)
                dve.tensor_copy(xT[:, k, :], banks[k % 4][:, :]).then_inc(bank01_free if k % 4 < 2 else bank23_free, 1)
            lo(0)
            norm_stats(0)
            rstd_diag(0)
            dve.wait_ge(cact_ready, 1)
            for j in range(2):
                for k in range(KC):
                    w, ck = ada_pro[j][:, k, :], c_act[:, k:k + 1]
                    dve.wait_ge(pro_landed[j * KC + k], 16)
                    if k == 0:
                        dve.tensor_scalar(acc_pro[j][:, :], w, ck, None, ALU.mult).then_inc(pro_step, 1)
                    else:
                        dve.wait_ge(pro_step, j * KC + k)
                        dve.scalar_tensor_tensor(out=acc_pro[j][:, :], in0=w, scalar=ck, in1=acc_pro[j][:, :],
                                                 op0=ALU.mult, op1=ALU.add).then_inc(pro_step, 1)
            for n in range(4):
                dve.wait_ge(pro_turned, n + 1)
                ins = dve.tensor_reduce(ada_col[:, TB * n:TB * (n + 1)],
                                        banks[n][:, :].rearrange("p (s k) -> p s k", s=TB), AX.X, ALU.add)
            ins.then_inc(pro_red, 1)
            dve.wait_ge(pro_red, 1)
            dve.tensor_tensor(mod[:, 0:2 * KC], ada_col[:, :], cols[:, 0:2 * KC], ALU.add).then_inc(mod_ready, 1)
            dve.wait_ge(mod_ready, 1)
            coef(0, None).then_inc(coef_ready, 1)
            dve.wait_ge(coef_ready, 1)
            norm_apply(0)
            lo(1)
            with dve.Fori(0, GU_IT) as i:
                gu(0, i, hid1)
            dve.wait_ge(mod_ready, GU_IT + 1)
            gate(0).then_inc(coef_ready, 1)
            dve.wait_ge(coef_ready, 2)
            with dve.Fori(0, 2) as j:
                down(0, j)
            dve.wait_ge(mod_ready, GU_IT + 3)
            gate(1)
            gate(2)
            coef(1, None)
            coef(2, None).then_inc(coef_ready, 1)
            dve.wait_ge(coef_ready, 3)
            norm(1)

            dve.wait_ge(wf_hi_ready, 1)
            dve.tensor_tensor(wf_lo[:, 0:KC * FH], wf[:, :, :].rearrange("p k h -> p (k h)"),
                              wf_hi[:, 0:KC * FH].bitcast(F32), ALU.subtract).then_inc(wf_ready, 1)
            dve.wait_ge(mask_ready, 3)
            dve.tensor_copy(rel[:, :], i_rel[:, :])
            dve.tensor_scalar(i_and[:, :], i_rel[:, P:2 * P], DILATION[2] // DILATION[1] - 1, None, ALU.bitwise_and)\
               .then_inc(res_ready, 1)
            dve.wait_ge(res_ready, 1)
            dve.scalar_tensor_tensor(out=m_res[:, :], in0=i_and[:, :], scalar=NEG, in1=m_causal[:, :],
                                     op0=ALU.mult, op1=ALU.add).then_inc(res_ready, 1)

            def evac_qkv(m):
                for b in range(2):
                    dve.wait_ge(slot_used, S_MIX + m + 1)
                    src = banks[2 * (m % 2) + b]
                    if m < NG:
                        dve.tensor_copy(dv[m][:, 2 * b:2 * b + 2, :], src[:, :].rearrange("p (t e) -> p t e", t=2))\
                           .then_inc(qkv_evac, 1)
                        continue
                    g, is_k = (m - NG) // 2, (m - NG) % 2
                    dst = (dk if is_k else dq)[g][:, b, :]
                    view = src[:, :]
                    if g:
                        view = view.rearrange("p (i r) -> p r i", r=TB)
                        dst = dst.rearrange("p (r i) -> p r i", r=TB)
                    dve.tensor_scalar(dst, view, 1.0 if is_k else 0.125, None, ALU.mult).then_inc(qkv_evac, 1)

            for m in range(N_QKV):
                evac_qkv(m)
                lo(S_MIX + 2 + m)
                if m == 1:
                    dve.wait_ge(f_ready, 1)
                    dve.wait_ge(fb_landed, 16)
                    dve.tensor_scalar(f_x, banks[7][0:FH, :], fbias[:, 0:1], None, ALU.add).then_inc(f_step, 1)
                    dve.wait_ge(f_step, 1)
                    dve.tensor_scalar(ls_row, f_x, -1.0, None, ALU.mult).then_inc(f_step, 1)
                    dve.wait_ge(f_step, 2)
                    dve.tensor_tensor(f_abs, f_x, ls_row, ALU.min).then_inc(f_step, 1)
                if m == 3:
                    dve.memset(zeros_row, 0.0)
                    dve.wait_ge(f_act, 2)
                    dve.scalar_tensor_tensor(out=ls_row, in0=f_x, scalar=0.0, in1=f_abs, op0=ALU.min,
                                             op1=ALU.subtract).then_inc(f_step, 1)
                    dve.wait_ge(f_step, 4)
                    dve.tensor_tensor_scan(cum_row[:, :], zeros_row, ls_row, 0.0, ALU.add, ALU.add)\
                       .then_inc(cum_ready, 1)
                if m == 6:
                    dve.wait_ge(cum_turned, 1)
                    dve.tensor_copy(cum_col[:, :, :], banks[7][:, 0:TB * FH].rearrange("p (t h) -> p t h", t=TB))\
                       .then_inc(cumcol_ready, 1)

            n_bias, n_max = [0], [0]

            def alibi_tile(job, g, h):
                slope = -SLOPE[g * GH + h] * (DILATION[1] if g else 1)
                w, mask = (2 * P, m_band[:, :]) if g == 0 else (P, m_causal[:, :] if g == 1 else m_res[:, :])
                r = rel[:, :] if g == 0 else rel[:, P:2 * P]
                dve.scalar_tensor_tensor(out=alibi[:, job % 2, 0:w], in0=r, scalar=slope, in1=mask,
                                         op0=ALU.mult, op1=ALU.add).then_inc(alibi_ready, 1)
                dve.wait_ge(alibi_ready, job + 1)

            def bias_tile(u):
                job, g, h, subs = TILES[u]
                w = subs[-1][1] + subs[-1][2]
                S, B = banks[2 + u % 2], tmpA[:, u % 2, :]
                if g < 3 and (u == 0 or TILES[u - 1][0] != job):
                    alibi_tile(job, g, h)
                dve.wait_ge(scores_ready, u + 1)
                if u >= 2:
                    dve.wait_ge(probs_ready, u - 1)
                if g == 0 and subs[0][0] == 0:
                    dve.tensor_tensor(B[:, 0:P], S[:, 0:P], alibi[:, job % 2, P:2 * P], ALU.add)
                    dve.tensor_tensor(B[:, P:w], S[:, P:w], alibi[:, job % 2, :], ALU.add).then_inc(scores_read, 1)
                elif g < 3:
                    n = 2 if g == 0 else TB
                    dve.tensor_tensor(B[:, 0:w].rearrange("p (n c) -> p n c", n=n),
                                      S[:, 0:w].rearrange("p (n c) -> p n c", n=n),
                                      alibi[:, job % 2, 0:w // n].unsqueeze(1).broadcast_to([P, n, w // n]),
                                      ALU.add).then_inc(scores_read, 1)
                else:
                    dve.wait_ge(ck_free, h + 1)
                    for i_, (t, c0, ws) in enumerate(subs):
                        ins = dve.scalar_tensor_tensor(out=B[:, c0:c0 + ws], in0=S[:, c0:c0 + ws],
                                                       scalar=cum_col[:, t, h:h + 1], in1=ckb[h % 2][:, 0:ws],
                                                       op0=ALU.add, op1=ALU.add)
                    ins.then_inc(scores_read, 1)
                    dve.wait_ge(scores_read, u + 1)
                    for t, c0, ws in subs:
                        ins = dve.tensor_tensor(B[:, c0 + ws - P:c0 + ws], B[:, c0 + ws - P:c0 + ws], m_causal[:, :],
                                                ALU.add)
                    n_bias[0] += 1
                    ins.then_inc(bias_step, 1)
                    dve.wait_ge(bias_step, n_bias[0])
                dve.wait_ge(scores_read, u + 1)
                if g in (1, 2):
                    ins = dve.tensor_reduce(mx[:, g, :, h], B.rearrange("p (n c) -> p n c", n=TB), AX.X, ALU.max)
                else:
                    for t, c0, ws in subs:
                        ins = dve.tensor_reduce(mx[:, g, t, h:h + 1], B[:, c0:c0 + ws], AX.X, ALU.max)
                ins.then_inc(max_step, 1)
                dve.wait_ge(max_step, u + 1)
                t0, n = subs[0][0], len(subs)
                dve.tensor_scalar(nmx[:, u % 2, 0:n], mx[:, g, t0:t0 + n, h], -1.0, None, ALU.mult).then_inc(max_ready, 1)

            def finish_job(job):
                g, h = JOBS[job]
                dve.wait_ge(pv_ready, LAST_TILE[job] + 1)
                dve.reciprocal(rz[:, job % 2, :], zs[:, g, :, h]).then_inc(rz_ready, 1)
                dve.wait_ge(rz_ready, job + 1)
                dst = o_dil[:, g, :, h * E_:(h + 1) * E_] if g < 3 else o_fox[:, :, h * E_:(h + 1) * E_]
                dve.tensor_tensor(dst, banks[6 + job % 2][:, 0:TB * E_].rearrange("p (t e) -> p t e", t=TB),
                                  rz[:, job % 2, :].unsqueeze(2).broadcast_to([P, TB, E_]), ALU.mult).then_inc(o_free, 1)

            def evac_over(m, f):
                if f == 0:
                    dve.wait_ge(proj_ready, m + 1)
                else:
                    dve.wait_ge(slot_used, S_OVER + m + 1)
                free = p1_free if f else p0_free
                if m < 2:
                    dve.tensor_scalar(fq[:, 2 * m + f, :], banks[f][:, :], 0.125, None, ALU.mult).then_inc(free, 1)
                elif m < 4:
                    dve.tensor_copy(fk[:, 2 * (m - 2) + f, :], banks[f][:, :]).then_inc(free, 1)
                elif m < 6:
                    dve.tensor_copy(fv[:, 2 * f:2 * f + 2, (m - 4) * SC:(m - 3) * SC],
                                    banks[f][:, :].rearrange("p (t e) -> p t e", t=2)).then_inc(free, 1)
                else:
                    dve.tensor_copy(gates[:, 2 * (m - 6) + f, :], banks[f][:, :]).then_inc(free, 1)

            def per_head(ap):
                return ap.unsqueeze(2).broadcast_to([P, TB * GH, E_])

            def combine(s):
                def tt(out_, a, b, op):
                    dve.tensor_tensor(out_, a, b, op).then_inc(comb, 1)
                    n_comb[0] += 1
                    dve.wait_ge(comb, n_comb[0])

                od = [o_dil[:, g, :, :].rearrange("p t (h e) -> p (t h) e", h=GH) for g in range(NG)]
                if s == COMB_LN + 1:
                    dve.wait_ge(comb_act, 1)
                    tt(lse[:, :, :].rearrange("p g (t h) -> p g t h", t=TB), mx[:, 0:NG, :, 0:GH],
                       gw[:, :, :].rearrange("p g (t h) -> p g t h", t=TB), ALU.add)
                if s == COMB_EXP - 1:
                    dve.wait_ge(lse_in, 16)
                    tt(gmax[:, :], lse[:, 0, :], lse[:, 1, :], ALU.max)
                    tt(gmax[:, :], gmax[:, :], lse[:, 2, :], ALU.max)
                    tt(gw[:, :, :], lse[:, :, :], gmax[:, :].unsqueeze(1).broadcast_to([P, NG, TB * GH]), ALU.subtract)
                if s == COMB_EXP + 1:
                    dve.wait_ge(comb_act, 2)
                    tt(gsum[:, :], gw[:, 0, :], gw[:, 1, :], ALU.add)
                    tt(gsum[:, :], gsum[:, :], gw[:, 2, :], ALU.add)
                    dve.reciprocal(gmax[:, :], gsum[:, :]).then_inc(comb, 1)
                    n_comb[0] += 1
                    dve.wait_ge(comb, n_comb[0])
                    tt(gw[:, :, :], gw[:, :, :], gmax[:, :].unsqueeze(1).broadcast_to([P, NG, TB * GH]), ALU.mult)
                if s == COMB_EXP + 2:
                    tt(od[1], od[1], per_head(gw[:, 1, :]), ALU.mult)
                if s == COMB_EXP + 3:
                    tt(od[2], od[2], per_head(gw[:, 2, :]), ALU.mult)
                if s == COMB_EXP + 4:
                    tt(od[1], od[1], od[2], ALU.add)
                if s == COMB_EXP + 8:
                    dve.wait_ge(gw_in, 16)
                    tt(od[0], od[0], per_head(gw0[:, :]), ALU.mult)

            n_comb = [0]
            dve.wait_ge(res_ready, 2)
            dve.wait_ge(cumcol_ready, 1)
            for m in range(N_OVER):
                for j in range(3):
                    s = 3 * m + j
                    if j == 0 and m >= 1:
                        evac_over(m - 1, 1)
                    if 0 <= s - 1 < N_TILES:
                        bias_tile(s - 1)
                    if j == 0 and m >= 1:
                        lo(S_OVER + m + 1)
                    if j == 1:
                        evac_over(m, 0)
                    if s - 3 >= 0 and LAST_TILE[TILES[s - 3][0]] == s - 3:
                        finish_job(TILES[s - 3][0])
                    combine(s)
            evac_over(N_OVER - 1, 1)
            finish_job(TILES[N_TILES - 1][0])
            lo(S_OVER + N_OVER + 1)

            for fb in range(2):
                dve.wait_ge(y_turned, 2 * fb + 2)
                dve.wait_ge(y0_ready, fb + 1)
                dve.tensor_tensor(tmpB[:, fb, :].rearrange("p (i r) -> p r i", r=TB),
                                  banks[3 + 2 * fb][:, :].rearrange("p (r i) -> p r i", r=TB),
                                  tmpA[:, fb, :].rearrange("p (i r) -> p r i", r=TB), ALU.add).then_inc(ysum_ready, 1)
            for fc in range(4):
                dve.wait_ge(y_hi_ready, fc + 1)
                dve.tensor_tensor(y_lo[:, 2 + fc, :], banks[(6 + fc) % 8][:, :], y_hi[:, 2 + fc, :].bitcast(F32),
                                  ALU.subtract).then_inc(y_ready, 1)
            for fb in range(2):
                dve.wait_ge(y_hi_ready, 4 + fb + 1)
                dve.tensor_tensor(y_lo[:, fb, :], tmpB[:, fb, :], y_hi[:, fb, :].bitcast(F32), ALU.subtract)\
                   .then_inc(y_ready, 1)

            def merge_lo(d):
                dve.wait_ge(merge_hi, d + 1)
                dve.tensor_tensor(h_lo[:, d, :], tmpB[:, d % 2, :], h_hi[:, d, :].bitcast(F32), ALU.subtract)\
                   .then_inc(merged, 1)

            for d in range(KC):
                b0 = 4 * (d // 2 % 2) + 2 * (d % 2)
                if d % 2 == 0:
                    dve.wait_ge(br_ready, d // 2 + 1)
                else:
                    dve.wait_ge(slot_used, S_BR + d // 2 + 1)
                dve.wait_ge(sig_ready, d + 1)
                if d >= 1:
                    dve.wait_ge(msum_ready, d)
                for x_ in range(2):
                    dve.tensor_tensor(tmpA[:, x_, :], banks[b0 + x_][:, :], gates[:, KC * x_ + d, :], ALU.mult)\
                       .then_inc(merge_step, 1)
                dve.wait_ge(merge_step, 2 * d + 2)
                dve.tensor_tensor(tmpB[:, d % 2, :], tmpA[:, 0, :], tmpA[:, 1, :], ALU.add).then_inc(msum_ready, 1)
                if d >= 1:
                    merge_lo(d - 1)
                if d % 2 == 1:
                    lo(S_BR + d // 2 + 2)
            merge_lo(KC - 1)
            for d2 in range(N_OUT):
                if d2 >= 1:
                    block_stats(KC + 2 * (d2 - 1))
                add_to_x(1, S_OUT + d2 + 1, KC + 2 * d2, 2 * (d2 % 2))
                if d2 == N_OUT - 1:
                    block_stats(KC + 2 * d2)
                lo(S_OUT + d2 + 2)
            norm(2)
            with dve.Fori(0, GU_IT) as i:
                gu(1, i, hid2)
            for j in range(2):
                down(1, j, last=j == 1)
            norm_stats(3)
            for t in range(TB):
                dve.wait_ge(fin_turned, 2 * t + 2)
                dve.tensor_scalar(y_sb[:, t, T:2 * T], banks[FIN_BANK[t] + 1][:, :], rstd[:, t:t + 1], None, ALU.mult)\
                   .then_inc(y_dve, 1)

        @block.tensor
        def _(pe):
            def mm3(out_, a, b, first, last):
                pe.matmul(out_, a[0], b[0], start=first, stop=False)
                pe.matmul(out_, a[0], b[1], start=False, stop=False)
                return pe.matmul(out_, a[1], b[0], start=False, stop=last)

            def w_blk(n, k, f, at=0):
                c0 = at + k * SC + f * P
                return w_hi[n % 2][:, c0:c0 + P], w_lo[n % 2][:, c0:c0 + P]

            def h_blk(k, sl=slice(0, T)):
                return h_hi[:, k, sl], h_lo[:, k, sl]

            def gate_up(fi, i):
                base, bank0, q = FFN_SLOT[fi], BANKS[fi], 2 * fi
                for j in range(2):
                    n = base + j
                    pe.wait_ge(split_done, n + 1 + 2 * i)
                    pe.wait_ge(bank23_free if j else bank01_free, bank0 + 2 * i)
                    for k in range(KC):
                        if j == 0:
                            pe.wait_ge(h_ready, KC * q + k + 1)
                        for f in range(2):
                            last = mm3(banks[2 * j + f][:, :], w_blk(n, k, f), h_blk(k), k == 0, k == KC - 1)
                    last.then_inc(slot_used, 1)
                if fi == 0:
                    per = GU_PAIRS * PAIR_STEPS
                    ada_sum(i, per * i + per, 2 * GU_PAIRS)

            def ada_sum(batch, step, n):
                pe.wait_ge(ada_step, step)
                pe.wait_ge(mod_ready, batch + 1)
                for s in range(n):
                    last = pe.transpose(banks[4 if s < TB else 6][:, s % TB * P:(s % TB + 1) * P], ada_acc[s][:, :],
                                        ident[:, :])
                last.then_inc(ada_mm, 1)

            def stats(x0, loop=0):
                for dd in range(2):
                    pe.wait_ge(sq_ready, x0 + dd + 1 + loop)
                    for t in range(TB):
                        last = pe.transpose(banks[(5, 7)[dd]][:, t * P:(t + 1) * P], tmpA[:, dd, t * P:(t + 1) * P],
                                            ident[:, :])
                    last.then_inc(stat_done, 1)

            def down(fi, j, hid):
                base, x0, hid0 = FFN_SLOT[fi] + 2 * GU_IT, 2 * KC * fi, 2 * GU_IT * fi
                pe.wait_ge(bank01_free, BANKS[fi] + 2 * GU_IT)
                pe.wait_ge(bank23_free, BANKS[fi] + 2 * GU_IT)
                for s in range(6):
                    n, (k0, nk) = base + s, DOWN_PARTS[s % 3]
                    pe.wait_ge(split_done, n + 1 + 6 * j)
                    pe.wait_ge(hid_ready, hid0 + min(k0 + nk, FB))
                    for k in range(nk):
                        for dd in range(2):
                            last = mm3(banks[2 * (s // 3) + dd][:, :], w_blk(n, k, dd),
                                       (hid[0][:, k0 + k, :], hid[1][:, k0 + k, :]), k0 + k == 0, k0 + k == FB - 1)
                    last.then_inc(slot_used, 1)
                    if s == 3:
                        stats(x0, 4 * j)
                stats(x0 + 2, 4 * j)
                if fi == 0:
                    done, per = GU_IT * GU_PAIRS * PAIR_STEPS, DOWN_PAIRS * PAIR_STEPS
                    ada_sum(GU_IT + j, done + per + per * j, 2 * DOWN_PAIRS)

            def rstd_rows(q):
                pe.wait_ge(diag_ready, q + 1)
                pe.matmul(banks[6][:, :], ones[:, :], tmpB[:, 0, :], start=True, stop=True).then_inc(rstd_bc, 1)

            pe.wait_ge(const_ready, 2)
            pe.wait_ge(rows_landed, 16 * 6)
            pe.transpose(banks[7][:, 0:112], rows[:, :], ident[0:112, 0:112]).then_inc(rows_turned, 1)
            for k in range(KC):
                if k >= 4:
                    pe.wait_ge(bank01_free if k % 4 < 2 else bank23_free, k % 2 + 1)
                for t in range(TB):
                    if k == 0:
                        pe.wait_ge(x_landed[t], 16)
                    last = pe.transpose(banks[k % 4][:, t * P:(t + 1) * P], x_nat[:, t, k * P:(k + 1) * P], ident[:, :])
                last.then_inc(x_turned, 1)
            rstd_rows(0)
            pe.wait_ge(bank01_free, 4)
            pe.wait_ge(bank23_free, 4)
            for j in range(2):
                pe.wait_ge(pro_step, (j + 1) * KC)
                for n in range(2 * j, 2 * j + 2):
                    for s in range(TB):
                        c0 = (n % 2 * TB + s) * P
                        last = pe.transpose(banks[n][:, s * P:(s + 1) * P], acc_pro[j][:, c0:c0 + P], ident[:, :])
                    last.then_inc(pro_turned, 1)
            with pe.Fori(0, GU_IT) as i:
                gate_up(0, i)
            with pe.Fori(0, 2) as j:
                down(0, j, hid1)
            rstd_rows(1)

            def tokens(g, t):
                return slice(t * P, (t + 1) * P) if g == 0 else slice(t, T, TB)

            for m in range(N_QKV):
                n = S_MIX + m
                pe.wait_ge(split_done, n + 1)
                if m >= 2:
                    pe.wait_ge(qkv_evac, 2 * (m - 1))
                b0 = 2 * (m % 2)
                if m < NG:
                    for t in range(TB):
                        for k in range(KC):
                            if m == 0 and t == 0:
                                pe.wait_ge(h_ready, KC + k + 1)
                            at = k * SC
                            last = mm3(banks[b0 + t // 2][:, t % 2 * SC:(t % 2 + 1) * SC], h_blk(k, tokens(m, t)),
                                       (w_hi[n % 2][:, at:at + SC], w_lo[n % 2][:, at:at + SC]), k == 0, k == KC - 1)
                else:
                    for f in range(2):
                        for k in range(KC):
                            last = mm3(banks[b0 + f][:, :], w_blk(n, k, f), h_blk(k), k == 0, k == KC - 1)
                last.then_inc(slot_used, 1)
                if m == 0:
                    pe.wait_ge(wf_ready, 1)
                    pe.wait_ge(wf_zero, 2)
                    for k in range(KC):
                        w = slice(k * FH, k * FH + P)
                        last = mm3(banks[7][:, :], (wf_hi[:, w], wf_lo[:, w]), h_blk(k), k == 0, k == KC - 1)
                    last.then_inc(f_ready, 1)
                if m == 5:
                    pe.wait_ge(cum_ready, 1)
                    for t in range(TB):
                        last = pe.transpose(banks[7][:, t * FH:(t + 1) * FH], cum_row[:, t * P:(t + 1) * P],
                                            ident[0:FH, 0:FH])
                    last.then_inc(cum_turned, 1)

            def scores(u):
                job, g, h, subs = TILES[u]
                if u >= 2:
                    pe.wait_ge(scores_read, u - 1)
                p0 = h % 2 * E_
                q, kk = (dq[g], dk[g]) if g < 3 else (fq, fk)
                for t, c0, w in subs:
                    k0 = key_blocks(g, t)[0] * P
                    last = pe.matmul(banks[2 + u % 2][:, c0:c0 + w], q[p0:p0 + E_, h // 2, t * P:(t + 1) * P],
                                     kk[p0:p0 + E_, h // 2, k0:k0 + w], start=True, stop=True)
                last.then_inc(scores_ready, 1)

            def turn_probs(u):
                _, _, _, subs = TILES[u]
                pe.wait_ge(probs_ready, u + 1)
                if u >= 2:
                    pe.wait_ge(pT_ready, u - 1)
                for c0 in range(0, subs[-1][1] + subs[-1][2], P):
                    last = pe.transpose(banks[4 + u % 2][:, c0:c0 + P], tmpB[:, u % 2, c0:c0 + P], ident[:, :])
                last.then_inc(turned, 1)

            def values(u):
                job, g, h, subs = TILES[u]
                pe.wait_ge(pT_ready, u + 1)
                if job >= 2:
                    pe.wait_ge(o_free, job - 1)
                if u == FIRST_FOX:
                    pe.wait_ge(p0_free, 6)
                    pe.wait_ge(p1_free, 6)
                for t, c0, w in subs:
                    blocks = key_blocks(g, t)
                    for i_, b in enumerate(blocks):
                        v = dv[g][:, b, h * E_:(h + 1) * E_] if g < 3 else fv[:, b, h * E_:(h + 1) * E_]
                        last = pe.matmul(banks[6 + job % 2][:, t * E_:(t + 1) * E_],
                                         pT[:, u % 2, c0 + i_ * P:c0 + (i_ + 1) * P], v,
                                         start=i_ == 0, stop=i_ == len(blocks) - 1)
                last.then_inc(pv_ready, 1)

            pe.wait_ge(qkv_evac, 2 * N_QKV)
            for m in range(N_OVER):
                n = S_OVER + m
                pe.wait_ge(split_done, n + 1)
                steps = []
                for f in range(2):
                    if m in (4, 5):
                        steps += [(f, t, k) for t in (2 * f, 2 * f + 1) for k in range(KC)]
                    else:
                        steps += [(f, None, k) for k in range(KC)]
                third = -(-len(steps) // 3)
                for j in range(3):
                    for f, t, k in steps[j * third:(j + 1) * third]:
                        if k == 0 and (t is None or t % 2 == 0):
                            if m >= 1:
                                pe.wait_ge(p1_free if f else p0_free, m)
                            if f == 0 and 0 <= m - 1 - 4 < FH:
                                pe.wait_ge(ck_free, m - 4)
                        if t is None:
                            last = mm3(banks[f][:, :], w_blk(n, k, f), h_blk(k), k == 0, k == KC - 1)
                        else:
                            last = mm3(banks[f][:, t % 2 * SC:(t % 2 + 1) * SC], h_blk(k, slice(t * P, (t + 1) * P)),
                                       (w_hi[n % 2][:, k * SC:(k + 1) * SC], w_lo[n % 2][:, k * SC:(k + 1) * SC]),
                                       k == 0, k == KC - 1)
                        if k == KC - 1 and t in (None, 1, 3):
                            last.then_inc(slot_used if f else proj_ready, 1)
                    s = 3 * m + j
                    if j == 2 and 4 <= m < 4 + FH:
                        pe.wait_ge(p0_free, m + 1)
                        pe.matmul(banks[0][:, :], nsel[:, m - 4, :], cum_row[:, :], start=True, stop=True)\
                          .then_inc(ck_ready, 1)
                    if 0 <= s - 2 < N_TILES:
                        values(s - 2)
                    if 0 <= s - 1 < N_TILES:
                        turn_probs(s - 1)
                    if s < N_TILES:
                        scores(s)

            pe.wait_ge(comb, 12)
            pe.wait_ge(o_free, len(JOBS))
            pe.wait_ge(p0_free, N_OVER)
            pe.wait_ge(p1_free, N_OVER)
            for fb in range(2):
                for g in range(2):
                    for t in range(TB):
                        last = pe.transpose(banks[2 + 2 * fb + g][:, t * P:(t + 1) * P],
                                            o_dil[:, g, t, fb * P:(fb + 1) * P], ident[:, :])
                    last.then_inc(y_turned, 1)
            for fc in range(4):
                for t in range(TB):
                    last = pe.transpose(banks[(6 + fc) % 8][:, t * P:(t + 1) * P], o_fox[:, t, fc * P:(fc + 1) * P],
                                        ident[:, :])
                last.then_inc(y_turned, 1)
            pe.wait_ge(y_ready, 6)
            for d2 in range(N_BR):
                n = S_BR + d2
                pe.wait_ge(split_done, n + 1)
                if d2 >= 2:
                    pe.wait_ge(msum_ready, 2 * (d2 - 1))
                for dd in range(2):
                    b0 = 4 * (d2 % 2) + 2 * dd
                    for k in range(2):
                        mm3(banks[b0][:, :], w_blk(n, k, dd), (y_hi[:, k, :], y_lo[:, k, :]), k == 0, k == 1)
                    for k in range(4):
                        last = mm3(banks[b0 + 1][:, :], w_blk(n, k, dd, at=2 * SC),
                                   (y_hi[:, 2 + k, :], y_lo[:, 2 + k, :]), k == 0, k == 3)
                    last.then_inc(slot_used if dd else br_ready, 1)
            for d2 in range(N_OUT):
                n = S_OUT + d2
                pe.wait_ge(split_done, n + 1)
                if d2 >= 2:
                    pe.wait_ge(x_updated, KC + 2 * (d2 - 1))
                for k in range(KC):
                    if d2 == 0:
                        pe.wait_ge(merged, k + 1)
                    for dd in range(2):
                        last = mm3(banks[2 * (d2 % 2) + dd][:, :], w_blk(n, k, dd), h_blk(k), k == 0, k == KC - 1)
                    if k == 3 and d2 >= 1:
                        stats(KC + 2 * (d2 - 1))
                last.then_inc(slot_used, 1)
            stats(KC + 2 * (N_OUT - 1))
            rstd_rows(2)
            with pe.Fori(0, GU_IT) as i:
                gate_up(1, i)
            with pe.Fori(0, 2) as j:
                down(1, j, hid2)
            pe.wait_ge(xg_ready, KC)
            pe.wait_ge(var_ready, 4)
            for t in range(TB):
                for half in range(2):
                    for k in range(4):
                        last = pe.transpose(banks[FIN_BANK[t] + half][:, k * P:(k + 1) * P],
                                            xT[:, 4 * half + k, t * P:(t + 1) * P], ident[:, :])
                    last.then_inc(fin_turned, 1)


_INS = ["x", "c", "ada_w", "ada_b", "norm_ffn1", "ffn1_w_gate", "ffn1_w_up", "ffn1_w_down", "norm_mix", "w_in",
        "forget_bias", "w_branch_a", "w_branch_b", "w_out", "norm_ffn2", "ffn2_w_gate", "ffn2_w_up", "ffn2_w_down",
        "norm_final"]


def kernel(**inputs):
    import numpy as _np
    import concourse.bacc as _bacc
    from concourse import mybir as _mybir
    from concourse.bass_utils import run_bass_kernel_spmd as _run

    nc = _bacc.Bacc("TRN2", target_bir_lowering=False, num_devices=1)
    arrays, args = {}, []
    for name in _INS:
        a = _np.ascontiguousarray(inputs[name])
        if name != "norm_final":
            a = a[0]
        arrays[f"in_{name}"] = a
        args.append(nc.dram_tensor(f"in_{name}", a.shape, _mybir.dt.from_np(a.dtype), kind="ExternalInput").ap())
    args.append(nc.dram_tensor("out_y", (T, D), F32, kind="ExternalOutput").ap())
    build(nc, *args)
    r = _run(nc, [arrays], core_ids=[0])
    return r.results[0]["out_y"].reshape(1, T, D)
```

```python
from contextlib import ExitStack

import concourse.bass as bass
from concourse import mybir

F32 = mybir.dt.float32
F32R = mybir.dt.float32r
I32 = mybir.dt.int32
ALU = mybir.AluOpType
ACT = mybir.ActivationFunctionType
AX = mybir.AxisListType

P = 128
D = 1024
T = 512
KC = D // P
TB = T // P
DFF = 2816
FB = DFF // P
SC = 256
E_ = 64
NG, GH, FH = 3, 4, 8
DILW, FOXW = NG * GH * E_, FH * E_
DILATION = (1, 4, 16)
EPS = 1e-6
NEG = -1e30
COL_Q, COL_K, COL_V = 0, DILW, 2 * DILW
COL_FQ = 3 * DILW
COL_FK, COL_FV, COL_F = COL_FQ + FOXW, COL_FQ + 2 * FOXW, COL_FQ + 3 * FOXW
COL_GA = COL_F + FH

GU_IT = DFF // SC
DOWN_PARTS = ((0, 8), (8, 8), (16, 6))
N_DOWN = (D // SC) * len(DOWN_PARTS)
N_FFN = 2 * GU_IT + N_DOWN
N_QKV, N_OVER, N_BR, N_OUT = 9, 14, 4, 4
S_MIX = N_FFN
S_OVER = S_MIX + N_QKV
S_BR = S_OVER + N_OVER
S_OUT = S_BR + N_BR
S_FFN2 = S_OUT + N_OUT
N_SLOTS = S_FFN2 + N_FFN

PRO_CHUNKS = 2 * KC
GU_PAIRS, DOWN_PAIRS = 2, 3
PAIR_STEPS = 2 * KC
ADA_REST = ((GU_IT - 1, GU_PAIRS, (), 1), (GU_IT, DOWN_PAIRS, (1, 2, 3), 5), (GU_IT + 1, DOWN_PAIRS, (6, 7, 8), 10))

SLOPE = [2.0 ** (-8.0 * (i + 1) / (NG * GH)) for i in range(NG * GH)]


def attention_tiles():
    tiles, job = [], 0
    for h in range(GH):
        tiles.append((job, 0, h, [(0, 0, P), (1, P, 2 * P)]))
        tiles.append((job, 0, h, [(2, 0, 2 * P), (3, 2 * P, 2 * P)]))
        job += 1
    for g in (1, 2):
        for h in range(GH):
            tiles.append((job, g, h, [(r, r * P, P) for r in range(TB)]))
            job += 1
    for h in range(FH):
        tiles.append((job, 3, h, [(0, 0, P), (1, P, 2 * P)]))
        tiles.append((job, 3, h, [(2, 0, 3 * P)]))
        tiles.append((job, 3, h, [(3, 0, 4 * P)]))
        job += 1
    return tiles


TILES = attention_tiles()
N_TILES = len(TILES)
LAST_TILE = {}
for _u, _t in enumerate(TILES):
    LAST_TILE[_t[0]] = _u
FIRST_FOX = 2 * GH + 2 * GH
QKV = [("q", 0), ("v", 0), ("v", 1), ("v", 2), ("k", 0), ("q", 1), ("k", 1), ("q", 2), ("k", 2)]
PRO_PE = (1, 3, 5)
PRO_DVE = (0, 2, 4, 6, 7)
COMB_LN, COMB_EXP = FIRST_FOX + 4, FIRST_FOX + 11
FIN_BANK = (0, 2, 6, 4)
JOBS = {t[0]: (t[1], t[2]) for t in TILES}


def mixer_columns():
    cols_ = [{"q": COL_Q, "k": COL_K, "v": COL_V}[what] + SC * g for what, g in QKV]
    for c0 in (COL_FQ, COL_FK, COL_FV):
        cols_ += [c0, c0 + SC]
    return cols_ + [COL_GA + SC * j for j in range(2 * D // SC)]


def key_blocks(group, t):
    if group == 0:
        return [t] if t == 0 else [t - 1, t]
    if group in (1, 2):
        return [t]
    return list(range(t + 1))


def build(nc, x, c, ada_w, ada_b, norm_ffn1, w_gate1, w_up1, w_down1, norm_mix, w_in, forget_bias,
          w_branch_a, w_branch_b, w_out, norm_ffn2, w_gate2, w_up2, w_down2, norm_final, out):
    ctx = ExitStack()
    with ctx:
        def sb(name, shape, dt=F32, where=ctx):
            return where.enter_context(nc.sbuf_tensor(name, shape, dt))

        def sem(name):
            return ctx.enter_context(nc.semaphore(name))

        GAIN = 9 * KC
        xT = sb("xT", [P, KC, T])
        h_hi = sb("h_hi", [P, KC, T], F32R)
        h_lo = sb("h_lo", [P, KC, T], F32R)
        raw = [sb(f"raw{s}", [P, KC * SC]) for s in range(2)]
        w_hi = [sb(f"w_hi{s}", [P, KC * SC], F32R) for s in range(2)]
        w_lo = [sb(f"w_lo{s}", [P, KC * SC], F32R) for s in range(2)]
        tmpA = sb("tmpA", [P, 2, T])
        tmpB = sb("tmpB", [P, 2, T])
        ident = sb("ident", [P, P])
        half_neg = sb("half_neg", [P, P])
        c_rows = sb("c_rows", [KC, P])
        rows = sb("rows", [GAIN + 4 * KC, P])
        cols = sb("cols", [P, GAIN + 4 * KC])
        c_act = sb("c_act", [P, KC])
        mod = sb("mod", [P, 9 * KC])
        scale_a = sb("scale_a", [P, 3, KC])
        gate_c = sb("gate_c", [P, 3, KC])
        ada_col = sb("ada_col", [P, 2 * KC])
        ss = sb("ss", [P, TB])
        var = sb("var", [P, TB])
        std = sb("std", [P, TB])
        r0 = sb("r0", [P, TB])
        nw = sb("nw", [P, TB])
        rstd_m2 = sb("rstd_m2", [P, TB])
        rstd = sb("rstd", [P, TB])
        mod_part = sb("mod_part", [P, 2 * KC])
        ss_part = sb("ss_part", [P, TB, KC])
        fbias = sb("fbias", [FH, 1])

        banks = [ctx.enter_context(nc.psum_tensor(f"bank{i}", [P, T], F32)) for i in range(8)]

        ffn1 = ExitStack()
        ada_ring = sb("ada_ring", [P, KC, 2 * P], where=ffn1)
        ada_acc = [sb(f"ada_acc{s}", [P, P], where=ffn1) for s in range(2 * DOWN_PAIRS)]
        pro = ExitStack()
        x_nat = sb("x_nat", [P, TB, D], where=pro)
        ada_pro = [sb(f"ada_pro{s}", [P, KC, D], where=pro) for s in range(2)]
        acc_pro = [sb(f"acc_pro{s}", [P, D], where=pro) for s in range(2)]
        pro.close()
        hid1 = [sb(f"hid1_{s}", [P, FB, T], F32R, where=ffn1) for s in ("hi", "lo")]
        ffn1.close()

        mix = ExitStack()
        dil = sb("dil", [P, 9 * 2 * T], where=mix)
        dq = [dil[:, (g * 6) * T:(g * 6 + 2) * T].rearrange("p (c t) -> p c t", c=2) for g in range(NG)]
        dk = [dil[:, (g * 6 + 2) * T:(g * 6 + 4) * T].rearrange("p (c t) -> p c t", c=2) for g in range(NG)]
        dv = [dil[:, (g * 6 + 4) * T:(g * 6 + 6) * T].rearrange("p (t e) -> p t e", t=TB) for g in range(NG)]
        ckb = [dil[:, s * T:(s + 1) * T] for s in range(2)]
        gates = dil[:, 2 * T:18 * T].rearrange("p (c t) -> p c t", c=16)
        o_dil = sb("o_dil", [P, NG, TB, GH * E_], where=mix)
        o_fox = sb("o_fox", [P, TB, FOXW], where=mix)
        pT = sb("pT", [P, 2, T], where=mix)
        alibi = sb("alibi", [P, 2, 2 * P], where=mix)
        rel = sb("rel", [P, 2 * P], where=mix)
        m_band = sb("m_band", [P, 2 * P], where=mix)
        m_causal = sb("m_causal", [P, P], where=mix)
        m_res = sb("m_res", [P, P], where=mix)
        i_rel = sb("i_rel", [P, 2 * P], I32, where=mix)
        i_and = sb("i_and", [P, P], I32, where=mix)
        nsel = sb("nsel", [FH, FH, P], where=mix)
        wf = sb("wf", [P, KC, FH], where=mix)
        wf_hi = sb("wf_hi", [P, KC * FH + P], F32R, where=mix)
        wf_lo = sb("wf_lo", [P, KC * FH + P], F32R, where=mix)
        f_x, f_abs, ls_row, zeros_row = tmpA[0:FH, 0, :], tmpA[0:FH, 1, :], tmpB[0:FH, 0, :], tmpB[0:FH, 1, :]
        cum_row = sb("cum_row", [FH, T], where=mix)
        cum_col = sb("cum_col", [P, TB, FH], where=mix)
        mx = sb("mx", [P, 4, TB, FH], where=mix)
        nmx = sb("nmx", [P, 2, TB], where=mix)
        zs = sb("zs", [P, 4, TB, FH], where=mix)
        rz = sb("rz", [P, 2, TB], where=mix)
        lse = sb("lse", [P, NG, TB * GH], where=mix)
        gmax = sb("gmax", [P, TB * GH], where=mix)
        gw = sb("gw", [P, NG, TB * GH], where=mix)
        gsum = sb("gsum", [P, TB * GH], where=mix)
        gw0 = sb("gw0", [P, TB * GH], where=mix)
        foxmem = ExitStack()
        fq = sb("fq", [P, 4, T], where=foxmem)
        fk = sb("fk", [P, 4, T], where=foxmem)
        fv = sb("fv", [P, TB, FOXW], where=foxmem)
        foxmem.close()
        ybr = ExitStack()
        y_hi = sb("y_hi", [P, 6, T], F32R, where=ybr)
        y_lo = sb("y_lo", [P, 6, T], F32R, where=ybr)
        ybr.close()
        mix.close()

        ffn2 = ExitStack()
        hid2 = [sb(f"hid2_{s}", [P, FB, T], F32R, where=ffn2) for s in ("hi", "lo")]
        ffn2.close()
        fin = ExitStack()
        y_sb = sb("y_sb", [P, TB, D], where=fin)
        fin.close()

        lse_dram = nc.dram_tensor("lse_scratch", [T, GH], F32).ap()
        gw_dram = nc.dram_tensor("gw_scratch", [T, GH], F32).ap()

        raw_landed = [sem(f"raw_landed{s}") for s in range(2)]
        br_b_landed = [sem(f"br_b_landed{s}") for s in range(2)]
        split_hi = sem("split_hi")
        split_done = sem("split_done")
        slot_used = sem("slot_used")
        bank01_free = sem("bank01_free")
        bank23_free = sem("bank23_free")
        hid_hi_ready, hid_ready = sem("hid_hi_ready"), sem("hid_ready")
        half_done = sem("half_done")
        x_updated = sem("x_updated")
        sq_ready, stat_done = sem("sq_ready"), sem("stat_done")
        ident_step, const_ready = sem("ident_step"), sem("const_ready")
        rows_landed, fb_landed = sem("rows_landed"), sem("fb_landed")
        x_landed = [sem(f"x_landed{t}") for t in range(TB)]
        c_landed, c_turned, cact_ready = sem("c_landed"), sem("c_turned"), sem("cact_ready")
        rows_turned, cols_ready = sem("rows_turned"), sem("cols_ready")
        x_turned, ss_ready = sem("x_turned"), sem("ss_ready")
        pro_landed = [sem(f"pro_landed{k}") for k in range(2 * KC)]
        ada_landed = [sem(f"ada_landed{s}") for s in range(2)]
        pro_step, pro_turned, pro_red = sem("pro_step"), sem("pro_turned"), sem("pro_red")
        pro_mm, scale1_ready = sem("pro_mm"), sem("scale1_ready")
        ada_step = sem("ada_step")
        ada_red = sem("ada_red")
        ada_mm = sem("ada_mm")
        mod_ready = sem("mod_ready")
        coef_ready = sem("coef_ready")
        ss_step, neg_step = sem("ss_step"), sem("neg_step")
        rstd_ready = sem("rstd_ready")
        var_ready, std_ready, rstd_step = sem("var_ready"), sem("std_ready"), sem("rstd_step")
        rstd_bc = sem("rstd_bc")
        t_ready, h_hi_ready, h_ready = sem("t_ready"), sem("h_hi_ready"), sem("h_ready")
        qkv_evac = sem("qkv_evac")
        mask_step, mask_ready, res_ready = sem("mask_step"), sem("mask_ready"), sem("res_ready")
        wf_zero = sem("wf_zero")
        wf_landed, wf_hi_ready, wf_ready = sem("wf_landed"), sem("wf_hi_ready"), sem("wf_ready")
        f_ready, f_step, f_act = sem("f_ready"), sem("f_step"), sem("f_act")
        cum_ready = sem("cum_ready")
        cum_turned, cumcol_ready = sem("cum_turned"), sem("cumcol_ready")
        proj_ready = sem("proj_ready")
        p0_free, p1_free = sem("p0_free"), sem("p1_free")
        ck_ready, ck_free = sem("ck_ready"), sem("ck_free")
        scores_ready = sem("scores_ready")
        alibi_ready, bias_step = sem("alibi_ready"), sem("bias_step")
        scores_read = sem("scores_read")
        max_step, max_ready = sem("max_step"), sem("max_ready")
        probs_ready, turned, pT_ready = sem("probs_ready"), sem("turned"), sem("pT_ready")
        pv_ready, rz_ready, o_free = sem("pv_ready"), sem("rz_ready"), sem("o_free")
        comb, comb_act = sem("comb"), sem("comb_act")
        lse_out, lse_in, gw_out, gw_in = sem("lse_out"), sem("lse_in"), sem("gw_out"), sem("gw_in")
        y_turned, y0_ready, ysum_ready = sem("y_turned"), sem("y0_ready"), sem("ysum_ready")
        y_hi_ready, y_ready = sem("y_hi_ready"), sem("y_ready")
        sig_ready, br_ready = sem("sig_ready"), sem("br_ready")
        merge_step, msum_ready, merge_hi, merged = sem("merge_step"), sem("msum_ready"), sem("merge_hi"), sem("merged")
        xg_ready, fin_turned = sem("xg_ready"), sem("fin_turned")
        y_act, y_dve, out_done = sem("y_act"), sem("y_dve"), sem("out_done")

        BANKS = (KC // 2, KC // 2 + 2 * GU_IT)
        FFN_SLOT = (0, S_FFN2)
        N_PAIRS = GU_IT * GU_PAIRS + 2 * DOWN_PAIRS
        assert PRO_CHUNKS + 2 * N_PAIRS == 9 * KC

        def slot_size(n):
            for base in FFN_SLOT:
                if base + 2 * GU_IT <= n < base + N_FFN and (n - base - 2 * GU_IT) % 3 == 2:
                    return DOWN_PARTS[2][1] * SC
            return 6 * SC if S_BR <= n < S_OUT else KC * SC

        def landed(eng, n, loop=0):
            eng.wait_ge(raw_landed[n % 2], 16 * (n // 2 + 1) + loop)
            if S_BR <= n < S_OUT:
                eng.wait_ge(br_b_landed[n % 2], 16 * ((n - S_BR) // 2 + 1))

        def norm_t(k):
            return (tmpA, tmpB)[k // 2 % 2][:, k % 2, :]

        block = ctx.enter_context(nc.Block())

        @block.sync
        def _(sp):
            def rows_of(w):
                return w.rearrange("(k p) c -> p k c", p=P)

            def slot_dst(n, nk, at=0):
                return raw[n % 2][:, at:at + nk * SC].rearrange("p (k c) -> p k c", k=nk)

            def load(n, nk, src, loop=0):
                if n >= 2:
                    sp.wait_ge(split_done, n - 1 + loop)
                sp.dma_start(slot_dst(n, nk), src).then_inc(raw_landed[n % 2], 16)

            def gate_up(base, wg, wu, i):
                for j, w in enumerate((wg, wu)):
                    load(base + j, KC, rows_of(w)[:, :, bass.ds(SC * i, SC)], 2 * i)

            def gate_up_from1(wg, wu, i):
                for j, w in enumerate((wg, wu)):
                    load(2 + j, KC, rows_of(w)[:, :, bass.ds(SC * i + SC, SC)], 2 * i)

            def down(base, w, j):
                for s in range(6):
                    k0, nk = DOWN_PARTS[s % 3]
                    load(base + s, nk, rows_of(w)[:, k0:k0 + nk, bass.ds(2 * SC * j + SC * (s // 3), SC)], 6 * j)

            sp.dma_start(c_rows[:, :], c.rearrange("(r p) -> r p", p=P)).then_inc(c_landed, 16)
            for t in range(TB):
                sp.dma_start(x_nat[:, t, :], x[t * P:(t + 1) * P, :]).then_inc(x_landed[t], 16)
            for j in (1, 0):
                for k in range(KC):
                    sp.dma_start(ada_pro[j][:, k, :], ada_w[k * P:(k + 1) * P, j * D:(j + 1) * D])\
                      .then_inc(pro_landed[j * KC + k], 16)
                if j == 1:
                    load(0, KC, rows_of(w_gate1)[:, :, 0:SC])
            load(1, KC, rows_of(w_up1)[:, :, 0:SC])
            with sp.Fori(0, GU_IT - 1) as i:
                gate_up_from1(w_gate1, w_up1, i)
            with sp.Fori(0, 2) as j:
                down(2 * GU_IT, w_down1, j)
            for m, col in enumerate(mixer_columns()):
                load(S_MIX + m, KC, rows_of(w_in)[:, :, col:col + SC])
                if m == 1:
                    sp.wait_ge(slot_used, N_FFN)
                    sp.dma_start(wf[:, :, :], rows_of(w_in)[:, :, COL_F:COL_F + FH]).then_inc(wf_landed, 16)
            for d2 in range(N_BR):
                n = S_BR + d2
                load(n, 2, rows_of(w_branch_a)[:, :, d2 * SC:(d2 + 1) * SC])
                sp.dma_start(slot_dst(n, 4, at=2 * SC), rows_of(w_branch_b)[:, :, d2 * SC:(d2 + 1) * SC])\
                  .then_inc(br_b_landed[n % 2], 16)
            for d2 in range(N_OUT):
                load(S_OUT + d2, KC, rows_of(w_out)[:, :, d2 * SC:(d2 + 1) * SC])
            with sp.Fori(0, GU_IT) as i:
                gate_up(S_FFN2, w_gate2, w_up2, i)
            with sp.Fori(0, 2) as j:
                down(S_FFN2 + 2 * GU_IT, w_down2, j)
            for t in range(TB):
                sp.wait_ge(y_act, t + 1)
                sp.wait_ge(y_dve, t + 1)
                sp.dma_start(out[t * P:(t + 1) * P, :], y_sb[:, t, :]).then_inc(out_done, 16)
            sp.wait_ge(out_done, 16 * TB)

        @block.gpsimd
        def _(pool):
            pool.memset(ident[:, :], 0.0).then_inc(ident_step, 1)
            pool.memset(half_neg[:, :], 0.0).then_inc(ident_step, 1)
            pool.wait_ge(ident_step, 2)
            pool.affine_select(out=ident[:, :], in_=ident[:, :], compare_op=ALU.not_equal, fill=1.0,
                               base=0, pattern=[[-1, P]], channel_multiplier=1).then_inc(const_ready, 1)
            pool.affine_select(out=half_neg[:, :], in_=half_neg[:, :], compare_op=ALU.not_equal, fill=-0.5,
                               base=0, pattern=[[-1, P]], channel_multiplier=1).then_inc(const_ready, 1)

            def ada_pair(pair, i=0):
                for half in range(2):
                    if pair:
                        pool.wait_ge(ada_step, PAIR_STEPS * pair - PAIR_STEPS // 2 * (1 - half) + GU_PAIRS * PAIR_STEPS * i)
                    k0 = KC // 2 * half
                    col = (PRO_CHUNKS + 2 * pair) * P + 2 * GU_PAIRS * P * i
                    pool.dma_start(ada_ring[:, k0:k0 + KC // 2, :],
                                   ada_w.rearrange("(k p) c -> p k c", p=P)[:, k0:k0 + KC // 2, bass.ds(col, 2 * P)])\
                        .then_inc(ada_landed[half], 16)

            pool.wait_ge(pro_landed[KC - 1], 16)
            ada_pair(0)
            with pool.Fori(0, GU_IT) as i:
                for q in range(GU_PAIRS):
                    ada_pair(q + 1, i)
            for pair in range(GU_IT * GU_PAIRS + 1, N_PAIRS):
                ada_pair(pair)

            pool.wait_ge(slot_used, N_FFN)
            pool.iota(i_rel[:, :], pattern=[[-1, 2 * P]], base=P, channel_multiplier=1).then_inc(mask_step, 1)
            pool.memset(m_band[:, :], 0.0).then_inc(mask_step, 1)
            pool.memset(m_causal[:, :], 0.0).then_inc(mask_step, 1)
            pool.memset(nsel[:, :, :], 0.0).then_inc(mask_step, 1)
            for w in (wf_hi, wf_lo):
                pool.memset(w[:, KC * FH:].bitcast(F32), 0.0).then_inc(wf_zero, 1)
            pool.wait_ge(mask_step, 4)
            pool.affine_select(out=m_band[:, :], in_=m_band[:, :], compare_op=ALU.is_ge, fill=NEG, base=P,
                               pattern=[[-1, 2 * P]], channel_multiplier=1).then_inc(mask_step, 1)
            pool.wait_ge(mask_step, 5)
            pool.affine_select(out=m_band[:, :], in_=m_band[:, :], compare_op=ALU.is_ge, fill=NEG, base=0,
                               pattern=[[1, 2 * P]], channel_multiplier=-1).then_inc(mask_ready, 1)
            pool.affine_select(out=m_causal[:, :], in_=m_causal[:, :], compare_op=ALU.is_ge, fill=NEG, base=0,
                               pattern=[[-1, P]], channel_multiplier=1).then_inc(mask_ready, 1)
            pool.affine_select(out=nsel[:, :, :], in_=nsel[:, :, :], compare_op=ALU.not_equal, fill=-1.0, base=0,
                               pattern=[[-1, FH], [0, P]], channel_multiplier=1).then_inc(mask_ready, 1)

            pool.wait_ge(comb, 1)
            pool.dma_start(lse_dram.rearrange("(t p) h -> p t h", p=P),
                           lse[:, 0, :].rearrange("p (t h) -> p t h", t=TB)).then_inc(lse_out, 16)
            pool.wait_ge(lse_out, 16)
            pool.dma_start(lse[:, 0, :], lse_dram.rearrange("(i r) h -> i (r h)", r=TB)).then_inc(lse_in, 16)
            pool.wait_ge(comb, 8)
            pool.dma_start(gw_dram.rearrange("(i r) h -> i (r h)", r=TB), gw[:, 0, :]).then_inc(gw_out, 16)
            pool.wait_ge(gw_out, 16)
            pool.dma_start(gw0[:, :].rearrange("p (t h) -> p t h", t=TB),
                           gw_dram.rearrange("(t p) h -> p t h", p=P)).then_inc(gw_in, 16)

        @block.scalar
        def _(act):
            def hi(n, loop=0, loop_landed=0):
                landed(act, n, loop_landed)
                if n >= 2:
                    act.wait_ge(slot_used, n - 1 + loop)
                m = slot_size(n)
                act.activation(w_hi[n % 2][:, 0:m], raw[n % 2][:, 0:m], ACT.Copy).then_inc(split_hi, 1)

            def norm_std(q):
                act.wait_ge(var_ready, q + 1)
                act.activation(std[:, :], var[:, :], ACT.Sqrt).then_inc(std_ready, 1)

            def norm_hi(q, shift_col):
                for k in range(KC):
                    act.wait_ge(t_ready, KC * q + k + 1)
                    act.activation(h_hi[:, k, :], norm_t(k), ACT.Identity,
                                   bias=mod[:, shift_col + k:shift_col + k + 1]).then_inc(h_hi_ready, 1)

            def ffn_gate_up(fi, i, hid):
                base, bank0, hid0 = FFN_SLOT[fi], BANKS[fi], 2 * GU_IT * fi
                for f in range(2):
                    act.wait_ge(slot_used, base + 1 + 2 * i)
                    act.wait_ge(bank23_free, bank0 - 1 + f + 2 * i)
                    act.activation(tmpA[:, f, :], banks[f][:, :], ACT.Silu).then_inc(bank01_free, 1)
                hi(base + 2, loop=2 * i, loop_landed=16 * i)
                for f in range(2):
                    act.wait_ge(bank23_free, bank0 + 1 + f + 2 * i)
                    act.activation(hid[0][:, 2 * i + f, :], tmpB[:, f, :], ACT.Copy).then_inc(hid_hi_ready, 1)
                hi(base + 3, loop=2 * i, loop_landed=16 * i)

            def ffn_down(fi, j):
                base = FFN_SLOT[fi] + 2 * GU_IT + 6 * j
                for s in range(6):
                    if s % 3 == 2:
                        squares(2 * KC * fi + 4 * j + 2 * (s // 3))
                    if j == 1 and s == 5:
                        norm_std(2 * fi + 1)
                    if base + s + 2 < N_SLOTS:
                        hi(base + s + 2)

            def squares(x0):
                for dd in range(2):
                    act.wait_ge(x_updated, x0 + dd + 1)
                    act.activation(tmpA[:, dd, :], xT[:, (x0 + dd) % KC, :], ACT.Square).then_inc(sq_ready, 1)

            def merge_hi_part(d):
                act.wait_ge(msum_ready, d + 1)
                act.activation(h_hi[:, d, :], tmpB[:, d % 2, :], ACT.Copy).then_inc(merge_hi, 1)

            act.dma_start(rows[0:72, :], ada_b.rearrange("(r p) -> r p", p=P)).then_inc(rows_landed, 16)
            for n, g in enumerate((norm_ffn1, norm_mix, norm_ffn2, norm_final)):
                act.dma_start(rows[GAIN + KC * n:GAIN + KC * (n + 1), :], g.rearrange("(r p) -> r p", p=P))\
                   .then_inc(rows_landed, 16)
            act.dma_start(fbias[:, :], forget_bias.rearrange("(h a) -> h a", a=1)).then_inc(fb_landed, 16)
            act.wait_ge(c_turned, 1)
            act.activation(c_act[:, :], banks[7][:, 0:KC], ACT.Silu).then_inc(cact_ready, 1)
            for t in range(TB):
                act.wait_ge(x_landed[t], 16)
                act.activation(tmpA[:, :, :].rearrange("p a t -> p (a t)"), x_nat[:, t, :], ACT.Square,
                               accum_out=ss[:, t:t + 1]).then_inc(ss_ready, 1)
                act.wait_ge(ss_ready, t + 1)
            norm_std(0)
            hi(0)
            norm_hi(0, 0)
            hi(1)
            with act.Fori(0, GU_IT) as i:
                ffn_gate_up(0, i, hid1)
            for j in range(2):
                ffn_down(0, j)
            norm_hi(1, 3 * KC)

            act.wait_ge(wf_landed, 16)
            act.activation(wf_hi[:, 0:KC * FH], wf[:, :, :].rearrange("p k h -> p (k h)"), ACT.Copy)\
               .then_inc(wf_hi_ready, 1)
            for m in range(N_QKV):
                if m == 2:
                    act.wait_ge(f_step, 3)
                    act.activation(f_abs, f_abs, ACT.Exp).then_inc(f_act, 1)
                    act.wait_ge(f_act, 1)
                    act.activation(f_abs, f_abs, ACT.Ln, bias=1.0).then_inc(f_act, 1)
                hi(S_MIX + 2 + m)

            def exp_tile(u):
                job, g, h, subs = TILES[u]
                act.wait_ge(max_ready, u + 1)
                if u >= 2:
                    act.wait_ge(turned, u - 1)
                for n, (t, c0, w) in enumerate(subs):
                    last = act.activation(tmpB[:, u % 2, c0:c0 + w], tmpA[:, u % 2, c0:c0 + w], ACT.Exp,
                                          bias=nmx[:, u % 2, n:n + 1], accum_out=zs[:, g, t, h:h + 1])
                last.then_inc(probs_ready, 1)

            def evac_pT(u):
                _, _, _, subs = TILES[u]
                w = subs[-1][1] + subs[-1][2]
                act.wait_ge(turned, u + 1)
                if u >= 2:
                    act.wait_ge(pv_ready, u - 1)
                act.activation(pT[:, u % 2, 0:w], banks[4 + u % 2][:, 0:w], ACT.Copy).then_inc(pT_ready, 1)

            for m in range(N_OVER):
                for j in range(3):
                    s = 3 * m + j
                    if j == 0 and 4 <= m - 1 < 4 + FH:
                        h = m - 1 - 4
                        act.wait_ge(ck_ready, h + 1)
                        if h >= 2:
                            act.wait_ge(scores_read, FIRST_FOX + 3 * (h - 1))
                        act.activation(ckb[h % 2], banks[0][:, :], ACT.Copy).then_inc(ck_free, 1)
                    if 0 <= s - 2 < N_TILES:
                        evac_pT(s - 2)
                    if 0 <= s - 1 < N_TILES:
                        exp_tile(s - 1)
                    if j == 0 and m >= 1:
                        hi(S_OVER + m + 1)
                    if s == COMB_LN:
                        act.wait_ge(o_free, len(JOBS) - FH)
                        act.activation(gw[:, :, :].rearrange("p g (t h) -> p g t h", t=TB), zs[:, 0:NG, :, 0:GH],
                                       ACT.Ln).then_inc(comb_act, 1)
                    if s == COMB_EXP:
                        act.wait_ge(comb, 4)
                        act.activation(gw[:, :, :], gw[:, :, :], ACT.Exp).then_inc(comb_act, 1)
            hi(S_OVER + N_OVER + 1)

            for fb in range(2):
                act.wait_ge(y_turned, 2 * fb + 1)
                act.activation(tmpA[:, fb, :], banks[2 + 2 * fb][:, :], ACT.Copy).then_inc(y0_ready, 1)
            for fc in range(4):
                act.wait_ge(y_turned, 4 + fc + 1)
                act.activation(y_hi[:, 2 + fc, :], banks[(6 + fc) % 8][:, :], ACT.Copy).then_inc(y_hi_ready, 1)
            for fb in range(2):
                act.wait_ge(ysum_ready, fb + 1)
                act.activation(y_hi[:, fb, :], tmpB[:, fb, :], ACT.Copy).then_inc(y_hi_ready, 1)
            act.wait_ge(p1_free, N_OVER)
            for d in range(KC):
                act.activation(gates[:, d::KC, :], gates[:, d::KC, :], ACT.Sigmoid).then_inc(sig_ready, 1)
                if d >= 1:
                    merge_hi_part(d - 1)
                if d % 2 == 1:
                    hi(S_BR + d // 2 + 2)
            merge_hi_part(KC - 1)
            for d2 in range(N_OUT):
                squares(KC + 2 * d2)
                if d2 == N_OUT - 1:
                    norm_std(2)
                hi(S_OUT + d2 + 2)
            norm_hi(2, 6 * KC)
            with act.Fori(0, GU_IT) as i:
                ffn_gate_up(1, i, hid2)
            for j in range(2):
                ffn_down(1, j)
            for k in range(KC):
                act.activation(xT[:, k, :], xT[:, k, :], ACT.Copy, scale=cols[:, GAIN + 3 * KC + k:GAIN + 3 * KC + k + 1])\
                   .then_inc(xg_ready, 1)
            for t in range(TB):
                act.wait_ge(fin_turned, 2 * t + 1)
                act.wait_ge(rstd_ready, 1)
                act.activation(y_sb[:, t, 0:T], banks[FIN_BANK[t]][:, :], ACT.Copy, scale=rstd[:, t:t + 1]).then_inc(y_act, 1)

        @block.vector
        def _(dve):
            def lo(n, loop=0):
                dve.wait_ge(split_hi, n + 1 + loop)
                m = slot_size(n)
                dve.tensor_tensor(w_lo[n % 2][:, 0:m], raw[n % 2][:, 0:m], w_hi[n % 2][:, 0:m].bitcast(F32),
                                  ALU.subtract).then_inc(split_done, 1)

            def norm_stats(q):
                if q == 0:
                    dve.wait_ge(ss_ready, TB)
                else:
                    dve.wait_ge(ss_step, (KC + 1) * q - 1)
                    dve.tensor_reduce(ss[:, :], ss_part[:, :, :], AX.X, ALU.add).then_inc(ss_step, 1)
                    dve.wait_ge(ss_step, (KC + 1) * q)
                dve.tensor_scalar(var[:, :], ss[:, :], 1.0 / D, EPS, ALU.mult, ALU.add).then_inc(var_ready, 1)
                dve.wait_ge(std_ready, q + 1)
                dve.reciprocal(r0[:, :], std[:, :]).then_inc(rstd_step, 1)
                dve.wait_ge(rstd_step, 3 * q + 1)
                dve.tensor_tensor(nw[:, :], r0[:, :], r0[:, :], ALU.mult).then_inc(rstd_step, 1)
                dve.wait_ge(rstd_step, 3 * q + 2)
                dve.tensor_tensor(nw[:, :], nw[:, :], var[:, :], ALU.mult).then_inc(rstd_step, 1)
                dve.wait_ge(rstd_step, 3 * q + 3)
                dve.scalar_tensor_tensor(out=rstd_m2[:, :], in0=nw[:, :], scalar=-3.0, in1=r0[:, :], op0=ALU.add,
                                         op1=ALU.mult).then_inc(neg_step, 1)

            def block_stats(x0):
                for dd in range(2):
                    dve.wait_ge(stat_done, x0 + dd + 1)
                    dve.tensor_reduce(ss_part[:, :, (x0 + dd) % KC], banks[(5, 7)[dd]][:, :].rearrange("p (t f) -> p t f", t=TB),
                                      AX.X, ALU.add).then_inc(ss_step, 1)

            def norm_apply(q):
                dve.wait_ge(rstd_bc, q + 1)
                for k in range(KC + 1):
                    if k < KC:
                        if k >= 4:
                            dve.wait_ge(h_ready, KC * q + k - 3)
                        dve.scalar_tensor_tensor(out=norm_t(k), in0=banks[6][:, :], scalar=scale_a[:, q, k:k + 1],
                                                 in1=xT[:, k, :], op0=ALU.mult, op1=ALU.mult).then_inc(t_ready, 1)
                    if k >= 1:
                        c0 = 3 * KC * q + k - 1
                        dve.wait_ge(h_hi_ready, KC * q + k)
                        dve.scalar_tensor_tensor(out=h_lo[:, k - 1, :], in0=norm_t(k - 1), scalar=mod[:, c0:c0 + 1],
                                                 in1=h_hi[:, k - 1, :].bitcast(F32), op0=ALU.add,
                                                 op1=ALU.subtract).then_inc(h_ready, 1)

            def ada_pair(q, batch, step, landed_):
                for k in range(KC):
                    for s in range(2):
                        acc, w, ck = ada_acc[2 * q + s], ada_ring[:, k, s * P:(s + 1) * P], c_act[:, k:k + 1]
                        if s == 0 and k % (KC // 2) == 0:
                            dve.wait_ge(ada_landed[k // (KC // 2)], landed_)
                        if k == 0:
                            if not isinstance(batch, int) or batch:
                                dve.wait_ge(mod_ready, batch + 1)
                            dve.tensor_scalar(acc[:, :], w, ck, None, ALU.mult).then_inc(ada_step, 1)
                        else:
                            dve.wait_ge(ada_step, step + 2 * (k - 1) + s + 1)
                            dve.scalar_tensor_tensor(out=acc[:, :], in0=w, scalar=ck, in1=acc[:, :], op0=ALU.mult,
                                                     op1=ALU.add).then_inc(ada_step, 1)

            def ada_add(batch, col, n):
                dve.wait_ge(ada_mm, batch + 1)
                for s0 in range(0, n, TB):
                    m = min(n - s0, TB)
                    ins = dve.tensor_reduce(ada_col[:, s0:s0 + m],
                                            banks[4 if s0 == 0 else 6][:, 0:m * P].rearrange("p (s k) -> p s k", s=m),
                                            AX.X, ALU.add)
                ins.then_inc(ada_red, 1)
                dve.wait_ge(ada_red, batch + 1)
                dve.tensor_tensor(mod[:, bass.ds(col, n)], ada_col[:, 0:n], cols[:, bass.ds(col, n)], ALU.add)\
                   .then_inc(mod_ready, 1)

            def gu(fi, i, hid, prev=None):
                base, bank0, hid0 = FFN_SLOT[fi], BANKS[fi], 2 * GU_IT * fi
                lo(base + 2, 2 * i)
                if fi == 0:
                    if prev is not None:
                        ada_add(prev, PRO_CHUNKS + 2 * GU_PAIRS * prev, 2 * GU_PAIRS)
                    ada_pair(0, i, GU_PAIRS * PAIR_STEPS * i, 16 + 32 * i)
                for f in range(2):
                    dve.wait_ge(slot_used, base + 2 + 2 * i)
                    dve.wait_ge(bank01_free, bank0 + 1 + f + 2 * i)
                    dve.tensor_tensor(tmpB[:, f, :], banks[2 + f][:, :], tmpA[:, f, :], ALU.mult)\
                       .then_inc(bank23_free, 1)
                for f in range(2):
                    dve.wait_ge(hid_hi_ready, hid0 + 1 + f + 2 * i)
                    dve.tensor_tensor(hid[1][:, 2 * i + f, :], tmpB[:, f, :],
                                      hid[0][:, 2 * i + f, :].bitcast(F32), ALU.subtract).then_inc(hid_ready, 1)
                lo(base + 3, 2 * i)
                if fi == 0:
                    ada_pair(1, i, PAIR_STEPS + GU_PAIRS * PAIR_STEPS * i, 32 + 32 * i)

            def add_to_x(g, n, x0, bank):
                for dd in range(2):
                    if dd:
                        dve.wait_ge(slot_used, n + 1)
                    else:
                        dve.wait_ge(half_done, x0 // 2 + 1)
                    b = (x0 + dd) % KC
                    dve.scalar_tensor_tensor(out=xT[:, b, :], in0=banks[bank + dd][:, :], scalar=gate_c[:, g, b:b + 1],
                                             in1=xT[:, b, :], op0=ALU.mult, op1=ALU.add).then_inc(x_updated, 1)

            def down(fi, j):
                base, x0 = FFN_SLOT[fi] + 2 * GU_IT + 6 * j, 2 * KC * fi + 4 * j
                for s in range(6):
                    if s % 3 == 2:
                        add_to_x(2 * fi, base + s, x0 + 2 * (s // 3), 2 * (s // 3))
                    if s == 5 and j == 1:
                        block_stats(x0 + 2)
                        return
                    if fi == 0:
                        ada_rest(6 * j + s)
                    if base + s + 2 < N_SLOTS:
                        lo(base + s + 2)
                    if s == 0 and j == 1:
                        block_stats(x0 - 2)
                    if s == 3:
                        block_stats(x0)

            def ada_rest(s):
                for batch, n, slots, add_at in ADA_REST:
                    first = GU_PAIRS * GU_IT + DOWN_PAIRS * (batch - GU_IT) if batch >= GU_IT else GU_PAIRS * batch
                    if s == add_at:
                        ada_add(batch, PRO_CHUNKS + 2 * first, 2 * n)
                        if batch == GU_IT + 1:
                            dve.wait_ge(mod_ready, GU_IT + 3)
                            gate(1)
                            gate(2)
                            coef(1)
                            coef(2).then_inc(coef_ready, 1)
                    if s in slots:
                        pair = first + slots.index(s)
                        ada_pair(slots.index(s), batch, PAIR_STEPS * pair, 16 * (pair + 1))

            def coef(q):
                return dve.scalar_tensor_tensor(out=scale_a[:, q, :], in0=mod[:, (3 * q + 1) * KC:(3 * q + 2) * KC],
                                                scalar=1.0, in1=cols[:, GAIN + KC * q:GAIN + KC * (q + 1)],
                                                op0=ALU.add, op1=ALU.mult)

            def gate(q):
                return dve.tensor_scalar(gate_c[:, q, :], mod[:, (3 * q + 2) * KC:(3 * q + 3) * KC],
                                         1.0 if q == 1 else 0.5, None, ALU.mult)

            for k in range(KC):
                dve.wait_ge(x_turned, k + 1)
                dve.tensor_copy(xT[:, k, :], banks[k % 4][:, :]).then_inc(bank01_free if k % 4 < 2 else bank23_free, 1)
            norm_stats(0)
            dve.wait_ge(cact_ready, 1)
            for j in (1, 0):
                for i_, k in enumerate(PRO_DVE):
                    w, ck, step = ada_pro[j][:, k, :], c_act[:, k:k + 1], len(PRO_DVE) * (1 - j) + i_
                    dve.wait_ge(pro_landed[j * KC + k], 16)
                    if i_ == 0:
                        dve.tensor_scalar(acc_pro[j][:, :], w, ck, None, ALU.mult).then_inc(pro_step, 1)
                    else:
                        dve.wait_ge(pro_step, step)
                        dve.scalar_tensor_tensor(out=acc_pro[j][:, :], in0=w, scalar=ck, in1=acc_pro[j][:, :],
                                                 op0=ALU.mult, op1=ALU.add).then_inc(pro_step, 1)
                    if j == 1 and i_ == 0:
                        dve.wait_ge(rows_turned, 1)
                        dve.tensor_copy(cols[:, :], banks[5][:, 0:GAIN + 4 * KC]).then_inc(cols_ready, 1)
                c_, red = slice(j * KC, (j + 1) * KC), 3 * (1 - j)
                dve.wait_ge(pro_mm, 2 - j)
                dve.tensor_reduce(mod_part[:, c_], banks[4 if j else 7][:, 0:KC * len(PRO_PE)]
                                  .rearrange("p (k c) -> p c k", k=len(PRO_PE)), AX.X, ALU.add)\
                   .then_inc(pro_red, 1)
                dve.wait_ge(cols_ready, 1)
                dve.wait_ge(pro_red, red + 1)
                dve.tensor_tensor(mod_part[:, c_], mod_part[:, c_], cols[:, c_], ALU.add).then_inc(pro_red, 1)
                for n in range(2):
                    dve.wait_ge(pro_turned, 2 * (1 - j) + n + 1)
                    ins = dve.tensor_reduce(ada_col[:, j * KC + TB * n:j * KC + TB * (n + 1)],
                                            banks[2 * (1 - j) + n][:, :].rearrange("p (s k) -> p s k", s=TB), AX.X, ALU.add)
                ins.then_inc(pro_red, 1)
                dve.wait_ge(pro_red, red + 3)
                dve.tensor_tensor(mod[:, c_], ada_col[:, c_], mod_part[:, c_], ALU.add)\
                   .then_inc(scale1_ready if j else mod_ready, 1)
                if j:
                    dve.wait_ge(scale1_ready, 1)
                    coef(0).then_inc(coef_ready, 1)
                    lo(0)
            dve.wait_ge(mod_ready, 1)
            dve.wait_ge(coef_ready, 1)
            norm_apply(0)
            lo(1)
            gu(0, 0, hid1)
            with dve.Fori(0, GU_IT - 1) as i:
                gu(0, i + 1, hid1, prev=i)
            dve.wait_ge(mod_ready, GU_IT)
            gate(0).then_inc(coef_ready, 1)
            dve.wait_ge(coef_ready, 2)
            for j in range(2):
                down(0, j)
            norm_stats(1)
            dve.wait_ge(coef_ready, 3)
            norm_apply(1)
            lo(S_MIX + 1)

            dve.wait_ge(wf_hi_ready, 1)
            dve.tensor_tensor(wf_lo[:, 0:KC * FH], wf[:, :, :].rearrange("p k h -> p (k h)"),
                              wf_hi[:, 0:KC * FH].bitcast(F32), ALU.subtract).then_inc(wf_ready, 1)
            dve.wait_ge(mask_ready, 3)
            dve.tensor_copy(rel[:, :], i_rel[:, :])
            dve.tensor_scalar(i_and[:, :], i_rel[:, P:2 * P], DILATION[2] // DILATION[1] - 1, None, ALU.bitwise_and)\
               .then_inc(res_ready, 1)
            dve.wait_ge(res_ready, 1)
            dve.scalar_tensor_tensor(out=m_res[:, :], in0=i_and[:, :], scalar=NEG, in1=m_causal[:, :],
                                     op0=ALU.mult, op1=ALU.add).then_inc(res_ready, 1)

            def evac_qkv(m):
                for b in range(2):
                    dve.wait_ge(slot_used, S_MIX + m + 1)
                    src = banks[2 * (m % 2) + b]
                    what, g = QKV[m]
                    if what == "v":
                        dve.tensor_copy(dv[g][:, 2 * b:2 * b + 2, :], src[:, :].rearrange("p (t e) -> p t e", t=2))\
                           .then_inc(qkv_evac, 1)
                        continue
                    is_k = what == "k"
                    dst = (dk if is_k else dq)[g][:, b, :]
                    view = src[:, :]
                    if g:
                        view = view.rearrange("p (i r) -> p r i", r=TB)
                        dst = dst.rearrange("p (r i) -> p r i", r=TB)
                    dve.tensor_scalar(dst, view, 1.0 if is_k else 0.125, None, ALU.mult).then_inc(qkv_evac, 1)

            for m in range(N_QKV):
                evac_qkv(m)
                lo(S_MIX + 2 + m)
                if m == 1:
                    dve.wait_ge(f_ready, 1)
                    dve.wait_ge(fb_landed, 16)
                    dve.tensor_scalar(f_x, banks[7][0:FH, :], fbias[:, 0:1], None, ALU.add).then_inc(f_step, 1)
                    dve.wait_ge(f_step, 1)
                    dve.tensor_scalar(ls_row, f_x, -1.0, None, ALU.mult).then_inc(f_step, 1)
                    dve.wait_ge(f_step, 2)
                    dve.tensor_tensor(f_abs, f_x, ls_row, ALU.min).then_inc(f_step, 1)
                if m == 3:
                    dve.memset(zeros_row, 0.0)
                    dve.wait_ge(f_act, 2)
                    dve.scalar_tensor_tensor(out=ls_row, in0=f_x, scalar=0.0, in1=f_abs, op0=ALU.min,
                                             op1=ALU.subtract).then_inc(f_step, 1)
                    dve.wait_ge(f_step, 4)
                    dve.tensor_tensor_scan(cum_row[:, :], zeros_row, ls_row, 0.0, ALU.add, ALU.add)\
                       .then_inc(cum_ready, 1)
                if m == 6:
                    dve.wait_ge(cum_turned, 1)
                    dve.tensor_copy(cum_col[:, :, :], banks[7][:, 0:TB * FH].rearrange("p (t h) -> p t h", t=TB))\
                       .then_inc(cumcol_ready, 1)

            n_bias, n_max = [0], [0]

            def alibi_tile(job, g, h):
                slope = -SLOPE[g * GH + h] * (DILATION[1] if g else 1)
                w, mask = (2 * P, m_band[:, :]) if g == 0 else (P, m_causal[:, :] if g == 1 else m_res[:, :])
                r = rel[:, :] if g == 0 else rel[:, P:2 * P]
                dve.scalar_tensor_tensor(out=alibi[:, job % 2, 0:w], in0=r, scalar=slope, in1=mask,
                                         op0=ALU.mult, op1=ALU.add).then_inc(alibi_ready, 1)
                dve.wait_ge(alibi_ready, job + 1)

            def bias_tile(u):
                job, g, h, subs = TILES[u]
                w = subs[-1][1] + subs[-1][2]
                S, B = banks[2 + u % 2], tmpA[:, u % 2, :]
                if g < 3 and (u == 0 or TILES[u - 1][0] != job):
                    alibi_tile(job, g, h)
                dve.wait_ge(scores_ready, u + 1)
                if u >= 2:
                    dve.wait_ge(probs_ready, u - 1)
                if g == 0 and subs[0][0] == 0:
                    dve.tensor_tensor(B[:, 0:P], S[:, 0:P], alibi[:, job % 2, P:2 * P], ALU.add)
                    dve.tensor_tensor(B[:, P:w], S[:, P:w], alibi[:, job % 2, :], ALU.add).then_inc(scores_read, 1)
                elif g < 3:
                    n = 2 if g == 0 else TB
                    dve.tensor_tensor(B[:, 0:w].rearrange("p (n c) -> p n c", n=n),
                                      S[:, 0:w].rearrange("p (n c) -> p n c", n=n),
                                      alibi[:, job % 2, 0:w // n].unsqueeze(1).broadcast_to([P, n, w // n]),
                                      ALU.add).then_inc(scores_read, 1)
                else:
                    dve.wait_ge(ck_free, h + 1)
                    for i_, (t, c0, ws) in enumerate(subs):
                        ins = dve.scalar_tensor_tensor(out=B[:, c0:c0 + ws], in0=S[:, c0:c0 + ws],
                                                       scalar=cum_col[:, t, h:h + 1], in1=ckb[h % 2][:, 0:ws],
                                                       op0=ALU.add, op1=ALU.add)
                    ins.then_inc(scores_read, 1)
                    dve.wait_ge(scores_read, u + 1)
                    for t, c0, ws in subs:
                        ins = dve.tensor_tensor(B[:, c0 + ws - P:c0 + ws], B[:, c0 + ws - P:c0 + ws], m_causal[:, :],
                                                ALU.add)
                    n_bias[0] += 1
                    ins.then_inc(bias_step, 1)
                    dve.wait_ge(bias_step, n_bias[0])
                dve.wait_ge(scores_read, u + 1)
                if g in (1, 2):
                    ins = dve.tensor_reduce(mx[:, g, :, h], B.rearrange("p (n c) -> p n c", n=TB), AX.X, ALU.max)
                else:
                    for t, c0, ws in subs:
                        ins = dve.tensor_reduce(mx[:, g, t, h:h + 1], B[:, c0:c0 + ws], AX.X, ALU.max)
                ins.then_inc(max_step, 1)
                dve.wait_ge(max_step, u + 1)
                t0, n = subs[0][0], len(subs)
                dve.tensor_scalar(nmx[:, u % 2, 0:n], mx[:, g, t0:t0 + n, h], -1.0, None, ALU.mult).then_inc(max_ready, 1)

            def finish_job(job):
                g, h = JOBS[job]
                dve.wait_ge(pv_ready, LAST_TILE[job] + 1)
                dve.reciprocal(rz[:, job % 2, :], zs[:, g, :, h]).then_inc(rz_ready, 1)
                dve.wait_ge(rz_ready, job + 1)
                dst = o_dil[:, g, :, h * E_:(h + 1) * E_] if g < 3 else o_fox[:, :, h * E_:(h + 1) * E_]
                dve.tensor_tensor(dst, banks[6 + job % 2][:, 0:TB * E_].rearrange("p (t e) -> p t e", t=TB),
                                  rz[:, job % 2, :].unsqueeze(2).broadcast_to([P, TB, E_]), ALU.mult).then_inc(o_free, 1)

            def evac_over(m, f):
                if f == 0:
                    dve.wait_ge(proj_ready, m + 1)
                else:
                    dve.wait_ge(slot_used, S_OVER + m + 1)
                free = p1_free if f else p0_free
                if m < 2:
                    dve.tensor_scalar(fq[:, 2 * m + f, :], banks[f][:, :], 0.125, None, ALU.mult).then_inc(free, 1)
                elif m < 4:
                    dve.tensor_copy(fk[:, 2 * (m - 2) + f, :], banks[f][:, :]).then_inc(free, 1)
                elif m < 6:
                    dve.tensor_copy(fv[:, 2 * f:2 * f + 2, (m - 4) * SC:(m - 3) * SC],
                                    banks[f][:, :].rearrange("p (t e) -> p t e", t=2)).then_inc(free, 1)
                else:
                    dve.tensor_copy(gates[:, 2 * (m - 6) + f, :], banks[f][:, :]).then_inc(free, 1)

            def per_head(ap):
                return ap.unsqueeze(2).broadcast_to([P, TB * GH, E_])

            def combine(s):
                def tt(out_, a, b, op):
                    dve.tensor_tensor(out_, a, b, op).then_inc(comb, 1)
                    n_comb[0] += 1
                    dve.wait_ge(comb, n_comb[0])

                od = [o_dil[:, g, :, :].rearrange("p t (h e) -> p (t h) e", h=GH) for g in range(NG)]
                if s == COMB_LN + 1:
                    dve.wait_ge(comb_act, 1)
                    tt(lse[:, :, :].rearrange("p g (t h) -> p g t h", t=TB), mx[:, 0:NG, :, 0:GH],
                       gw[:, :, :].rearrange("p g (t h) -> p g t h", t=TB), ALU.add)
                if s == COMB_EXP - 1:
                    dve.wait_ge(lse_in, 16)
                    tt(gmax[:, :], lse[:, 0, :], lse[:, 1, :], ALU.max)
                    tt(gmax[:, :], gmax[:, :], lse[:, 2, :], ALU.max)
                    tt(gw[:, :, :], lse[:, :, :], gmax[:, :].unsqueeze(1).broadcast_to([P, NG, TB * GH]), ALU.subtract)
                if s == COMB_EXP + 1:
                    dve.wait_ge(comb_act, 2)
                    tt(gsum[:, :], gw[:, 0, :], gw[:, 1, :], ALU.add)
                    tt(gsum[:, :], gsum[:, :], gw[:, 2, :], ALU.add)
                    dve.reciprocal(gmax[:, :], gsum[:, :]).then_inc(comb, 1)
                    n_comb[0] += 1
                    dve.wait_ge(comb, n_comb[0])
                    tt(gw[:, :, :], gw[:, :, :], gmax[:, :].unsqueeze(1).broadcast_to([P, NG, TB * GH]), ALU.mult)
                if s == COMB_EXP + 2:
                    tt(od[1], od[1], per_head(gw[:, 1, :]), ALU.mult)
                if s == COMB_EXP + 3:
                    tt(od[2], od[2], per_head(gw[:, 2, :]), ALU.mult)
                if s == COMB_EXP + 4:
                    tt(od[1], od[1], od[2], ALU.add)
                if s == COMB_EXP + 8:
                    dve.wait_ge(gw_in, 16)
                    tt(od[0], od[0], per_head(gw0[:, :]), ALU.mult)

            n_comb = [0]
            dve.wait_ge(res_ready, 2)
            dve.wait_ge(cumcol_ready, 1)
            for m in range(N_OVER):
                for j in range(3):
                    s = 3 * m + j
                    if j == 0 and m >= 1:
                        evac_over(m - 1, 1)
                    if 0 <= s - 1 < N_TILES:
                        bias_tile(s - 1)
                    if j == 0 and m >= 1:
                        lo(S_OVER + m + 1)
                    if j == 1:
                        evac_over(m, 0)
                    if s - 3 >= 0 and LAST_TILE[TILES[s - 3][0]] == s - 3:
                        finish_job(TILES[s - 3][0])
                    combine(s)
            evac_over(N_OVER - 1, 1)
            finish_job(TILES[N_TILES - 1][0])
            lo(S_OVER + N_OVER + 1)

            for fb in range(2):
                dve.wait_ge(y_turned, 2 * fb + 2)
                dve.wait_ge(y0_ready, fb + 1)
                dve.tensor_tensor(tmpB[:, fb, :].rearrange("p (i r) -> p r i", r=TB),
                                  banks[3 + 2 * fb][:, :].rearrange("p (r i) -> p r i", r=TB),
                                  tmpA[:, fb, :].rearrange("p (i r) -> p r i", r=TB), ALU.add).then_inc(ysum_ready, 1)
            for fc in range(4):
                dve.wait_ge(y_hi_ready, fc + 1)
                dve.tensor_tensor(y_lo[:, 2 + fc, :], banks[(6 + fc) % 8][:, :], y_hi[:, 2 + fc, :].bitcast(F32),
                                  ALU.subtract).then_inc(y_ready, 1)
            for fb in range(2):
                dve.wait_ge(y_hi_ready, 4 + fb + 1)
                dve.tensor_tensor(y_lo[:, fb, :], tmpB[:, fb, :], y_hi[:, fb, :].bitcast(F32), ALU.subtract)\
                   .then_inc(y_ready, 1)

            def merge_lo(d):
                dve.wait_ge(merge_hi, d + 1)
                dve.tensor_tensor(h_lo[:, d, :], tmpB[:, d % 2, :], h_hi[:, d, :].bitcast(F32), ALU.subtract)\
                   .then_inc(merged, 1)

            for d in range(KC):
                b0 = 4 * (d // 2 % 2) + 2 * (d % 2)
                if d % 2 == 0:
                    dve.wait_ge(br_ready, d // 2 + 1)
                else:
                    dve.wait_ge(slot_used, S_BR + d // 2 + 1)
                dve.wait_ge(sig_ready, d + 1)
                if d >= 1:
                    dve.wait_ge(msum_ready, d)
                for x_ in range(2):
                    dve.tensor_tensor(tmpA[:, x_, :], banks[b0 + x_][:, :], gates[:, KC * x_ + d, :], ALU.mult)\
                       .then_inc(merge_step, 1)
                dve.wait_ge(merge_step, 2 * d + 2)
                dve.tensor_tensor(tmpB[:, d % 2, :], tmpA[:, 0, :], tmpA[:, 1, :], ALU.add).then_inc(msum_ready, 1)
                if d >= 1:
                    merge_lo(d - 1)
                if d % 2 == 1:
                    lo(S_BR + d // 2 + 2)
            merge_lo(KC - 1)
            for d2 in range(N_OUT):
                if d2 >= 1:
                    block_stats(KC + 2 * (d2 - 1))
                add_to_x(1, S_OUT + d2, KC + 2 * d2, 2 * (d2 % 2))
                if d2 == N_OUT - 1:
                    block_stats(KC + 2 * d2)
                else:
                    lo(S_OUT + d2 + 2)
            norm_stats(2)
            norm_apply(2)
            lo(S_FFN2 + 1)
            with dve.Fori(0, GU_IT) as i:
                gu(1, i, hid2)
            for j in range(2):
                down(1, j)
            norm_stats(3)
            dve.wait_ge(neg_step, 4)
            dve.tensor_scalar(rstd[:, :], rstd_m2[:, :], -0.5, None, ALU.mult).then_inc(rstd_ready, 1)
            dve.wait_ge(rstd_ready, 1)
            for t in range(TB):
                dve.wait_ge(fin_turned, 2 * t + 2)
                dve.tensor_scalar(y_sb[:, t, T:2 * T], banks[FIN_BANK[t] + 1][:, :], rstd[:, t:t + 1], None, ALU.mult)\
                   .then_inc(y_dve, 1)

        @block.tensor
        def _(pe):
            def mm3(out_, a, b, first, last):
                pe.matmul(out_, a[0], b[0], start=first, stop=False)
                pe.matmul(out_, a[0], b[1], start=False, stop=False)
                return pe.matmul(out_, a[1], b[0], start=False, stop=last)

            def w_blk(n, k, f, at=0):
                c0 = at + k * SC + f * P
                return w_hi[n % 2][:, c0:c0 + P], w_lo[n % 2][:, c0:c0 + P]

            def h_blk(k, sl=slice(0, T)):
                return h_hi[:, k, sl], h_lo[:, k, sl]

            def gate_up(fi, i, prev=None):
                base, bank0, q = FFN_SLOT[fi], BANKS[fi], 2 * fi
                for j in range(2):
                    n = base + j
                    pe.wait_ge(split_done, n + 1 + 2 * i)
                    pe.wait_ge(bank23_free if j else bank01_free, bank0 + 2 * i)
                    for k in range(KC):
                        if j == 0:
                            pe.wait_ge(h_ready, KC * q + k + 1)
                        for f in range(2):
                            last = mm3(banks[2 * j + f][:, :], w_blk(n, k, f), h_blk(k), k == 0, k == KC - 1)
                        if prev is not None and j == 1 and k == 3:
                            per = GU_PAIRS * PAIR_STEPS
                            ada_sum(prev, per * prev + per, 2 * GU_PAIRS)
                    last.then_inc(slot_used, 1)

            def ada_sum(batch, step, n):
                pe.wait_ge(ada_step, step)
                pe.wait_ge(mod_ready, batch + 1)
                for s in range(n):
                    last = pe.transpose(banks[4 if s < TB else 6][:, s % TB * P:(s % TB + 1) * P], ada_acc[s][:, :],
                                        ident[:, :])
                last.then_inc(ada_mm, 1)

            def stats(b):
                pe.wait_ge(sq_ready, b + 1)
                for t in range(TB):
                    last = pe.transpose(banks[(5, 7)[b % 2]][:, t * P:(t + 1) * P], tmpA[:, b % 2, t * P:(t + 1) * P],
                                        ident[:, :])
                last.then_inc(stat_done, 1)

            def last_slot(n, nk, bank, x0, act_blk, start, ends):
                for dd in range(2):
                    for k in range(nk):
                        if ends and dd == 1 and k == nk - 1:
                            stats(x0)
                        last = mm3(banks[bank + dd][:, :], w_blk(n, k, dd), act_blk(k), start and k == 0, k == nk - 1)
                    last.then_inc(slot_used if dd else half_done, 1)
                if ends:
                    stats(x0 + 1)

            def down(fi, j, hid):
                base, x0, hid0 = FFN_SLOT[fi] + 2 * GU_IT + 6 * j, 2 * KC * fi + 4 * j, 2 * GU_IT * fi
                if j == 0:
                    pe.wait_ge(bank01_free, BANKS[fi] + 2 * GU_IT)
                    pe.wait_ge(bank23_free, BANKS[fi] + 2 * GU_IT)
                for s in range(6):
                    n, (k0, nk) = base + s, DOWN_PARTS[s % 3]
                    pe.wait_ge(split_done, n + 1)
                    pe.wait_ge(hid_ready, hid0 + min(k0 + nk, FB))
                    if s % 3 == 2:
                        last_slot(n, nk, 2 * (s // 3), x0 + 2 * (s // 3),
                                  lambda k: (hid[0][:, k0 + k, :], hid[1][:, k0 + k, :]), False, j == 1 and s == 5)
                    else:
                        for k in range(nk):
                            for dd in range(2):
                                last = mm3(banks[2 * (s // 3) + dd][:, :], w_blk(n, k, dd),
                                           (hid[0][:, k0 + k, :], hid[1][:, k0 + k, :]), k0 + k == 0, False)
                        last.then_inc(slot_used, 1)
                    if s == 0 and j == 1:
                        stats(x0 - 2)
                        stats(x0 - 1)
                    if s == 3:
                        stats(x0)
                        stats(x0 + 1)
                    for batch, n, _, add_at in ADA_REST:
                        if fi == 0 and 6 * j + s == add_at - 1:
                            pairs = GU_PAIRS * GU_IT + DOWN_PAIRS * (batch - GU_IT + 1)
                            if batch < GU_IT:
                                pairs = GU_PAIRS * (batch + 1)
                            ada_sum(batch, PAIR_STEPS * pairs, 2 * n)

            def rstd_rows(q):
                pe.wait_ge(neg_step, q + 1)
                for t in range(TB):
                    last = pe.matmul(banks[6][:, t * P:(t + 1) * P], rstd_m2[:, t:t + 1].broadcast_to([P, P]),
                                     half_neg[:, :], start=True, stop=True)
                last.then_inc(rstd_bc, 1)

            pe.wait_ge(const_ready, 2)
            pe.wait_ge(c_landed, 16)
            pe.transpose(banks[7][:, 0:KC], c_rows[:, :], ident[0:KC, 0:KC]).then_inc(c_turned, 1)
            for k in range(KC):
                if k >= 4:
                    pe.wait_ge(bank01_free if k % 4 < 2 else bank23_free, k % 2 + 1)
                for t in range(TB):
                    if k == 0:
                        pe.wait_ge(x_landed[t], 16)
                    last = pe.transpose(banks[k % 4][:, t * P:(t + 1) * P], x_nat[:, t, k * P:(k + 1) * P], ident[:, :])
                last.then_inc(x_turned, 1)
            pe.wait_ge(rows_landed, 16 * 5)
            pe.transpose(banks[5][:, 0:GAIN + 4 * KC], rows[:, :], ident[0:GAIN + 4 * KC, 0:GAIN + 4 * KC])\
              .then_inc(rows_turned, 1)
            pe.wait_ge(cact_ready, 1)
            for j in (1, 0):
                for i_, k in enumerate(PRO_PE):
                    pe.wait_ge(pro_landed[j * KC + k], 16)
                    for c0 in range(KC):
                        col = KC * i_ + c0
                        last = pe.matmul(banks[4 if j else 7][:, col:col + 1], ada_pro[j][:, k, c0 * P:(c0 + 1) * P],
                                         c_act[:, k:k + 1], start=True, stop=True)
                last.then_inc(pro_mm, 1)
                if j:
                    rstd_rows(0)
                    pe.wait_ge(bank01_free, 4)
                    pe.wait_ge(bank23_free, 4)
                pe.wait_ge(pro_step, (2 - j) * len(PRO_DVE))
                for n in range(2):
                    for s in range(TB):
                        c0 = (n * TB + s) * P
                        last = pe.transpose(banks[2 * (1 - j) + n][:, s * P:(s + 1) * P], acc_pro[j][:, c0:c0 + P],
                                            ident[:, :])
                    last.then_inc(pro_turned, 1)
            gate_up(0, 0)
            with pe.Fori(0, GU_IT - 1) as i:
                gate_up(0, i + 1, prev=i)
            for j in range(2):
                down(0, j, hid1)
            rstd_rows(1)

            def tokens(g, t):
                return slice(t * P, (t + 1) * P) if g == 0 else slice(t, T, TB)

            for m in range(N_QKV):
                n = S_MIX + m
                pe.wait_ge(split_done, n + 1)
                if m >= 2:
                    pe.wait_ge(qkv_evac, 2 * (m - 1))
                b0 = 2 * (m % 2)
                what, g = QKV[m]
                if what == "v":
                    for t in range(TB):
                        for k in range(KC):
                            at = k * SC
                            last = mm3(banks[b0 + t // 2][:, t % 2 * SC:(t % 2 + 1) * SC], h_blk(k, tokens(g, t)),
                                       (w_hi[n % 2][:, at:at + SC], w_lo[n % 2][:, at:at + SC]), k == 0, k == KC - 1)
                else:
                    for k in range(KC):
                        if m == 0:
                            pe.wait_ge(h_ready, KC + k + 1)
                        for f in range(2):
                            last = mm3(banks[b0 + f][:, :], w_blk(n, k, f), h_blk(k), k == 0, k == KC - 1)
                last.then_inc(slot_used, 1)
                if m == 0:
                    pe.wait_ge(wf_ready, 1)
                    pe.wait_ge(wf_zero, 2)
                    for k in range(KC):
                        w = slice(k * FH, k * FH + P)
                        last = mm3(banks[7][:, :], (wf_hi[:, w], wf_lo[:, w]), h_blk(k), k == 0, k == KC - 1)
                    last.then_inc(f_ready, 1)
                if m == 5:
                    pe.wait_ge(cum_ready, 1)
                    for t in range(TB):
                        last = pe.transpose(banks[7][:, t * FH:(t + 1) * FH], cum_row[:, t * P:(t + 1) * P],
                                            ident[0:FH, 0:FH])
                    last.then_inc(cum_turned, 1)

            def scores(u):
                job, g, h, subs = TILES[u]
                if u >= 2:
                    pe.wait_ge(scores_read, u - 1)
                p0 = h % 2 * E_
                q, kk = (dq[g], dk[g]) if g < 3 else (fq, fk)
                for t, c0, w in subs:
                    k0 = key_blocks(g, t)[0] * P
                    last = pe.matmul(banks[2 + u % 2][:, c0:c0 + w], q[p0:p0 + E_, h // 2, t * P:(t + 1) * P],
                                     kk[p0:p0 + E_, h // 2, k0:k0 + w], start=True, stop=True)
                last.then_inc(scores_ready, 1)

            def turn_probs(u):
                _, _, _, subs = TILES[u]
                pe.wait_ge(probs_ready, u + 1)
                if u >= 2:
                    pe.wait_ge(pT_ready, u - 1)
                for c0 in range(0, subs[-1][1] + subs[-1][2], P):
                    last = pe.transpose(banks[4 + u % 2][:, c0:c0 + P], tmpB[:, u % 2, c0:c0 + P], ident[:, :])
                last.then_inc(turned, 1)

            def values(u):
                job, g, h, subs = TILES[u]
                pe.wait_ge(pT_ready, u + 1)
                if job >= 2:
                    pe.wait_ge(o_free, job - 1)
                if u == FIRST_FOX:
                    pe.wait_ge(p0_free, 6)
                    pe.wait_ge(p1_free, 6)
                for t, c0, w in subs:
                    blocks = key_blocks(g, t)
                    for i_, b in enumerate(blocks):
                        v = dv[g][:, b, h * E_:(h + 1) * E_] if g < 3 else fv[:, b, h * E_:(h + 1) * E_]
                        last = pe.matmul(banks[6 + job % 2][:, t * E_:(t + 1) * E_],
                                         pT[:, u % 2, c0 + i_ * P:c0 + (i_ + 1) * P], v,
                                         start=i_ == 0, stop=i_ == len(blocks) - 1)
                last.then_inc(pv_ready, 1)

            pe.wait_ge(qkv_evac, 2 * N_QKV)
            for m in range(N_OVER):
                n = S_OVER + m
                pe.wait_ge(split_done, n + 1)
                steps = []
                for f in range(2):
                    if m in (4, 5):
                        steps += [(f, t, k) for t in (2 * f, 2 * f + 1) for k in range(KC)]
                    else:
                        steps += [(f, None, k) for k in range(KC)]
                third = -(-len(steps) // 3)
                for j in range(3):
                    for f, t, k in steps[j * third:(j + 1) * third]:
                        if k == 0 and (t is None or t % 2 == 0):
                            if m >= 1:
                                pe.wait_ge(p1_free if f else p0_free, m)
                            if f == 0 and 0 <= m - 1 - 4 < FH:
                                pe.wait_ge(ck_free, m - 4)
                        if t is None:
                            last = mm3(banks[f][:, :], w_blk(n, k, f), h_blk(k), k == 0, k == KC - 1)
                        else:
                            last = mm3(banks[f][:, t % 2 * SC:(t % 2 + 1) * SC], h_blk(k, slice(t * P, (t + 1) * P)),
                                       (w_hi[n % 2][:, k * SC:(k + 1) * SC], w_lo[n % 2][:, k * SC:(k + 1) * SC]),
                                       k == 0, k == KC - 1)
                        if k == KC - 1 and t in (None, 1, 3):
                            last.then_inc(slot_used if f else proj_ready, 1)
                    s = 3 * m + j
                    if j == 2 and 4 <= m < 4 + FH:
                        pe.wait_ge(p0_free, m + 1)
                        pe.matmul(banks[0][:, :], nsel[:, m - 4, :], cum_row[:, :], start=True, stop=True)\
                          .then_inc(ck_ready, 1)
                    if 0 <= s - 2 < N_TILES:
                        values(s - 2)
                    if 0 <= s - 1 < N_TILES:
                        turn_probs(s - 1)
                    if s < N_TILES:
                        scores(s)

            pe.wait_ge(comb, 12)
            pe.wait_ge(o_free, len(JOBS))
            pe.wait_ge(p0_free, N_OVER)
            pe.wait_ge(p1_free, N_OVER)
            for fb in range(2):
                for g in range(2):
                    for t in range(TB):
                        last = pe.transpose(banks[2 + 2 * fb + g][:, t * P:(t + 1) * P],
                                            o_dil[:, g, t, fb * P:(fb + 1) * P], ident[:, :])
                    last.then_inc(y_turned, 1)
            for fc in range(4):
                for t in range(TB):
                    last = pe.transpose(banks[(6 + fc) % 8][:, t * P:(t + 1) * P], o_fox[:, t, fc * P:(fc + 1) * P],
                                        ident[:, :])
                last.then_inc(y_turned, 1)
            pe.wait_ge(y_ready, 6)
            for d2 in range(N_BR):
                n = S_BR + d2
                pe.wait_ge(split_done, n + 1)
                if d2 >= 2:
                    pe.wait_ge(msum_ready, 2 * (d2 - 1))
                for dd in range(2):
                    b0 = 4 * (d2 % 2) + 2 * dd
                    for k in range(2):
                        mm3(banks[b0][:, :], w_blk(n, k, dd), (y_hi[:, k, :], y_lo[:, k, :]), k == 0, k == 1)
                    for k in range(4):
                        last = mm3(banks[b0 + 1][:, :], w_blk(n, k, dd, at=2 * SC),
                                   (y_hi[:, 2 + k, :], y_lo[:, 2 + k, :]), k == 0, k == 3)
                    last.then_inc(slot_used if dd else br_ready, 1)
            for d2 in range(N_OUT):
                n = S_OUT + d2
                pe.wait_ge(split_done, n + 1)
                if d2 >= 2:
                    pe.wait_ge(x_updated, KC + 2 * (d2 - 1))
                if d2 == N_OUT - 1:
                    stats(KC + 2 * (d2 - 1))
                    stats(KC + 2 * (d2 - 1) + 1)
                    last_slot(n, KC, 2 * (d2 % 2), KC + 2 * d2, h_blk, True, True)
                    continue
                for k in range(KC):
                    if d2 == 0:
                        pe.wait_ge(merged, k + 1)
                    for dd in range(2):
                        last = mm3(banks[2 * (d2 % 2) + dd][:, :], w_blk(n, k, dd), h_blk(k), k == 0, k == KC - 1)
                        if dd == 0 and k == KC - 1:
                            last.then_inc(half_done, 1)
                    if k == 3 and d2 >= 1:
                        stats(KC + 2 * (d2 - 1))
                        stats(KC + 2 * (d2 - 1) + 1)
                last.then_inc(slot_used, 1)
            rstd_rows(2)
            with pe.Fori(0, GU_IT) as i:
                gate_up(1, i)
            for j in range(2):
                down(1, j, hid2)
            pe.wait_ge(xg_ready, KC)
            pe.wait_ge(var_ready, 4)
            for t in range(TB):
                for half in range(2):
                    for k in range(4):
                        last = pe.transpose(banks[FIN_BANK[t] + half][:, k * P:(k + 1) * P],
                                            xT[:, 4 * half + k, t * P:(t + 1) * P], ident[:, :])
                    last.then_inc(fin_turned, 1)


_INS = ["x", "c", "ada_w", "ada_b", "norm_ffn1", "ffn1_w_gate", "ffn1_w_up", "ffn1_w_down", "norm_mix", "w_in",
        "forget_bias", "w_branch_a", "w_branch_b", "w_out", "norm_ffn2", "ffn2_w_gate", "ffn2_w_up", "ffn2_w_down",
        "norm_final"]


def kernel(**inputs):
    import numpy as _np
    import concourse.bacc as _bacc
    from concourse import mybir as _mybir
    from concourse.bass_utils import run_bass_kernel_spmd as _run

    nc = _bacc.Bacc("TRN2", target_bir_lowering=False, num_devices=1)
    arrays, args = {}, []
    for name in _INS:
        a = _np.ascontiguousarray(inputs[name])
        if name != "norm_final":
            a = a[0]
        arrays[f"in_{name}"] = a
        args.append(nc.dram_tensor(f"in_{name}", a.shape, _mybir.dt.from_np(a.dtype), kind="ExternalInput").ap())
    args.append(nc.dram_tensor("out_y", (T, D), F32, kind="ExternalOutput").ap())
    build(nc, *args)
    r = _run(nc, [arrays], core_ids=[0])
    return r.results[0]["out_y"].reshape(1, T, D)
```

```python
from contextlib import ExitStack

import concourse.bass as bass
from concourse import mybir

F32 = mybir.dt.float32
F32R = mybir.dt.float32r
I32 = mybir.dt.int32
ALU = mybir.AluOpType
ACT = mybir.ActivationFunctionType
AX = mybir.AxisListType

P = 128
D = 1024
T = 512
KC = D // P
TB = T // P
DFF = 2816
FB = DFF // P
SC = 256
E_ = 64
NG, GH, FH = 3, 4, 8
DILW, FOXW = NG * GH * E_, FH * E_
DILATION = (1, 4, 16)
EPS = 1e-6
NEG = -1e30
COL_Q, COL_K, COL_V = 0, DILW, 2 * DILW
COL_FQ = 3 * DILW
COL_FK, COL_FV, COL_F = COL_FQ + FOXW, COL_FQ + 2 * FOXW, COL_FQ + 3 * FOXW
COL_GA = COL_F + FH

GU_IT = DFF // SC
DOWN_PARTS = ((0, 8), (8, 8), (16, 6))
N_DOWN = (D // SC) * len(DOWN_PARTS)
N_FFN = 2 * GU_IT + N_DOWN
N_QKV, N_OVER, N_BR, N_OUT = 9, 14, 4, 4
S_MIX = N_FFN
S_OVER = S_MIX + N_QKV
S_BR = S_OVER + N_OVER
S_OUT = S_BR + N_BR
S_FFN2 = S_OUT + N_OUT
N_SLOTS = S_FFN2 + N_FFN

PRO_CHUNKS = 2 * KC
GU_PAIRS, DOWN_PAIRS = 2, 3
PAIR_STEPS = 2 * KC
ADA_REST = ((GU_IT - 1, GU_PAIRS, (), 2), (GU_IT, DOWN_PAIRS, (2, 3, 4), 6), (GU_IT + 1, DOWN_PAIRS, (6, 7, 8), 10))

SLOPE = [2.0 ** (-8.0 * (i + 1) / (NG * GH)) for i in range(NG * GH)]


def attention_tiles():
    tiles, job = [], 0
    for h in range(GH):
        tiles.append((job, 0, h, [(0, 0, P), (1, P, 2 * P)]))
        tiles.append((job, 0, h, [(2, 0, 2 * P), (3, 2 * P, 2 * P)]))
        job += 1
    for g in (1, 2):
        for h in range(GH):
            tiles.append((job, g, h, [(r, r * P, P) for r in range(TB)]))
            job += 1
    for h in range(FH):
        tiles.append((job, 3, h, [(0, 0, P), (1, P, 2 * P)]))
        tiles.append((job, 3, h, [(2, 0, 3 * P)]))
        tiles.append((job, 3, h, [(3, 0, 4 * P)]))
        job += 1
    return tiles


TILES = attention_tiles()
N_TILES = len(TILES)
LAST_TILE = {}
for _u, _t in enumerate(TILES):
    LAST_TILE[_t[0]] = _u
FIRST_FOX = 2 * GH + 2 * GH
QKV = [("q", 0), ("v", 0), ("v", 1), ("v", 2), ("k", 0), ("q", 1), ("k", 1), ("q", 2), ("k", 2)]
PRO_PE = ((1, 4), (1, 3, 5))
PRO_DVE = tuple([k for k in range(KC) if k not in pe_] for pe_ in PRO_PE)
COMB_LN, COMB_EXP = FIRST_FOX + 5, FIRST_FOX + 12
FOX_BANK = (6, 0, 1, 7)
BR_BANK = ((6, 0), (2, 4))
FIN_BANK = ((4, 6, 0, 5), (2, 3, 1, 7))
TAIL_BANK = ((2, 3), (0, 1))
JOBS = {t[0]: (t[1], t[2]) for t in TILES}


def mixer_columns():
    cols_ = [{"q": COL_Q, "k": COL_K, "v": COL_V}[what] + SC * g for what, g in QKV]
    for c0 in (COL_FQ, COL_FK, COL_FV):
        cols_ += [c0, c0 + SC]
    return cols_ + [COL_GA + SC * j for j in range(2 * D // SC)]


def key_blocks(group, t):
    if group == 0:
        return [t] if t == 0 else [t - 1, t]
    if group in (1, 2):
        return [t]
    return list(range(t + 1))


def build(nc, x, c, ada_w, ada_b, norm_ffn1, w_gate1, w_up1, w_down1, norm_mix, w_in, forget_bias,
          w_branch_a, w_branch_b, w_out, norm_ffn2, w_gate2, w_up2, w_down2, norm_final, out):
    ctx = ExitStack()
    with ctx:
        def sb(name, shape, dt=F32, where=ctx):
            return where.enter_context(nc.sbuf_tensor(name, shape, dt))

        def sem(name):
            return ctx.enter_context(nc.semaphore(name))

        GAIN = 9 * KC
        xT = sb("xT", [P, KC, T])
        h_hi = sb("h_hi", [P, KC, T], F32R)
        h_lo = sb("h_lo", [P, KC, T], F32R)
        raw = [sb(f"raw{s}", [P, KC * SC]) for s in range(2)]
        w_hi = [sb(f"w_hi{s}", [P, KC * SC], F32R) for s in range(2)]
        w_lo = [sb(f"w_lo{s}", [P, KC * SC], F32R) for s in range(2)]
        tmpA = sb("tmpA", [P, 2, T])
        tmpB = sb("tmpB", [P, 2, T])
        ident = sb("ident", [P, P])
        half_neg = sb("half_neg", [P, P])
        c_rows = sb("c_rows", [KC, P])
        rows = sb("rows", [GAIN + 4 * KC, P])
        cols = sb("cols", [P, GAIN + 4 * KC])
        c_act = sb("c_act", [P, KC])
        mod = sb("mod", [P, 9 * KC])
        scale_a = sb("scale_a", [P, 3, KC])
        gate_c = sb("gate_c", [P, 3, KC])
        ada_col = sb("ada_col", [P, 2 * KC])
        ss = sb("ss", [P, TB])
        var = sb("var", [P, TB])
        std = sb("std", [P, TB])
        r0 = sb("r0", [P, TB])
        nw = sb("nw", [P, TB])
        rstd_m2 = sb("rstd_m2", [P, TB])
        rstd = sb("rstd", [P, TB])
        mod_part = sb("mod_part", [P, 2 * KC])
        ss_part = sb("ss_part", [P, 2, TB])
        eps_col = sb("eps_col", [P, 1])
        fbias = sb("fbias", [FH, 1])

        banks = [ctx.enter_context(nc.psum_tensor(f"bank{i}", [P, T], F32)) for i in range(8)]

        ffn1 = ExitStack()
        ada_ring = sb("ada_ring", [P, KC, 2 * P], where=ffn1)
        ada_acc = [sb(f"ada_acc{s}", [P, P], where=ffn1) for s in range(2 * DOWN_PAIRS)]
        pro = ExitStack()
        x_nat = sb("x_nat", [P, TB, D], where=pro)
        ada_pro = [sb(f"ada_pro{s}", [P, KC, D], where=pro) for s in range(2)]
        acc_pro = [sb(f"acc_pro{s}", [P, D], where=pro) for s in range(2)]
        pro.close()
        hid1 = [sb(f"hid1_{s}", [P, FB, T], F32R, where=ffn1) for s in ("hi", "lo")]
        ffn1.close()

        mix = ExitStack()
        dil = sb("dil", [P, 9 * 2 * T], where=mix)
        dq = [dil[:, (g * 6) * T:(g * 6 + 2) * T].rearrange("p (c t) -> p c t", c=2) for g in range(NG)]
        dk = [dil[:, (g * 6 + 2) * T:(g * 6 + 4) * T].rearrange("p (c t) -> p c t", c=2) for g in range(NG)]
        dv = [dil[:, (g * 6 + 4) * T:(g * 6 + 6) * T].rearrange("p (t e) -> p t e", t=TB) for g in range(NG)]
        ckb = [dil[:, s * T:(s + 1) * T] for s in range(2)]
        gates = dil[:, 2 * T:18 * T].rearrange("p (c t) -> p c t", c=16)
        o_dil = sb("o_dil", [P, NG, TB, GH * E_], where=mix)
        o_fox = sb("o_fox", [P, TB, FOXW], where=mix)
        pT = sb("pT", [P, 2, T], where=mix)
        alibi = sb("alibi", [P, 2, 2 * P], where=mix)
        rel = sb("rel", [P, 2 * P], where=mix)
        m_band = sb("m_band", [P, 2 * P], where=mix)
        m_causal = sb("m_causal", [P, P], where=mix)
        m_res = sb("m_res", [P, P], where=mix)
        i_rel = sb("i_rel", [P, 2 * P], I32, where=mix)
        i_and = sb("i_and", [P, P], I32, where=mix)
        neg_head = sb("neg_head", [FH, FH], F32R, where=mix)
        cum_hi = sb("cum_hi", [FH, T], F32R, where=mix)
        cum_lo = sb("cum_lo", [FH, T], F32R, where=mix)
        wf = sb("wf", [P, KC, FH], where=mix)
        wf_hi = sb("wf_hi", [P, KC * FH + P], F32R, where=mix)
        wf_lo = sb("wf_lo", [P, KC * FH + P], F32R, where=mix)
        f_x, f_abs, ls_row, zeros_row = tmpA[0:FH, 0, :], tmpA[0:FH, 1, :], tmpB[0:FH, 0, :], tmpB[0:FH, 1, :]
        cum_row = sb("cum_row", [FH, T], where=mix)
        cum_col = sb("cum_col", [P, TB, FH], where=mix)
        mx = sb("mx", [P, 4, TB, FH], where=mix)
        nmx = sb("nmx", [P, 2, TB], where=mix)
        zs = sb("zs", [P, 4, TB, FH], where=mix)
        rz = sb("rz", [P, 2, TB], where=mix)
        lse = sb("lse", [P, NG, TB * GH], where=mix)
        gmax = sb("gmax", [P, TB * GH], where=mix)
        gw = sb("gw", [P, NG, TB * GH], where=mix)
        gsum = sb("gsum", [P, TB * GH], where=mix)
        gw0 = sb("gw0", [P, TB * GH], where=mix)
        foxmem = ExitStack()
        fq = sb("fq", [P, 4, T], where=foxmem)
        fk = sb("fk", [P, 4, T], where=foxmem)
        fv = sb("fv", [P, TB, FOXW], where=foxmem)
        foxmem.close()
        ybr = ExitStack()
        y_hi = sb("y_hi", [P, 6, T], F32R, where=ybr)
        y_lo = sb("y_lo", [P, 6, T], F32R, where=ybr)
        ybr.close()
        mix.close()

        ffn2 = ExitStack()
        hid2 = [sb(f"hid2_{s}", [P, FB, T], F32R, where=ffn2) for s in ("hi", "lo")]
        ffn2.close()
        fin = ExitStack()
        y_sb = sb("y_sb", [P, TB, D], where=fin)
        fin.close()

        lse_dram = nc.dram_tensor("lse_scratch", [T, GH], F32).ap()
        gw_dram = nc.dram_tensor("gw_scratch", [T, GH], F32).ap()

        raw_landed = [sem(f"raw_landed{s}") for s in range(2)]
        br_b_landed = [sem(f"br_b_landed{s}") for s in range(2)]
        split_hi = sem("split_hi")
        split_done = sem("split_done")
        split_half = sem("split_half")
        slot_used = sem("slot_used")
        bank01_free = sem("bank01_free")
        bank23_free = sem("bank23_free")
        hid_hi_ready, hid_ready = sem("hid_hi_ready"), sem("hid_ready")
        half_done = sem("half_done")
        tail_done = sem("tail_done")
        tail_updated, tail_sq, tail_added = sem("tail_updated"), sem("tail_sq"), sem("tail_added")
        x_updated = sem("x_updated")
        sq_ready = sem("sq_ready")
        sq_added = sem("sq_added")
        stat_done = sem("stat_done")
        ident_step, const_ready, eps_ready = sem("ident_step"), sem("const_ready"), sem("eps_ready")
        rows_landed, fb_landed = sem("rows_landed"), sem("fb_landed")
        x_landed = [sem(f"x_landed{t}") for t in range(TB)]
        c_landed, c_turned, cact_ready = sem("c_landed"), sem("c_turned"), sem("cact_ready")
        rows_turned, cols_ready = sem("rows_turned"), sem("cols_ready")
        x_turned, ss_ready = sem("x_turned"), sem("ss_ready")
        pro_landed = [sem(f"pro_landed{k}") for k in range(2 * KC)]
        ada_landed = [sem(f"ada_landed{s}") for s in range(2)]
        pro_step, pro_turned, pro_red = sem("pro_step"), sem("pro_turned"), sem("pro_red")
        pro_mm, scale1_ready = sem("pro_mm"), sem("scale1_ready")
        ada_step = sem("ada_step")
        ada_red = sem("ada_red")
        ada_mm = sem("ada_mm")
        mod_ready = sem("mod_ready")
        coef_ready = sem("coef_ready")
        ss_step, neg_step = sem("ss_step"), sem("neg_step")
        rstd_ready = sem("rstd_ready")
        var_ready, std_ready, rstd_step = sem("var_ready"), sem("std_ready"), sem("rstd_step")
        rstd_bc = sem("rstd_bc")
        t_ready, h_hi_ready, h_ready = sem("t_ready"), sem("h_hi_ready"), sem("h_ready")
        qkv_evac = sem("qkv_evac")
        mask_step, mask_ready, res_ready = sem("mask_step"), sem("mask_ready"), sem("res_ready")
        wf_zero = sem("wf_zero")
        wf_landed, wf_hi_ready, wf_ready = sem("wf_landed"), sem("wf_hi_ready"), sem("wf_ready")
        f_ready, f_step, f_act = sem("f_ready"), sem("f_step"), sem("f_act")
        cum_ready, cum_split = sem("cum_ready"), sem("cum_split")
        cum_turned, cumcol_ready = sem("cum_turned"), sem("cumcol_ready")
        proj_ready = sem("proj_ready")
        p0_free, p1_free = sem("p0_free"), sem("p1_free")
        ck_ready, ck_free = sem("ck_ready"), sem("ck_free")
        scores_ready = sem("scores_ready")
        alibi_ready, bias_step = sem("alibi_ready"), sem("bias_step")
        scores_read = sem("scores_read")
        max_step, max_ready = sem("max_step"), sem("max_ready")
        probs_ready, turned, pT_ready = sem("probs_ready"), sem("turned"), sem("pT_ready")
        pv_ready, rz_ready, o_free = sem("pv_ready"), sem("rz_ready"), sem("o_free")
        comb, comb_act = sem("comb"), sem("comb_act")
        lse_out, lse_in, gw_out, gw_in = sem("lse_out"), sem("lse_in"), sem("gw_out"), sem("gw_in")
        y_turned, y0_ready, ysum_ready = sem("y_turned"), sem("y0_ready"), sem("ysum_ready")
        y_hi_ready, y_ready = sem("y_hi_ready"), sem("y_ready")
        sig_ready, br_ready = sem("sig_ready"), sem("br_ready")
        merge_step, msum_ready, merge_hi, merged = sem("merge_step"), sem("msum_ready"), sem("merge_hi"), sem("merged")
        xg_ready, fin_turned = sem("xg_ready"), [sem(f"fin_turned{s}") for s in range(2)]
        y_act, y_dve, out_done = sem("y_act"), sem("y_dve"), sem("out_done")

        BANKS = (KC // 2, KC // 2 + 2 * GU_IT)
        FFN_SLOT = (0, S_FFN2)
        N_PAIRS = GU_IT * GU_PAIRS + 2 * DOWN_PAIRS
        assert PRO_CHUNKS + 2 * N_PAIRS == 9 * KC

        def slot_size(n):
            for base in FFN_SLOT:
                if base + 2 * GU_IT <= n < base + N_FFN and (n - base - 2 * GU_IT) % 3 == 2:
                    return DOWN_PARTS[2][1] * SC
            return 6 * SC if S_BR <= n < S_OUT else KC * SC

        def landed(eng, n, loop=0):
            eng.wait_ge(raw_landed[n % 2], 16 * (n // 2 + 1) + loop)
            if S_BR <= n < S_OUT:
                eng.wait_ge(br_b_landed[n % 2], 16 * ((n - S_BR) // 2 + 1))

        sq_sum = tmpB[:, 0, :]

        def qkv_bank(m):
            return 2 * ((m + 1) % 2)

        def added(b):
            return (KC - 2) * (b // KC) + b % KC

        def half_count(b):
            return (KC // 2 - 1) * (b // KC) + b % KC // 2 + 1

        def norm_of(r):
            return (r + 1) // 2

        def tiles_of(r):
            return range(TB) if r == 0 else range((r - 1) % 2 * TB // 2, ((r - 1) % 2 + 1) * TB // 2)

        def tl(r):
            return slice(tiles_of(r)[0], tiles_of(r)[-1] + 1)

        def tok(r):
            return slice(tiles_of(r)[0] * P, (tiles_of(r)[-1] + 1) * P)

        def rstd_bank(r):
            return banks[4 if r and r % 2 == 0 else 6]

        def norm_t(k, r):
            return (tmpA, tmpB)[k // 2 % 2][:, k % 2, tok(r)]

        block = ctx.enter_context(nc.Block())

        @block.sync
        def _(sp):
            def rows_of(w):
                return w.rearrange("(k p) c -> p k c", p=P)

            def slot_dst(n, nk, at=0):
                return raw[n % 2][:, at:at + nk * SC].rearrange("p (k c) -> p k c", k=nk)

            def load(n, nk, src, loop=0):
                if n >= 2:
                    sp.wait_ge(split_done, n - 1 + loop)
                sp.dma_start(slot_dst(n, nk), src).then_inc(raw_landed[n % 2], 16)

            def gate_up(base, wg, wu, i):
                for j, w in enumerate((wg, wu)):
                    load(base + j, KC, rows_of(w)[:, :, bass.ds(SC * i, SC)], 2 * i)

            def gate_up_from1(wg, wu, i):
                for j, w in enumerate((wg, wu)):
                    load(2 + j, KC, rows_of(w)[:, :, bass.ds(SC * i + SC, SC)], 2 * i)

            def down(base, w, j):
                for s in range(6):
                    k0, nk = DOWN_PARTS[s % 3]
                    load(base + s, nk, rows_of(w)[:, k0:k0 + nk, bass.ds(2 * SC * j + SC * (s // 3), SC)], 6 * j)

            sp.dma_start(c_rows[:, :], c.rearrange("(r p) -> r p", p=P)).then_inc(c_landed, 16)
            for t in range(TB):
                sp.dma_start(x_nat[:, t, :], x[t * P:(t + 1) * P, :]).then_inc(x_landed[t], 16)
            for j in (1, 0):
                for k in range(KC):
                    sp.dma_start(ada_pro[j][:, k, :], ada_w[k * P:(k + 1) * P, j * D:(j + 1) * D])\
                      .then_inc(pro_landed[j * KC + k], 16)
            load(0, KC, rows_of(w_gate1)[:, :, 0:SC])
            load(1, KC, rows_of(w_up1)[:, :, 0:SC])
            with sp.Fori(0, GU_IT - 1) as i:
                gate_up_from1(w_gate1, w_up1, i)
            with sp.Fori(0, 2) as j:
                down(2 * GU_IT, w_down1, j)
            for m, col in enumerate(mixer_columns()):
                load(S_MIX + m, KC, rows_of(w_in)[:, :, col:col + SC])
                if m == 1:
                    sp.wait_ge(slot_used, N_FFN)
                    sp.dma_start(wf[:, :, :], rows_of(w_in)[:, :, COL_F:COL_F + FH]).then_inc(wf_landed, 16)
            for d2 in range(N_BR):
                n = S_BR + d2
                load(n, 2, rows_of(w_branch_a)[:, :, d2 * SC:(d2 + 1) * SC])
                sp.dma_start(slot_dst(n, 4, at=2 * SC), rows_of(w_branch_b)[:, :, d2 * SC:(d2 + 1) * SC])\
                  .then_inc(br_b_landed[n % 2], 16)
            for d2 in range(N_OUT):
                load(S_OUT + d2, KC, rows_of(w_out)[:, :, d2 * SC:(d2 + 1) * SC])
            with sp.Fori(0, GU_IT) as i:
                gate_up(S_FFN2, w_gate2, w_up2, i)
            with sp.Fori(0, 2) as j:
                down(S_FFN2 + 2 * GU_IT, w_down2, j)
            for t in range(TB):
                for half, done in enumerate((y_act, y_dve)):
                    sp.wait_ge(done, t + 1)
                    sp.dma_start(out[t * P:(t + 1) * P, half * T:(half + 1) * T], y_sb[:, t, half * T:(half + 1) * T])\
                      .then_inc(out_done, 16)
            sp.wait_ge(out_done, 16 * 2 * TB)

        @block.gpsimd
        def _(pool):
            pool.memset(ident[:, :], 0.0).then_inc(ident_step, 1)
            pool.memset(half_neg[:, :], 0.0).then_inc(ident_step, 1)
            pool.memset(eps_col[:, :], EPS).then_inc(eps_ready, 1)
            pool.wait_ge(ident_step, 2)
            pool.affine_select(out=ident[:, :], in_=ident[:, :], compare_op=ALU.not_equal, fill=1.0,
                               base=0, pattern=[[-1, P]], channel_multiplier=1).then_inc(const_ready, 1)
            pool.affine_select(out=half_neg[:, :], in_=half_neg[:, :], compare_op=ALU.not_equal, fill=-0.5,
                               base=0, pattern=[[-1, P]], channel_multiplier=1).then_inc(const_ready, 1)

            def ada_pair(pair, i=0):
                for half in range(2):
                    if pair:
                        pool.wait_ge(ada_step, PAIR_STEPS * pair - PAIR_STEPS // 2 * (1 - half) + GU_PAIRS * PAIR_STEPS * i)
                    k0 = KC // 2 * half
                    col = (PRO_CHUNKS + 2 * pair) * P + 2 * GU_PAIRS * P * i
                    pool.dma_start(ada_ring[:, k0:k0 + KC // 2, :],
                                   ada_w.rearrange("(k p) c -> p k c", p=P)[:, k0:k0 + KC // 2, bass.ds(col, 2 * P)])\
                        .then_inc(ada_landed[half], 16)

            pool.wait_ge(pro_landed[KC - 1], 16)
            ada_pair(0)
            with pool.Fori(0, GU_IT) as i:
                for q in range(GU_PAIRS):
                    ada_pair(q + 1, i)
            for pair in range(GU_IT * GU_PAIRS + 1, N_PAIRS):
                ada_pair(pair)

            def lo_beside(n):
                pool.wait_ge(split_hi, n + 1)
                pool.wait_ge(split_done, n)
                pool.tensor_tensor(w_lo[n % 2][:, :], raw[n % 2][:, :], w_hi[n % 2][:, :].bitcast(F32),
                                   ALU.subtract).then_inc(split_done, 1)

            pool.wait_ge(slot_used, N_FFN)
            pool.iota(i_rel[:, :], pattern=[[-1, 2 * P]], base=P, channel_multiplier=1).then_inc(mask_step, 1)
            pool.memset(m_band[:, :], 0.0).then_inc(mask_step, 1)
            pool.memset(m_causal[:, :], 0.0).then_inc(mask_step, 1)
            for w in (wf_hi, wf_lo):
                pool.memset(w[:, KC * FH:].bitcast(F32), 0.0).then_inc(wf_zero, 1)
            pool.wait_ge(mask_step, 3)
            pool.affine_select(out=m_band[:, :], in_=m_band[:, :], compare_op=ALU.is_ge, fill=NEG, base=P,
                               pattern=[[-1, 2 * P]], channel_multiplier=1).then_inc(mask_step, 1)
            pool.wait_ge(mask_step, 4)
            pool.affine_select(out=m_band[:, :], in_=m_band[:, :], compare_op=ALU.is_ge, fill=NEG, base=0,
                               pattern=[[1, 2 * P]], channel_multiplier=-1).then_inc(mask_ready, 1)
            pool.affine_select(out=m_causal[:, :], in_=m_causal[:, :], compare_op=ALU.is_ge, fill=NEG, base=0,
                               pattern=[[-1, P]], channel_multiplier=1).then_inc(mask_ready, 1)

            lo_beside(S_MIX + 1)

            pool.wait_ge(comb, 1)
            pool.dma_start(lse_dram.rearrange("(t p) h -> p t h", p=P),
                           lse[:, 0, :].rearrange("p (t h) -> p t h", t=TB)).then_inc(lse_out, 16)
            pool.wait_ge(lse_out, 16)
            pool.dma_start(lse[:, 0, :], lse_dram.rearrange("(i r) h -> i (r h)", r=TB)).then_inc(lse_in, 16)
            pool.wait_ge(comb, 8)
            pool.dma_start(gw_dram.rearrange("(i r) h -> i (r h)", r=TB), gw[:, 0, :]).then_inc(gw_out, 16)
            pool.wait_ge(gw_out, 16)
            pool.dma_start(gw0[:, :].rearrange("p (t h) -> p t h", t=TB),
                           gw_dram.rearrange("(t p) h -> p t h", p=P)).then_inc(gw_in, 16)
            lo_beside(S_FFN2 + 1)

        @block.scalar
        def _(act):
            def hi(n, loop=0, loop_landed=0):
                landed(act, n, loop_landed)
                if n >= 2:
                    act.wait_ge(slot_used, n - 1 + loop)
                m = slot_size(n)
                act.activation(w_hi[n % 2][:, 0:m], raw[n % 2][:, 0:m], ACT.Copy).then_inc(split_hi, 1)

            HI_AFTER = (1, KC - 4, KC - 3, KC - 2)

            def hi_part(n, part):
                if part == 0:
                    landed(act, n)
                    act.wait_ge(slot_used, n - 1)
                c_ = slice(part * 2 * SC, (part + 1) * 2 * SC)
                ins = act.activation(w_hi[n % 2][:, c_], raw[n % 2][:, c_], ACT.Copy)
                if part == 3:
                    ins.then_inc(split_hi, 1)

            def norm_std(r):
                if r:
                    act.wait_ge(ss_step, 3 * r)
                else:
                    act.wait_ge(ss_ready, TB)
                    act.wait_ge(eps_ready, 1)
                act.activation(std[:, tl(r)], ss[:, tl(r)], ACT.Sqrt, scale=1.0 / D, bias=eps_col[:, 0:1])\
                   .then_inc(std_ready, 1)

            def norm_hi(r, next_slot):
                if r == 0:
                    act.wait_ge(mod_ready, 1)
                for k in range(KC):
                    c0 = 3 * KC * norm_of(r) + k
                    act.wait_ge(t_ready, KC * r + k + 1)
                    act.activation(h_hi[:, k, tok(r)], norm_t(k, r), ACT.Identity, bias=mod[:, c0:c0 + 1])\
                       .then_inc(h_hi_ready, 1)
                    if r % 2 == 1 and k == KC // 2 - 1:
                        norm_std(r + 1)
                    if r == 0 and k == KC // 2 - 1:
                        hi(next_slot)
                    if r % 2 == 1 and k in HI_AFTER:
                        hi_part(next_slot, HI_AFTER.index(k))

            def tail_squares(q):
                b0 = KC * q - 2
                for e in range(2):
                    r = 2 * q - 1 + e
                    for b in (b0, b0 + 1):
                        if e:
                            act.wait_ge(x_updated, b + 1)
                        else:
                            act.wait_ge(tail_updated, 2 * (q - 1) + b - b0 + 1)
                        act.wait_ge(sq_added, added(b - 2))
                        act.activation(tmpA[:, b % 2, tok(r)], xT[:, b % KC, tok(r)], ACT.Square)\
                           .then_inc(sq_ready if e else tail_sq, 1)
                        if q == 3:
                            act.wait_ge(sq_ready if e else tail_sq, b + 1 if e else 2 * (q - 1) + b - b0 + 1)
                            gain(b % KC, tok(r))
                    if e == 0:
                        norm_std(r)

            def ffn_gate_up(fi, i, hid):
                base, bank0, hid0 = FFN_SLOT[fi], BANKS[fi], 2 * GU_IT * fi
                for f in range(2):
                    act.wait_ge(slot_used, base + 1 + 2 * i)
                    act.wait_ge(bank23_free, bank0 - 1 + f + 2 * i)
                    act.activation(tmpA[:, f, :], banks[f][:, :], ACT.Silu).then_inc(bank01_free, 1)
                hi(base + 2, loop=2 * i, loop_landed=16 * i)
                for f in range(2):
                    act.wait_ge(bank23_free, bank0 + 1 + f + 2 * i)
                    act.activation(hid[0][:, 2 * i + f, :], tmpB[:, f, :], ACT.Copy).then_inc(hid_hi_ready, 1)
                hi(base + 3, loop=2 * i, loop_landed=16 * i)

            def ffn_down(fi, j):
                base = FFN_SLOT[fi] + 2 * GU_IT + 6 * j
                for s in range(6):
                    if j == 1 and s == 5:
                        tail_squares(2 * fi + 1)
                        return
                    if s % 3 == 2:
                        squares(2 * KC * fi + 4 * j + 2 * (s // 3))
                    if base + s + 2 < N_SLOTS:
                        hi(base + s + 2)
                    if fi == 1 and s % 3 == 2:
                        for k in range(4 * j + 2 * (s // 3), 4 * j + 2 * (s // 3) + 2):
                            act.wait_ge(sq_ready, 2 * KC + k + 1)
                            gain(k, slice(0, T))

            def gain(k, tok_):
                act.activation(xT[:, k, tok_], xT[:, k, tok_], ACT.Copy,
                               scale=cols[:, GAIN + 3 * KC + k:GAIN + 3 * KC + k + 1]).then_inc(xg_ready, 1)

            def squares(x0):
                for b in (x0, x0 + 1):
                    act.wait_ge(x_updated, b + 1)
                    if b % KC >= 3:
                        act.wait_ge(sq_added, added(b - 2))
                    act.activation(tmpA[:, b % 2, :] if b % KC else sq_sum, xT[:, b % KC, :], ACT.Square)\
                       .then_inc(sq_ready, 1)

            def merge_hi_part(d):
                act.wait_ge(msum_ready, d + 1)
                act.activation(h_hi[:, d, :], tmpB[:, d % 2, :], ACT.Copy).then_inc(merge_hi, 1)

            act.dma_start(rows[0:72, :], ada_b.rearrange("(r p) -> r p", p=P)).then_inc(rows_landed, 16)
            for n, g in enumerate((norm_ffn1, norm_mix, norm_ffn2, norm_final)):
                act.dma_start(rows[GAIN + KC * n:GAIN + KC * (n + 1), :], g.rearrange("(r p) -> r p", p=P))\
                   .then_inc(rows_landed, 16)
            act.dma_start(fbias[:, :], forget_bias.rearrange("(h a) -> h a", a=1)).then_inc(fb_landed, 16)
            act.wait_ge(c_turned, 1)
            act.activation(c_act[:, :], banks[7][:, 0:KC], ACT.Silu).then_inc(cact_ready, 1)
            for t in range(TB):
                act.wait_ge(x_landed[t], 16)
                act.activation(tmpA[:, :, :].rearrange("p a t -> p (a t)"), x_nat[:, t, :], ACT.Square,
                               accum_out=ss[:, t:t + 1]).then_inc(ss_ready, 1)
                act.wait_ge(ss_ready, t + 1)
            norm_std(0)
            hi(0)
            norm_hi(0, 1)
            with act.Fori(0, GU_IT) as i:
                ffn_gate_up(0, i, hid1)
            for j in range(2):
                ffn_down(0, j)
            norm_hi(1, S_MIX + 1)
            norm_hi(2, None)

            act.wait_ge(wf_landed, 16)
            act.activation(wf_hi[:, 0:KC * FH], wf[:, :, :].rearrange("p k h -> p (k h)"), ACT.Copy)\
               .then_inc(wf_hi_ready, 1)
            for m in range(N_QKV):
                if m == 2:
                    act.wait_ge(f_step, 3)
                    act.activation(f_abs, f_abs, ACT.Exp).then_inc(f_act, 1)
                    act.wait_ge(f_act, 1)
                    act.activation(f_abs, f_abs, ACT.Ln, bias=1.0).then_inc(f_act, 1)
                if m == 5:
                    act.wait_ge(cum_ready, 1)
                    act.activation(neg_head[:, :], ident[0:FH, 0:FH], ACT.Copy, scale=-1.0)
                    act.activation(cum_hi[:, :], cum_row[:, :], ACT.Copy).then_inc(cum_split, 1)
                hi(S_MIX + 2 + m)

            def exp_tile(u):
                job, g, h, subs = TILES[u]
                act.wait_ge(max_ready, u + 1)
                if u >= 2:
                    act.wait_ge(turned, u - 1)
                for n, (t, c0, w) in enumerate(subs):
                    last = act.activation(tmpB[:, u % 2, c0:c0 + w], tmpA[:, u % 2, c0:c0 + w], ACT.Exp,
                                          bias=nmx[:, u % 2, n:n + 1], accum_out=zs[:, g, t, h:h + 1])
                last.then_inc(probs_ready, 1)

            def evac_pT(u):
                _, _, _, subs = TILES[u]
                w = subs[-1][1] + subs[-1][2]
                act.wait_ge(turned, u + 1)
                if u >= 2:
                    act.wait_ge(pv_ready, u - 1)
                act.activation(pT[:, u % 2, 0:w], banks[4 + u % 2][:, 0:w], ACT.Copy).then_inc(pT_ready, 1)

            for m in range(N_OVER):
                for j in range(3):
                    s = 3 * m + j
                    if j == 0 and 4 <= m - 1 < 4 + FH:
                        h = m - 1 - 4
                        act.wait_ge(ck_ready, h + 1)
                        if h >= 2:
                            act.wait_ge(scores_read, FIRST_FOX + 3 * (h - 1))
                        act.activation(ckb[h % 2], banks[0][:, :], ACT.Copy).then_inc(ck_free, 1)
                    if 0 <= s - 3 < N_TILES:
                        evac_pT(s - 3)
                    if 0 <= s - 1 < N_TILES:
                        exp_tile(s - 1)
                    if j == 0 and m >= 1:
                        hi(S_OVER + m + 1)
                    if s == COMB_LN:
                        act.wait_ge(o_free, len(JOBS) - FH)
                        act.activation(gw[:, :, :].rearrange("p g (t h) -> p g t h", t=TB), zs[:, 0:NG, :, 0:GH],
                                       ACT.Ln).then_inc(comb_act, 1)
                    if s == COMB_EXP:
                        act.wait_ge(comb, 4)
                        act.activation(gw[:, :, :], gw[:, :, :], ACT.Exp).then_inc(comb_act, 1)
            evac_pT(N_TILES - 1)

            for fb in range(2):
                act.wait_ge(y_turned, 2 * fb + 1)
                act.activation(tmpA[:, fb, :], banks[2 + 2 * fb][:, :], ACT.Copy).then_inc(y0_ready, 1)
            for fc in range(4):
                act.wait_ge(y_turned, 4 + fc + 1)
                act.activation(y_hi[:, 2 + fc, :], banks[FOX_BANK[fc]][:, :], ACT.Copy).then_inc(y_hi_ready, 1)
            for fb in range(2):
                act.wait_ge(ysum_ready, fb + 1)
                act.activation(y_hi[:, fb, :], tmpB[:, fb, :], ACT.Copy).then_inc(y_hi_ready, 1)
            hi(S_BR + 1)
            act.wait_ge(p1_free, N_OVER)
            for d in range(KC):
                act.activation(gates[:, d::KC, :], gates[:, d::KC, :], ACT.Sigmoid).then_inc(sig_ready, 1)
                if d >= 1:
                    merge_hi_part(d - 1)
                if d % 2 == 1:
                    hi(S_BR + d // 2 + 2)
            merge_hi_part(KC - 1)
            for d2 in range(N_OUT):
                if d2 == N_OUT - 1:
                    tail_squares(2)
                else:
                    squares(KC + 2 * d2)
                    hi(S_OUT + d2 + 2)
            norm_hi(3, S_FFN2 + 1)
            norm_hi(4, None)
            with act.Fori(0, GU_IT) as i:
                ffn_gate_up(1, i, hid2)
            for j in range(2):
                ffn_down(1, j)
            for t in range(TB):
                if t == 1:
                    norm_std(6)
                act.wait_ge(fin_turned[0], t + 1)
                act.wait_ge(rstd_ready, t // 2 + 1)
                act.activation(y_sb[:, t, 0:T], banks[FIN_BANK[0][t]][:, :], ACT.Copy, scale=rstd[:, t:t + 1]).then_inc(y_act, 1)

        @block.vector
        def _(dve):
            def lo(n, loop=0):
                dve.wait_ge(split_hi, n + 1 + loop)
                m = slot_size(n)
                dve.tensor_tensor(w_lo[n % 2][:, 0:m], raw[n % 2][:, 0:m], w_hi[n % 2][:, 0:m].bitcast(F32),
                                  ALU.subtract).then_inc(split_done, 1)

            def lo_half(n, half):
                if half == 0:
                    dve.wait_ge(split_hi, n + 1)
                c_ = slice(half * KC * SC // 2, (half + 1) * KC * SC // 2)
                dve.tensor_tensor(w_lo[n % 2][:, c_], raw[n % 2][:, c_], w_hi[n % 2][:, c_].bitcast(F32),
                                  ALU.subtract).then_inc(split_done if half else split_half, 1)

            def sums(r, p):
                dve.wait_ge(stat_done, 2 * (r - 1) + p + 1)
                dve.tensor_reduce(ss_part[:, p, tl(r)],
                                  banks[(5, 7)[p]][:, tok(r)].rearrange("p (t f) -> p t f", t=len(tiles_of(r))), AX.X,
                                  ALU.add).then_inc(ss_step, 1)

            def variance(r):
                if r:
                    dve.wait_ge(ss_step, 3 * r - 1)
                    dve.tensor_tensor(ss[:, tl(r)], ss_part[:, 0, tl(r)], ss_part[:, 1, tl(r)], ALU.add).then_inc(ss_step, 1)
                    dve.wait_ge(ss_step, 3 * r)
                else:
                    dve.wait_ge(ss_ready, TB)
                dve.tensor_scalar(var[:, tl(r)], ss[:, tl(r)], 1.0 / D, EPS, ALU.mult, ALU.add).then_inc(var_ready, 1)

            def root(r, step):
                c_ = tl(r)
                if step == 0:
                    dve.wait_ge(std_ready, r + 1)
                    dve.reciprocal(r0[:, c_], std[:, c_]).then_inc(rstd_step, 1)
                if step == 1:
                    dve.wait_ge(rstd_step, 3 * r + 1)
                    dve.tensor_tensor(nw[:, c_], r0[:, c_], r0[:, c_], ALU.mult).then_inc(rstd_step, 1)
                if step == 2:
                    dve.wait_ge(var_ready, r + 1)
                    dve.wait_ge(rstd_step, 3 * r + 2)
                    dve.tensor_tensor(nw[:, c_], nw[:, c_], var[:, c_], ALU.mult).then_inc(rstd_step, 1)
                if step == 3:
                    dve.wait_ge(rstd_step, 3 * r + 3)
                    dve.scalar_tensor_tensor(out=rstd_m2[:, c_], in0=nw[:, c_], scalar=-3.0, in1=r0[:, c_],
                                             op0=ALU.add, op1=ALU.mult).then_inc(neg_step, 1)

            def final_rstd(r):
                dve.wait_ge(neg_step, r + 1)
                dve.tensor_scalar(rstd[:, tl(r)], rstd_m2[:, tl(r)], -0.5, None, ALU.mult).then_inc(rstd_ready, 1)
                dve.wait_ge(rstd_ready, r - 4)

            def add_squares(b):
                if b % KC == 0:
                    return
                dve.wait_ge(sq_ready, b + 1)
                if b % KC >= 2:
                    dve.wait_ge(sq_added, added(b - 1))
                dve.tensor_tensor(sq_sum, sq_sum, tmpA[:, b % 2, :], ALU.add).then_inc(sq_added, 1)

            def tail(q, n):
                b0 = KC * q - 2

                def update(dd, e):
                    r = 2 * q - 1 + e
                    if dd and e:
                        dve.wait_ge(slot_used, n + 1)
                    else:
                        dve.wait_ge(tail_done, 3 * (q - 1) + 2 * e + dd + 1)
                    b = (b0 + dd) % KC
                    dve.scalar_tensor_tensor(out=xT[:, b, tok(r)], in0=banks[TAIL_BANK[e][dd]][:, tok(r)],
                                             scalar=gate_c[:, q - 1, b:b + 1], in1=xT[:, b, tok(r)], op0=ALU.mult,
                                             op1=ALU.add).then_inc(x_updated if e else tail_updated, 1)

                def add(e):
                    r = 2 * q - 1 + e
                    if e:
                        dve.wait_ge(sq_ready, b0 + 1)
                    else:
                        dve.wait_ge(tail_sq, 2 * (q - 1) + 1)
                    dve.wait_ge(sq_added, added(b0 - 1))
                    dve.tensor_tensor(sq_sum[:, tok(r)], sq_sum[:, tok(r)], tmpA[:, 0, tok(r)], ALU.add)\
                       .then_inc(sq_added if e else tail_added, 1)

                update(0, 0)
                update(1, 0)
                add(0)
                r = 2 * q - 1
                for p in range(2):
                    sums(r, p)
                variance(r)
                update(0, 1)
                for step in range(4):
                    root(r, step)
                update(1, 1)
                add(1)

            def norm_block(r, k):
                if k >= 4:
                    dve.wait_ge(h_ready, KC * r + k - 3)
                q = norm_of(r)
                dve.scalar_tensor_tensor(out=norm_t(k, r), in0=rstd_bank(r)[:, tok(r)], scalar=scale_a[:, q, k:k + 1],
                                         in1=xT[:, k, tok(r)], op0=ALU.mult, op1=ALU.mult).then_inc(t_ready, 1)

            def norm_apply(r, done=0):
                dve.wait_ge(rstd_bc, r + 1)
                for k in range(KC + 1):
                    if done <= k < KC:
                        norm_block(r, k)
                    if k >= 1:
                        c0 = 3 * KC * norm_of(r) + k - 1
                        dve.wait_ge(h_hi_ready, KC * r + k)
                        dve.scalar_tensor_tensor(out=h_lo[:, k - 1, tok(r)], in0=norm_t(k - 1, r),
                                                 scalar=mod[:, c0:c0 + 1], in1=h_hi[:, k - 1, tok(r)].bitcast(F32),
                                                 op0=ALU.add, op1=ALU.subtract).then_inc(h_ready, 1)
                    if r == 0 and k == KC // 2:
                        lo_half(0, 1)
                    if r % 2 == 1:
                        if k in (2, 3):
                            sums(r + 1, k - 2)
                        if k == 3:
                            variance(r + 1)
                        if 4 <= k < KC:
                            root(r + 1, k - 4)

            def ada_pair(q, batch, step, landed_):
                for k in range(KC):
                    for s in range(2):
                        acc, w, ck = ada_acc[2 * q + s], ada_ring[:, k, s * P:(s + 1) * P], c_act[:, k:k + 1]
                        if s == 0 and k % (KC // 2) == 0:
                            dve.wait_ge(ada_landed[k // (KC // 2)], landed_)
                        if k == 0:
                            if not isinstance(batch, int) or batch:
                                dve.wait_ge(mod_ready, batch + 1)
                            dve.tensor_scalar(acc[:, :], w, ck, None, ALU.mult).then_inc(ada_step, 1)
                        else:
                            dve.wait_ge(ada_step, step + 2 * (k - 1) + s + 1)
                            dve.scalar_tensor_tensor(out=acc[:, :], in0=w, scalar=ck, in1=acc[:, :], op0=ALU.mult,
                                                     op1=ALU.add).then_inc(ada_step, 1)

            def ada_add(batch, col, n):
                dve.wait_ge(ada_mm, batch + 1)
                for s0 in range(0, n, TB):
                    m = min(n - s0, TB)
                    ins = dve.tensor_reduce(ada_col[:, s0:s0 + m],
                                            banks[4 if s0 == 0 else 6][:, 0:m * P].rearrange("p (s k) -> p s k", s=m),
                                            AX.X, ALU.add)
                ins.then_inc(ada_red, 1)
                dve.wait_ge(ada_red, batch + 1)
                dve.tensor_tensor(mod[:, bass.ds(col, n)], ada_col[:, 0:n], cols[:, bass.ds(col, n)], ALU.add)\
                   .then_inc(mod_ready, 1)

            def gu(fi, i, hid, prev=None):
                base, bank0, hid0 = FFN_SLOT[fi], BANKS[fi], 2 * GU_IT * fi
                lo(base + 2, 2 * i)
                if fi == 0:
                    if prev is not None:
                        ada_add(prev, PRO_CHUNKS + 2 * GU_PAIRS * prev, 2 * GU_PAIRS)
                    ada_pair(0, i, GU_PAIRS * PAIR_STEPS * i, 16 + 32 * i)
                for f in range(2):
                    dve.wait_ge(slot_used, base + 2 + 2 * i)
                    dve.wait_ge(bank01_free, bank0 + 1 + f + 2 * i)
                    dve.tensor_tensor(tmpB[:, f, :], banks[2 + f][:, :], tmpA[:, f, :], ALU.mult)\
                       .then_inc(bank23_free, 1)
                for f in range(2):
                    dve.wait_ge(hid_hi_ready, hid0 + 1 + f + 2 * i)
                    dve.tensor_tensor(hid[1][:, 2 * i + f, :], tmpB[:, f, :],
                                      hid[0][:, 2 * i + f, :].bitcast(F32), ALU.subtract).then_inc(hid_ready, 1)
                lo(base + 3, 2 * i)
                if fi == 0:
                    ada_pair(1, i, PAIR_STEPS + GU_PAIRS * PAIR_STEPS * i, 32 + 32 * i)

            def add_to_x(g, n, x0, bank):
                for dd in range(2):
                    if dd:
                        dve.wait_ge(slot_used, n + 1)
                    else:
                        dve.wait_ge(half_done, half_count(x0))
                    b = (x0 + dd) % KC
                    dve.scalar_tensor_tensor(out=xT[:, b, :], in0=banks[bank + dd][:, :], scalar=gate_c[:, g, b:b + 1],
                                             in1=xT[:, b, :], op0=ALU.mult, op1=ALU.add).then_inc(x_updated, 1)

            def down(fi, j):
                base, x0 = FFN_SLOT[fi] + 2 * GU_IT + 6 * j, 2 * KC * fi + 4 * j
                for s in range(6):
                    if s == 5 and j == 1:
                        tail(2 * fi + 1, base + s)
                        return
                    if s % 3 == 2:
                        add_to_x(2 * fi, base + s, x0 + 2 * (s // 3), 2 * (s // 3))
                        for dd in range(2):
                            add_squares(x0 + 2 * (s // 3) + dd)
                    if fi == 0:
                        ada_rest(6 * j + s)
                    if base + s + 2 < N_SLOTS:
                        lo(base + s + 2)

            def ada_rest(s):
                for batch, n, slots, add_at in ADA_REST:
                    first = GU_PAIRS * GU_IT + DOWN_PAIRS * (batch - GU_IT) if batch >= GU_IT else GU_PAIRS * batch
                    if s == add_at:
                        ada_add(batch, PRO_CHUNKS + 2 * first, 2 * n)
                        if batch == GU_IT + 1:
                            dve.wait_ge(mod_ready, GU_IT + 3)
                            gate(1)
                            gate(2)
                            coef(1)
                            coef(2).then_inc(coef_ready, 1)
                    if s in slots:
                        pair = first + slots.index(s)
                        ada_pair(slots.index(s), batch, PAIR_STEPS * pair, 16 * (pair + 1))

            def coef(q):
                return dve.scalar_tensor_tensor(out=scale_a[:, q, :], in0=mod[:, (3 * q + 1) * KC:(3 * q + 2) * KC],
                                                scalar=1.0, in1=cols[:, GAIN + KC * q:GAIN + KC * (q + 1)],
                                                op0=ALU.add, op1=ALU.mult)

            def gate(q):
                return dve.tensor_scalar(gate_c[:, q, :], mod[:, (3 * q + 2) * KC:(3 * q + 3) * KC],
                                         1.0 if q == 1 else 0.5, None, ALU.mult)

            for k in range(KC):
                dve.wait_ge(x_turned, k + 1)
                dve.tensor_copy(xT[:, k, :], banks[k % 4][:, :]).then_inc(bank01_free if k % 4 < 2 else bank23_free, 1)
            variance(0)
            for step in range(4):
                root(0, step)
            dve.wait_ge(cact_ready, 1)

            def pro_rows(j, which):
                for i_ in which:
                    k = PRO_DVE[j][i_]
                    w, ck, step = ada_pro[j][:, k, :], c_act[:, k:k + 1], len(PRO_DVE[1]) * (1 - j) + i_
                    dve.wait_ge(pro_landed[j * KC + k], 16)
                    if i_ == 0:
                        dve.tensor_scalar(acc_pro[j][:, :], w, ck, None, ALU.mult).then_inc(pro_step, 1)
                    else:
                        dve.wait_ge(pro_step, step)
                        dve.scalar_tensor_tensor(out=acc_pro[j][:, :], in0=w, scalar=ck, in1=acc_pro[j][:, :],
                                                 op0=ALU.mult, op1=ALU.add).then_inc(pro_step, 1)

            def pro_finish(j):
                c_, red = slice(j * KC, (j + 1) * KC), 3 * (1 - j)
                dve.wait_ge(pro_mm, 2 - j)
                dve.tensor_reduce(mod_part[:, c_], banks[4 if j else 7][:, 0:KC * len(PRO_PE[j])]
                                  .rearrange("p (k c) -> p c k", k=len(PRO_PE[j])), AX.X, ALU.add)\
                   .then_inc(pro_red, 1)
                dve.wait_ge(cols_ready, 1)
                dve.wait_ge(pro_red, red + 1)
                dve.tensor_tensor(mod_part[:, c_], mod_part[:, c_], cols[:, c_], ALU.add).then_inc(pro_red, 1)
                for n in range(2):
                    dve.wait_ge(pro_turned, 2 * (1 - j) + n + 1)
                    ins = dve.tensor_reduce(ada_col[:, j * KC + TB * n:j * KC + TB * (n + 1)],
                                            banks[2 * (1 - j) + n][:, :].rearrange("p (s k) -> p s k", s=TB), AX.X, ALU.add)
                ins.then_inc(pro_red, 1)
                dve.wait_ge(pro_red, red + 3)
                dve.tensor_tensor(mod[:, c_], ada_col[:, c_], mod_part[:, c_], ALU.add)\
                   .then_inc(scale1_ready if j else mod_ready, 1)

            pro_rows(1, range(1))
            dve.wait_ge(rows_turned, 1)
            dve.tensor_copy(cols[:, :], banks[5][:, 0:GAIN + 4 * KC]).then_inc(cols_ready, 1)
            pro_rows(1, range(1, len(PRO_DVE[1])))
            pro_rows(0, range(2))
            pro_finish(1)
            dve.wait_ge(scale1_ready, 1)
            coef(0).then_inc(coef_ready, 1)
            pro_rows(0, range(2, len(PRO_DVE[0])))
            dve.wait_ge(coef_ready, 1)
            dve.wait_ge(rstd_bc, 1)
            for k in range(2):
                norm_block(0, k)
            pro_finish(0)
            norm_block(0, 2)
            lo_half(0, 0)
            dve.wait_ge(mod_ready, 1)
            norm_apply(0, done=3)
            lo(1)
            gu(0, 0, hid1)
            with dve.Fori(0, GU_IT - 1) as i:
                gu(0, i + 1, hid1, prev=i)
            dve.wait_ge(mod_ready, GU_IT)
            gate(0).then_inc(coef_ready, 1)
            dve.wait_ge(coef_ready, 2)
            for j in range(2):
                down(0, j)
            dve.wait_ge(coef_ready, 3)
            norm_apply(1)
            norm_apply(2)
            dve.wait_ge(split_done, S_MIX + 2)

            dve.wait_ge(wf_hi_ready, 1)
            dve.tensor_tensor(wf_lo[:, 0:KC * FH], wf[:, :, :].rearrange("p k h -> p (k h)"),
                              wf_hi[:, 0:KC * FH].bitcast(F32), ALU.subtract).then_inc(wf_ready, 1)
            dve.wait_ge(mask_ready, 2)
            dve.tensor_copy(rel[:, :], i_rel[:, :])
            dve.tensor_scalar(i_and[:, :], i_rel[:, P:2 * P], DILATION[2] // DILATION[1] - 1, None, ALU.bitwise_and)\
               .then_inc(res_ready, 1)
            dve.wait_ge(res_ready, 1)
            dve.scalar_tensor_tensor(out=m_res[:, :], in0=i_and[:, :], scalar=NEG, in1=m_causal[:, :],
                                     op0=ALU.mult, op1=ALU.add).then_inc(res_ready, 1)

            def evac_qkv(m):
                for b in range(2):
                    dve.wait_ge(slot_used, S_MIX + m + 1)
                    src = banks[qkv_bank(m) + b]
                    what, g = QKV[m]
                    if what == "v":
                        dve.tensor_copy(dv[g][:, 2 * b:2 * b + 2, :], src[:, :].rearrange("p (t e) -> p t e", t=2))\
                           .then_inc(qkv_evac, 1)
                        continue
                    is_k = what == "k"
                    dst = (dk if is_k else dq)[g][:, b, :]
                    view = src[:, :]
                    if g:
                        view = view.rearrange("p (i r) -> p r i", r=TB)
                        dst = dst.rearrange("p (r i) -> p r i", r=TB)
                    dve.tensor_scalar(dst, view, 1.0 if is_k else 0.125, None, ALU.mult).then_inc(qkv_evac, 1)

            for m in range(N_QKV):
                evac_qkv(m)
                lo(S_MIX + 2 + m)
                if m == 1:
                    dve.wait_ge(f_ready, 1)
                    dve.wait_ge(fb_landed, 16)
                    dve.tensor_scalar(f_x, banks[7][0:FH, :], fbias[:, 0:1], None, ALU.add).then_inc(f_step, 1)
                    dve.wait_ge(f_step, 1)
                    dve.tensor_scalar(ls_row, f_x, -1.0, None, ALU.mult).then_inc(f_step, 1)
                    dve.wait_ge(f_step, 2)
                    dve.tensor_tensor(f_abs, f_x, ls_row, ALU.min).then_inc(f_step, 1)
                if m == 3:
                    dve.memset(zeros_row, 0.0)
                    dve.wait_ge(f_act, 2)
                    dve.scalar_tensor_tensor(out=ls_row, in0=f_x, scalar=0.0, in1=f_abs, op0=ALU.min,
                                             op1=ALU.subtract).then_inc(f_step, 1)
                    dve.wait_ge(f_step, 4)
                    dve.tensor_tensor_scan(cum_row[:, :], zeros_row, ls_row, 0.0, ALU.add, ALU.add)\
                       .then_inc(cum_ready, 1)
                if m == 6:
                    dve.wait_ge(cum_split, 1)
                    dve.tensor_tensor(cum_lo[:, :], cum_row[:, :], cum_hi[:, :].bitcast(F32), ALU.subtract)\
                       .then_inc(cum_split, 1)
                    dve.wait_ge(cum_turned, 1)
                    dve.tensor_copy(cum_col[:, :, :], banks[7][:, 0:TB * FH].rearrange("p (t h) -> p t h", t=TB))\
                       .then_inc(cumcol_ready, 1)

            n_bias, n_max = [0], [0]

            def alibi_tile(job, g, h):
                slope = -SLOPE[g * GH + h] * (DILATION[1] if g else 1)
                w, mask = (2 * P, m_band[:, :]) if g == 0 else (P, m_causal[:, :] if g == 1 else m_res[:, :])
                r = rel[:, :] if g == 0 else rel[:, P:2 * P]
                dve.scalar_tensor_tensor(out=alibi[:, job % 2, 0:w], in0=r, scalar=slope, in1=mask,
                                         op0=ALU.mult, op1=ALU.add).then_inc(alibi_ready, 1)
                dve.wait_ge(alibi_ready, job + 1)

            def bias_tile(u):
                job, g, h, subs = TILES[u]
                w = subs[-1][1] + subs[-1][2]
                S, B = banks[2 + u % 2], tmpA[:, u % 2, :]
                if g < 3 and (u == 0 or TILES[u - 1][0] != job):
                    alibi_tile(job, g, h)
                dve.wait_ge(scores_ready, u + 1)
                if u >= 2:
                    dve.wait_ge(probs_ready, u - 1)
                if g == 0 and subs[0][0] == 0:
                    dve.tensor_tensor(B[:, 0:P], S[:, 0:P], alibi[:, job % 2, P:2 * P], ALU.add)
                    dve.tensor_tensor(B[:, P:w], S[:, P:w], alibi[:, job % 2, :], ALU.add).then_inc(scores_read, 1)
                elif g < 3:
                    n = 2 if g == 0 else TB
                    dve.tensor_tensor(B[:, 0:w].rearrange("p (n c) -> p n c", n=n),
                                      S[:, 0:w].rearrange("p (n c) -> p n c", n=n),
                                      alibi[:, job % 2, 0:w // n].unsqueeze(1).broadcast_to([P, n, w // n]),
                                      ALU.add).then_inc(scores_read, 1)
                else:
                    dve.wait_ge(ck_free, h + 1)
                    for i_, (t, c0, ws) in enumerate(subs):
                        ins = dve.scalar_tensor_tensor(out=B[:, c0:c0 + ws], in0=S[:, c0:c0 + ws],
                                                       scalar=cum_col[:, t, h:h + 1], in1=ckb[h % 2][:, 0:ws],
                                                       op0=ALU.add, op1=ALU.add)
                    ins.then_inc(scores_read, 1)
                    dve.wait_ge(scores_read, u + 1)
                    for t, c0, ws in subs:
                        ins = dve.tensor_tensor(B[:, c0 + ws - P:c0 + ws], B[:, c0 + ws - P:c0 + ws], m_causal[:, :],
                                                ALU.add)
                    n_bias[0] += 1
                    ins.then_inc(bias_step, 1)
                    dve.wait_ge(bias_step, n_bias[0])
                dve.wait_ge(scores_read, u + 1)
                if g in (1, 2):
                    ins = dve.tensor_reduce(mx[:, g, :, h], B.rearrange("p (n c) -> p n c", n=TB), AX.X, ALU.max)
                else:
                    for t, c0, ws in subs:
                        ins = dve.tensor_reduce(mx[:, g, t, h:h + 1], B[:, c0:c0 + ws], AX.X, ALU.max)
                ins.then_inc(max_step, 1)
                dve.wait_ge(max_step, u + 1)
                t0, n = subs[0][0], len(subs)
                dve.tensor_scalar(nmx[:, u % 2, 0:n], mx[:, g, t0:t0 + n, h], -1.0, None, ALU.mult).then_inc(max_ready, 1)

            def finish_job(job):
                g, h = JOBS[job]
                dve.wait_ge(pv_ready, LAST_TILE[job] + 1)
                dve.reciprocal(rz[:, job % 2, :], zs[:, g, :, h]).then_inc(rz_ready, 1)
                dve.wait_ge(rz_ready, job + 1)
                dst = o_dil[:, g, :, h * E_:(h + 1) * E_] if g < 3 else o_fox[:, :, h * E_:(h + 1) * E_]
                dve.tensor_tensor(dst, banks[6 + job % 2][:, 0:TB * E_].rearrange("p (t e) -> p t e", t=TB),
                                  rz[:, job % 2, :].unsqueeze(2).broadcast_to([P, TB, E_]), ALU.mult).then_inc(o_free, 1)

            def evac_over(m, f):
                if f == 0:
                    dve.wait_ge(proj_ready, m + 1)
                else:
                    dve.wait_ge(slot_used, S_OVER + m + 1)
                free = p1_free if f else p0_free
                if m < 2:
                    dve.tensor_scalar(fq[:, 2 * m + f, :], banks[f][:, :], 0.125, None, ALU.mult).then_inc(free, 1)
                elif m < 4:
                    dve.tensor_copy(fk[:, 2 * (m - 2) + f, :], banks[f][:, :]).then_inc(free, 1)
                elif m < 6:
                    dve.tensor_copy(fv[:, 2 * f:2 * f + 2, (m - 4) * SC:(m - 3) * SC],
                                    banks[f][:, :].rearrange("p (t e) -> p t e", t=2)).then_inc(free, 1)
                else:
                    dve.tensor_copy(gates[:, 2 * (m - 6) + f, :], banks[f][:, :]).then_inc(free, 1)

            def per_head(ap):
                return ap.unsqueeze(2).broadcast_to([P, TB * GH, E_])

            def combine(s):
                def tt(out_, a, b, op):
                    dve.tensor_tensor(out_, a, b, op).then_inc(comb, 1)
                    n_comb[0] += 1
                    dve.wait_ge(comb, n_comb[0])

                od = [o_dil[:, g, :, :].rearrange("p t (h e) -> p (t h) e", h=GH) for g in range(NG)]
                if s == COMB_LN + 1:
                    dve.wait_ge(comb_act, 1)
                    tt(lse[:, :, :].rearrange("p g (t h) -> p g t h", t=TB), mx[:, 0:NG, :, 0:GH],
                       gw[:, :, :].rearrange("p g (t h) -> p g t h", t=TB), ALU.add)
                if s == COMB_EXP - 1:
                    dve.wait_ge(lse_in, 16)
                    tt(gmax[:, :], lse[:, 0, :], lse[:, 1, :], ALU.max)
                    tt(gmax[:, :], gmax[:, :], lse[:, 2, :], ALU.max)
                    tt(gw[:, :, :], lse[:, :, :], gmax[:, :].unsqueeze(1).broadcast_to([P, NG, TB * GH]), ALU.subtract)
                if s == COMB_EXP + 1:
                    dve.wait_ge(comb_act, 2)
                    tt(gsum[:, :], gw[:, 0, :], gw[:, 1, :], ALU.add)
                    tt(gsum[:, :], gsum[:, :], gw[:, 2, :], ALU.add)
                    dve.reciprocal(gmax[:, :], gsum[:, :]).then_inc(comb, 1)
                    n_comb[0] += 1
                    dve.wait_ge(comb, n_comb[0])
                    tt(gw[:, :, :], gw[:, :, :], gmax[:, :].unsqueeze(1).broadcast_to([P, NG, TB * GH]), ALU.mult)
                if s == COMB_EXP + 2:
                    tt(od[1], od[1], per_head(gw[:, 1, :]), ALU.mult)
                if s == COMB_EXP + 3:
                    tt(od[2], od[2], per_head(gw[:, 2, :]), ALU.mult)
                if s == COMB_EXP + 4:
                    tt(od[1], od[1], od[2], ALU.add)
                if s == COMB_EXP + 8:
                    dve.wait_ge(gw_in, 16)
                    tt(od[0], od[0], per_head(gw0[:, :]), ALU.mult)

            n_comb = [0]
            dve.wait_ge(res_ready, 2)
            dve.wait_ge(cumcol_ready, 1)
            for m in range(N_OVER):
                for j in range(3):
                    s = 3 * m + j
                    if j == 0 and m >= 1:
                        evac_over(m - 1, 1)
                    if 0 <= s - 1 < N_TILES:
                        bias_tile(s - 1)
                    if j == 0 and m >= 1:
                        lo(S_OVER + m + 1)
                    if j == 1:
                        evac_over(m, 0)
                    if s - 4 >= 0 and LAST_TILE[TILES[s - 4][0]] == s - 4:
                        finish_job(TILES[s - 4][0])
                    combine(s)
            evac_over(N_OVER - 1, 1)
            finish_job(TILES[N_TILES - 1][0])

            for fb in range(2):
                dve.wait_ge(y_turned, 2 * fb + 2)
                dve.wait_ge(y0_ready, fb + 1)
                dve.tensor_tensor(tmpB[:, fb, :].rearrange("p (i r) -> p r i", r=TB),
                                  banks[3 + 2 * fb][:, :].rearrange("p (r i) -> p r i", r=TB),
                                  tmpA[:, fb, :].rearrange("p (i r) -> p r i", r=TB), ALU.add).then_inc(ysum_ready, 1)
            for fc in range(4):
                dve.wait_ge(y_hi_ready, fc + 1)
                dve.tensor_tensor(y_lo[:, 2 + fc, :], banks[FOX_BANK[fc]][:, :], y_hi[:, 2 + fc, :].bitcast(F32),
                                  ALU.subtract).then_inc(y_ready, 1)
            for fb in range(2):
                dve.wait_ge(y_hi_ready, 4 + fb + 1)
                dve.tensor_tensor(y_lo[:, fb, :], tmpB[:, fb, :], y_hi[:, fb, :].bitcast(F32), ALU.subtract)\
                   .then_inc(y_ready, 1)

            lo(S_BR + 1)
            def merge_lo(d):
                dve.wait_ge(merge_hi, d + 1)
                dve.tensor_tensor(h_lo[:, d, :], tmpB[:, d % 2, :], h_hi[:, d, :].bitcast(F32), ALU.subtract)\
                   .then_inc(merged, 1)

            for d in range(KC):
                b0 = BR_BANK[d // 2 % 2][d % 2]
                if d % 2 == 0:
                    dve.wait_ge(br_ready, d // 2 + 1)
                else:
                    dve.wait_ge(slot_used, S_BR + d // 2 + 1)
                dve.wait_ge(sig_ready, d + 1)
                if d >= 1:
                    dve.wait_ge(msum_ready, d)
                for x_ in range(2):
                    dve.tensor_tensor(tmpA[:, x_, :], banks[b0 + 1 - x_][:, :], gates[:, KC * x_ + d, :], ALU.mult)\
                       .then_inc(merge_step, 1)
                dve.wait_ge(merge_step, 2 * d + 2)
                dve.tensor_tensor(tmpB[:, d % 2, :], tmpA[:, 0, :], tmpA[:, 1, :], ALU.add).then_inc(msum_ready, 1)
                if d >= 1:
                    merge_lo(d - 1)
                if d % 2 == 1:
                    lo(S_BR + d // 2 + 2)
            merge_lo(KC - 1)
            for d2 in range(N_OUT):
                x0 = KC + 2 * d2
                if d2 == N_OUT - 1:
                    tail(2, S_OUT + d2)
                else:
                    add_to_x(1, S_OUT + d2, x0, 2 * (d2 % 2))
                    for dd in range(2):
                        add_squares(x0 + dd)
                    lo(S_OUT + d2 + 2)
            norm_apply(3)
            norm_apply(4)
            dve.wait_ge(split_done, S_FFN2 + 2)
            with dve.Fori(0, GU_IT) as i:
                gu(1, i, hid2)
            for j in range(2):
                down(1, j)
            final_rstd(5)
            for t in range(TB):
                if t == 1:
                    for p in range(2):
                        sums(6, p)
                    variance(6)
                if t == TB // 2:
                    for step in range(4):
                        root(6, step)
                    final_rstd(6)
                dve.wait_ge(fin_turned[1], t + 1)
                dve.tensor_scalar(y_sb[:, t, T:2 * T], banks[FIN_BANK[1][t]][:, :], rstd[:, t:t + 1], None, ALU.mult)\
                   .then_inc(y_dve, 1)

        @block.tensor
        def _(pe):
            def mm3(out_, a, b, first, last):
                pe.matmul(out_, a[0], b[0], start=first, stop=False)
                pe.matmul(out_, a[0], b[1], start=False, stop=False)
                return pe.matmul(out_, a[1], b[0], start=False, stop=last)

            def products_of_norm(n, q, b0):
                for r in (0,) if q == 0 else (2 * q - 1, 2 * q):
                    for k in range(KC):
                        (hh, hl), blks = h_blk(k, tok(r)), [(banks[b0 + f][:, tok(r)], w_blk(n, k, f)) for f in range(2)]
                        if r == 0 and k == KC // 2:
                            pe.wait_ge(split_done, n + 1)
                        pe.wait_ge(h_hi_ready, KC * r + k + 1)
                        for bank, (wh, wl) in blks:
                            pe.matmul(bank, wh, hh, start=k == 0, stop=False)
                            pe.matmul(bank, wl, hh, start=False, stop=False)
                        pe.wait_ge(h_ready, KC * r + k + 1)
                        for bank, (wh, wl) in blks:
                            last = pe.matmul(bank, wh, hl, start=False, stop=k == KC - 1)
                        if r % 2 == 1 and k == 0:
                            turn_squares(r + 1, 0)
                            turn_squares(r + 1, 1)
                        if r % 2 == 1 and k == KC - 2:
                            rstd_rows(r + 1)
                return last

            def w_blk(n, k, f, at=0):
                c0 = at + k * SC + f * P
                return w_hi[n % 2][:, c0:c0 + P], w_lo[n % 2][:, c0:c0 + P]

            def h_blk(k, sl=slice(0, T)):
                return h_hi[:, k, sl], h_lo[:, k, sl]

            def gate_up(fi, i, prev=None, first=False):
                base, bank0, q = FFN_SLOT[fi], BANKS[fi], 2 * fi
                for j in range(2):
                    n = base + j
                    if first and fi == 0 and j == 0:
                        pe.wait_ge(split_half, 1)
                    else:
                        pe.wait_ge(split_done, n + 1 + 2 * i)
                    pe.wait_ge(bank23_free if j else bank01_free, bank0 + 2 * i)
                    if j == 0 and first:
                        products_of_norm(n, q, 0).then_inc(slot_used, 1)
                        continue
                    for k in range(KC):
                        for f in range(2):
                            last = mm3(banks[2 * j + f][:, :], w_blk(n, k, f), h_blk(k), k == 0, k == KC - 1)
                        if prev is not None and j == 1 and k == 3:
                            per = GU_PAIRS * PAIR_STEPS
                            ada_sum(prev, per * prev + per, 2 * GU_PAIRS)
                    last.then_inc(slot_used, 1)

            def ada_sum(batch, step, n):
                pe.wait_ge(ada_step, step)
                pe.wait_ge(mod_ready, batch + 1)
                for s in range(n):
                    last = pe.transpose(banks[4 if s < TB else 6][:, s % TB * P:(s % TB + 1) * P], ada_acc[s][:, :],
                                        ident[:, :])
                last.then_inc(ada_mm, 1)

            def turn_squares(r, p):
                q, second = norm_of(r), r % 2 == 0
                if p:
                    pe.wait_ge(sq_ready if second else tail_sq, KC * q if second else 2 * q)
                else:
                    pe.wait_ge(sq_added if second else tail_added, (KC - 2) * q if second else q)
                src = tmpA[:, 1, :] if p else sq_sum
                for t in tiles_of(r):
                    last = pe.transpose(banks[(5, 7)[p]][:, t * P:(t + 1) * P], src[:, t * P:(t + 1) * P], ident[:, :])
                last.then_inc(stat_done, 1)

            def last_slot(n, nk, bank, act_blk, start):
                for dd in range(2):
                    for k in range(nk):
                        last = mm3(banks[bank + dd][:, :], w_blk(n, k, dd), act_blk(k, slice(0, T)), start and k == 0,
                                   k == nk - 1)
                    last.then_inc(slot_used if dd else half_done, 1)

            def tail_slot(q, n, nk, act_blk, start):
                r = 2 * q - 1
                for e in range(2):
                    if e and start:
                        pe.wait_ge(x_updated, KC * q - 2)
                    for dd in range(2):
                        for k in range(nk):
                            if e and dd and k == 0:
                                turn_squares(r, 0)
                                turn_squares(r, 1)
                            if e and dd and k == 4 and q == 3:
                                for t in range(2):
                                    final_turn(1, t)
                            last = mm3(banks[TAIL_BANK[e][dd]][:, tok(r + e)], w_blk(n, k, dd), act_blk(k, tok(r + e)),
                                       start and k == 0, k == nk - 1)
                        last.then_inc(slot_used if dd and e else tail_done, 1)
                if q < 3:
                    rstd_rows(r)
                else:
                    pe.wait_ge(var_ready, r + 1)
                    turn_squares(r + 1, 0)
                    turn_squares(r + 1, 1)

            def down(fi, j, hid):
                base, x0, hid0 = FFN_SLOT[fi] + 2 * GU_IT + 6 * j, 2 * KC * fi + 4 * j, 2 * GU_IT * fi
                for s in range(6):
                    n, (k0, nk) = base + s, DOWN_PARTS[s % 3]
                    if s % 3 == 0 and j == 0:
                        pe.wait_ge(bank23_free if s else bank01_free, BANKS[fi] + 2 * GU_IT)
                    elif s % 3 == 0:
                        pe.wait_ge(x_updated, x0 if s else x0 - 2)
                    pe.wait_ge(split_done, n + 1)
                    pe.wait_ge(hid_ready, hid0 + min(k0 + nk, FB))

                    def hid_blk(k, t_):
                        return hid[0][:, k0 + k, t_], hid[1][:, k0 + k, t_]

                    if s % 3 == 2:
                        if j == 1 and s == 5:
                            tail_slot(2 * fi + 1, n, nk, hid_blk, False)
                        else:
                            last_slot(n, nk, 2 * (s // 3), hid_blk, False)
                    else:
                        by_half = j == 1 and s >= 3
                        for e in range(2 if by_half else 1):
                            if s == 3 and e:
                                pe.wait_ge(x_updated, x0 + 2)
                            t_ = tok(1 + e) if by_half else slice(0, T)
                            for k in range(nk):
                                for dd in range(2):
                                    bank = TAIL_BANK[e][dd] if by_half else 2 * (s // 3) + dd
                                    last = mm3(banks[bank][:, t_], w_blk(n, k, dd), hid_blk(k, t_), k0 + k == 0, False)
                        last.then_inc(slot_used, 1)
                    if s == 3 and fi == 1 and j == 1:
                        for t in range(2):
                            final_turn(0, t)
                    for batch, n, _, add_at in ADA_REST:
                        if fi == 0 and 6 * j + s == add_at - 1:
                            pairs = GU_PAIRS * GU_IT + DOWN_PAIRS * (batch - GU_IT + 1)
                            if batch < GU_IT:
                                pairs = GU_PAIRS * (batch + 1)
                            ada_sum(batch, PAIR_STEPS * pairs, 2 * n)

            def final_turn(half, t):
                for k in range(4 * half, 4 * half + 4):
                    pe.wait_ge(xg_ready, k + 1 if k < KC - 2 else k + 1 + t // 2 * 2)
                    last = pe.transpose(banks[FIN_BANK[half][t]][:, k % 4 * P:(k % 4 + 1) * P],
                                        xT[:, k, t * P:(t + 1) * P], ident[:, :])
                last.then_inc(fin_turned[half], 1)

            def rstd_rows(r):
                pe.wait_ge(neg_step, r + 1)
                for t in tiles_of(r):
                    last = pe.matmul(rstd_bank(r)[:, t * P:(t + 1) * P], rstd_m2[:, t:t + 1].broadcast_to([P, P]),
                                     half_neg[:, :], start=True, stop=True)
                last.then_inc(rstd_bc, 1)

            pe.wait_ge(const_ready, 2)
            pe.wait_ge(c_landed, 16)
            pe.transpose(banks[7][:, 0:KC], c_rows[:, :], ident[0:KC, 0:KC]).then_inc(c_turned, 1)
            for k in range(KC):
                if k >= 4:
                    pe.wait_ge(bank01_free if k % 4 < 2 else bank23_free, k % 2 + 1)
                for t in range(TB):
                    if k == 0:
                        pe.wait_ge(x_landed[t], 16)
                    last = pe.transpose(banks[k % 4][:, t * P:(t + 1) * P], x_nat[:, t, k * P:(k + 1) * P], ident[:, :])
                last.then_inc(x_turned, 1)
            pe.wait_ge(rows_landed, 16 * 5)
            pe.transpose(banks[5][:, 0:GAIN + 4 * KC], rows[:, :], ident[0:GAIN + 4 * KC, 0:GAIN + 4 * KC])\
              .then_inc(rows_turned, 1)
            pe.wait_ge(cact_ready, 1)
            for j in (1, 0):
                for i_, k in enumerate(PRO_PE[j]):
                    pe.wait_ge(pro_landed[j * KC + k], 16)
                    for c0 in range(KC):
                        col = KC * i_ + c0
                        last = pe.matmul(banks[4 if j else 7][:, col:col + 1], ada_pro[j][:, k, c0 * P:(c0 + 1) * P],
                                         c_act[:, k:k + 1], start=True, stop=True)
                last.then_inc(pro_mm, 1)
                if j:
                    rstd_rows(0)
                    pe.wait_ge(bank01_free, 4)
                    pe.wait_ge(bank23_free, 4)
                pe.wait_ge(pro_step, len(PRO_DVE[1]) + (0 if j else len(PRO_DVE[0])))
                for n in range(2):
                    for s in range(TB):
                        c0 = (n * TB + s) * P
                        last = pe.transpose(banks[2 * (1 - j) + n][:, s * P:(s + 1) * P], acc_pro[j][:, c0:c0 + P],
                                            ident[:, :])
                    last.then_inc(pro_turned, 1)
            gate_up(0, 0, first=True)
            with pe.Fori(0, GU_IT - 1) as i:
                gate_up(0, i + 1, prev=i)
            for j in range(2):
                down(0, j, hid1)

            def tokens(g, t):
                return slice(t * P, (t + 1) * P) if g == 0 else slice(t, T, TB)

            for m in range(N_QKV):
                n = S_MIX + m
                pe.wait_ge(split_done, n + 1)
                if m >= 2:
                    pe.wait_ge(qkv_evac, 2 * (m - 1))
                b0 = qkv_bank(m)
                what, g = QKV[m]
                if what == "v":
                    for t in range(TB):
                        for k in range(KC):
                            at = k * SC
                            last = mm3(banks[b0 + t // 2][:, t % 2 * SC:(t % 2 + 1) * SC], h_blk(k, tokens(g, t)),
                                       (w_hi[n % 2][:, at:at + SC], w_lo[n % 2][:, at:at + SC]), k == 0, k == KC - 1)
                elif m == 0:
                    last = products_of_norm(n, 1, b0)
                else:
                    for k in range(KC):
                        for f in range(2):
                            last = mm3(banks[b0 + f][:, :], w_blk(n, k, f), h_blk(k), k == 0, k == KC - 1)
                last.then_inc(slot_used, 1)
                if m == 0:
                    pe.wait_ge(wf_ready, 1)
                    pe.wait_ge(wf_zero, 2)
                    for k in range(KC):
                        w = slice(k * FH, k * FH + P)
                        last = mm3(banks[7][:, :], (wf_hi[:, w], wf_lo[:, w]), h_blk(k), k == 0, k == KC - 1)
                    last.then_inc(f_ready, 1)
                if m == 5:
                    pe.wait_ge(cum_ready, 1)
                    for t in range(TB):
                        last = pe.transpose(banks[7][:, t * FH:(t + 1) * FH], cum_row[:, t * P:(t + 1) * P],
                                            ident[0:FH, 0:FH])
                    last.then_inc(cum_turned, 1)

            def scores(u):
                job, g, h, subs = TILES[u]
                if u == 0:
                    pe.wait_ge(qkv_evac, 2 * N_QKV)
                if u >= 2:
                    pe.wait_ge(scores_read, u - 1)
                p0 = h % 2 * E_
                q, kk = (dq[g], dk[g]) if g < 3 else (fq, fk)
                for t, c0, w in subs:
                    k0 = key_blocks(g, t)[0] * P
                    last = pe.matmul(banks[2 + u % 2][:, c0:c0 + w], q[p0:p0 + E_, h // 2, t * P:(t + 1) * P],
                                     kk[p0:p0 + E_, h // 2, k0:k0 + w], start=True, stop=True)
                last.then_inc(scores_ready, 1)

            def turn_probs(u):
                _, _, _, subs = TILES[u]
                pe.wait_ge(probs_ready, u + 1)
                if u >= 2:
                    pe.wait_ge(pT_ready, u - 1)
                for c0 in range(0, subs[-1][1] + subs[-1][2], P):
                    last = pe.transpose(banks[4 + u % 2][:, c0:c0 + P], tmpB[:, u % 2, c0:c0 + P], ident[:, :])
                last.then_inc(turned, 1)

            def values(u):
                job, g, h, subs = TILES[u]
                pe.wait_ge(pT_ready, u + 1)
                if job >= 2:
                    pe.wait_ge(o_free, job - 1)
                if u == FIRST_FOX:
                    pe.wait_ge(p0_free, 6)
                    pe.wait_ge(p1_free, 6)
                for t, c0, w in subs:
                    blocks = key_blocks(g, t)
                    for i_, b in enumerate(blocks):
                        v = dv[g][:, b, h * E_:(h + 1) * E_] if g < 3 else fv[:, b, h * E_:(h + 1) * E_]
                        last = pe.matmul(banks[6 + job % 2][:, t * E_:(t + 1) * E_],
                                         pT[:, u % 2, c0 + i_ * P:c0 + (i_ + 1) * P], v,
                                         start=i_ == 0, stop=i_ == len(blocks) - 1)
                last.then_inc(pv_ready, 1)

            pe.wait_ge(qkv_evac, 2 * (N_QKV - 1))
            for m in range(N_OVER):
                n = S_OVER + m
                pe.wait_ge(split_done, n + 1)
                steps = []
                for f in range(2):
                    if m in (4, 5):
                        steps += [(f, t, k) for t in (2 * f, 2 * f + 1) for k in range(KC)]
                    else:
                        steps += [(f, None, k) for k in range(KC)]
                third = -(-len(steps) // 3)
                for j in range(3):
                    for f, t, k in steps[j * third:(j + 1) * third]:
                        if k == 0 and (t is None or t % 2 == 0):
                            if m >= 1:
                                pe.wait_ge(p1_free if f else p0_free, m)
                            if f == 0 and 0 <= m - 1 - 4 < FH:
                                pe.wait_ge(ck_free, m - 4)
                        if t is None:
                            last = mm3(banks[f][:, :], w_blk(n, k, f), h_blk(k), k == 0, k == KC - 1)
                        else:
                            last = mm3(banks[f][:, t % 2 * SC:(t % 2 + 1) * SC], h_blk(k, slice(t * P, (t + 1) * P)),
                                       (w_hi[n % 2][:, k * SC:(k + 1) * SC], w_lo[n % 2][:, k * SC:(k + 1) * SC]),
                                       k == 0, k == KC - 1)
                        if k == KC - 1 and t in (None, 1, 3):
                            last.then_inc(slot_used if f else proj_ready, 1)
                    s = 3 * m + j
                    if j == 2 and 4 <= m < 4 + FH:
                        pe.wait_ge(p0_free, m + 1)
                        pe.wait_ge(cum_split, 2)
                        head = neg_head[:, m - 4:m - 3].broadcast_to([FH, P])
                        pe.matmul(banks[0][:, :], head, cum_hi[:, :], start=True, stop=False)
                        pe.matmul(banks[0][:, :], head, cum_lo[:, :], start=False, stop=True)\
                          .then_inc(ck_ready, 1)
                    if 0 <= s - 3 < N_TILES:
                        values(s - 3)
                    if 0 <= s - 2 < N_TILES:
                        turn_probs(s - 2)
                    if s < N_TILES:
                        scores(s)

            def turn_dilated(fb):
                for g in range(2):
                    for t in range(TB):
                        last = pe.transpose(banks[2 + 2 * fb + g][:, t * P:(t + 1) * P],
                                            o_dil[:, g, t, fb * P:(fb + 1) * P], ident[:, :])
                    last.then_inc(y_turned, 1)

            pe.wait_ge(comb, 12)
            pe.wait_ge(scores_read, N_TILES)
            turn_dilated(0)
            values(N_TILES - 1)
            turn_dilated(1)
            for fc in range(4):
                if fc == 0:
                    pe.wait_ge(o_free, len(JOBS) - 1)
                elif fc == 3:
                    pe.wait_ge(o_free, len(JOBS))
                else:
                    pe.wait_ge(p1_free if fc == 2 else p0_free, N_OVER)
                for t in range(TB):
                    last = pe.transpose(banks[FOX_BANK[fc]][:, t * P:(t + 1) * P], o_fox[:, t, fc * P:(fc + 1) * P],
                                        ident[:, :])
                last.then_inc(y_turned, 1)
            for d2 in range(N_BR):
                n = S_BR + d2
                pe.wait_ge(split_done, n + 1)
                if d2 >= 2:
                    pe.wait_ge(msum_ready, 2 * (d2 - 1))
                for dd in range(2):
                    b0 = BR_BANK[d2 % 2][dd]
                    for k in range(4):
                        if d2 == 0 and dd == 0:
                            pe.wait_ge(y_ready, k + 1)
                        mm3(banks[b0][:, :], w_blk(n, k, dd, at=2 * SC),
                            (y_hi[:, 2 + k, :], y_lo[:, 2 + k, :]), k == 0, k == 3)
                    for k in range(2):
                        if d2 == 0 and dd == 0:
                            pe.wait_ge(y_ready, 4 + k + 1)
                        last = mm3(banks[b0 + 1][:, :], w_blk(n, k, dd), (y_hi[:, k, :], y_lo[:, k, :]), k == 0, k == 1)
                    last.then_inc(slot_used if dd else br_ready, 1)
            pe.wait_ge(msum_ready, 6)
            for d2 in range(N_OUT):
                n = S_OUT + d2
                pe.wait_ge(split_done, n + 1)
                if d2 >= 2:
                    pe.wait_ge(x_updated, KC + 2 * (d2 - 1))
                if d2 == N_OUT - 1:
                    tail_slot(2, n, KC, h_blk, True)
                    continue
                for k in range(KC):
                    if d2 == 0:
                        pe.wait_ge(merged, k + 1)
                    for dd in range(2):
                        last = mm3(banks[2 * (d2 % 2) + dd][:, :], w_blk(n, k, dd), h_blk(k), k == 0, k == KC - 1)
                        if dd == 0 and k == KC - 1:
                            last.then_inc(half_done, 1)
                last.then_inc(slot_used, 1)
            gate_up(1, 0, first=True)
            with pe.Fori(0, GU_IT - 1) as i:
                gate_up(1, i + 1)
            for j in range(2):
                down(1, j, hid2)
            pe.wait_ge(x_updated, 3 * KC)
            for half in range(2):
                final_turn(half, 2)
            pe.wait_ge(var_ready, 7)
            for half in range(2):
                final_turn(half, 3)


_INS = ["x", "c", "ada_w", "ada_b", "norm_ffn1", "ffn1_w_gate", "ffn1_w_up", "ffn1_w_down", "norm_mix", "w_in",
        "forget_bias", "w_branch_a", "w_branch_b", "w_out", "norm_ffn2", "ffn2_w_gate", "ffn2_w_up", "ffn2_w_down",
        "norm_final"]


def kernel(**inputs):
    import numpy as _np
    import concourse.bacc as _bacc
    from concourse import mybir as _mybir
    from concourse.bass_utils import run_bass_kernel_spmd as _run

    nc = _bacc.Bacc("TRN2", target_bir_lowering=False, num_devices=1)
    arrays, args = {}, []
    for name in _INS:
        a = _np.ascontiguousarray(inputs[name])
        if name != "norm_final":
            a = a[0]
        arrays[f"in_{name}"] = a
        args.append(nc.dram_tensor(f"in_{name}", a.shape, _mybir.dt.from_np(a.dtype), kind="ExternalInput").ap())
    args.append(nc.dram_tensor("out_y", (T, D), F32, kind="ExternalOutput").ap())
    build(nc, *args)
    r = _run(nc, [arrays], core_ids=[0])
    return r.results[0]["out_y"].reshape(1, T, D)
```
